# Optimizing a Trainium2 kernel written in Bass

```python
import math
import jax, jax.numpy as jnp
from jax import lax
import numpy as np

D_MODEL = 1024
BATCH = 1
SEQ = 256
DEPTH = 2

N_MIXERS = 4
D_FF = 2816
MEM_LEN = 256
X_HEADS = 4
X_HEAD_DIM = 128
X_WIDTH = X_HEADS * X_HEAD_DIM
POOL_WINDOWS = (2, 4, 8, 16)
POOL_GROUPS = len(POOL_WINDOWS)
POOL_GROUP_DIM = D_MODEL // POOL_GROUPS
DIFF_HEAD_DIM = 64
DIFF_HEADS = D_MODEL // (2 * DIFF_HEAD_DIM)
DIFF_QK = DIFF_HEADS * 2 * DIFF_HEAD_DIM
DIFF_V = DIFF_HEADS * 2 * DIFF_HEAD_DIM
Q_BLOCK = 128
MLSTM_HEADS = 4
MLSTM_HEAD_DIM = D_MODEL // MLSTM_HEADS
MLSTM_CONV = 4
MLSTM_CHUNK = 64
GLA_HEADS = 4
GLA_KEY_DIM = D_MODEL // 2 // GLA_HEADS
GLA_VALUE_DIM = D_MODEL // GLA_HEADS
GLA_GATE_RANK = 16
GLA_TAU = 16.0
GLA_CHUNK = 64
NORM_EPS = 1e-6
SUBLN_EPS = 1e-5
POOL_IN = D_MODEL + X_WIDTH
DIFF_IN = 2 * DIFF_QK + DIFF_V + X_WIDTH
MLSTM_IN = 4 * D_MODEL + 2 * MLSTM_HEADS + X_WIDTH
GLA_IN = 2 * GLA_HEADS * GLA_KEY_DIM + 2 * D_MODEL + GLA_GATE_RANK + X_WIDTH
MIX_OUT = D_MODEL + X_WIDTH


def rmsnorm(x, g, eps=NORM_EPS):
    x32 = x.astype(jnp.float32)
    y = x32 * lax.rsqrt(jnp.mean(x32 * x32, axis=-1, keepdims=True) + eps)
    return (y * g.astype(jnp.float32)).astype(x.dtype)

def swiglu(h, w_up, w_down):
    gate, up = jnp.split(h @ w_up, 2, axis=-1)
    return (jax.nn.silu(gate) * up) @ w_down

def causal_conv(x, w):
    K, C = w.shape
    return lax.conv_general_dilated(x, w[:, None, :].astype(x.dtype), (1,), [(K - 1, 0)],
                                    dimension_numbers=('NWC', 'WIO', 'NWC'), feature_group_count=C)

def alibi_slopes(n):
    return jnp.asarray([2.0 ** (-8.0 * (h + 1) / n) for h in range(n)], dtype=jnp.float32)

def memory_attention(xq, mem_k, mem_v):
    B, S, _ = xq.shape
    q = xq.reshape(B, S, X_HEADS, X_HEAD_DIM)
    s = jnp.einsum('bshd,bmhd->bhsm', q, mem_k).astype(jnp.float32) * (X_HEAD_DIM ** -0.5)
    p = jax.nn.softmax(s, axis=-1)
    o = jnp.einsum('bhsm,bmhd->bshd', p.astype(mem_v.dtype), mem_v)
    return o.reshape(B, S, X_WIDTH)

def _chunks(a, L):
    B, H, S = a.shape[:3]
    return jnp.moveaxis(a.reshape(B, H, S // L, L, *a.shape[3:]), 2, 0)

def _unchunk(a):
    NC, B, H, L = a.shape[:4]
    return jnp.moveaxis(a, 0, 2).reshape(B, H, NC * L, *a.shape[4:])

def multiscale_pool(u, w_group, scale):
    B, S, _ = u.shape
    u32 = u.astype(jnp.float32).reshape(B, S, POOL_GROUPS, POOL_GROUP_DIM)
    cs = jnp.cumsum(u32, axis=1)
    outs = []
    for g, w in enumerate(POOL_WINDOWS):
        c = cs[:, :, g]
        prev = jnp.pad(c[:, :S - w], ((0, 0), (w, 0), (0, 0)))
        count = jnp.minimum(jnp.arange(1, S + 1), w).astype(jnp.float32)
        outs.append((c - prev) / count[None, :, None] - u32[:, :, g])
    pooled = jnp.stack(outs, axis=2).astype(u.dtype)
    mixed = jnp.einsum('bsgc,gcd->bsgd', pooled, w_group).reshape(B, S, D_MODEL)
    return mixed * scale

def pool_layer(h, w_in, w_group, scale, w_out, mem_k, mem_v):
    proj = h @ w_in
    u, xq = proj[..., :D_MODEL], proj[..., D_MODEL:]
    mix = multiscale_pool(u, w_group, scale)
    xo = memory_attention(xq, mem_k, mem_v)
    return jnp.concatenate([mix, xo], axis=-1) @ w_out

def diff_attention(q, k, v, lam, slopes):
    S = q.shape[3]
    scale = DIFF_HEAD_DIM ** -0.5
    outs = []
    for start in range(0, S, Q_BLOCK):
        end = start + Q_BLOCK
        dist = (jnp.arange(start, end)[:, None] - jnp.arange(end)[None, :]).astype(jnp.float32)
        bias = jnp.where(dist >= 0, -slopes[:, None, None] * dist, -jnp.inf)
        s = jnp.einsum('bhcqd,bhckd->bhcqk', q[:, :, :, start:end], k[:, :, :, :end]).astype(jnp.float32) * scale
        p = jax.nn.softmax(s + bias[None, :, None], axis=-1)
        w = p[:, :, 0] - lam * p[:, :, 1]
        outs.append(jnp.einsum('bhqk,bhkd->bhqd', w.astype(v.dtype), v[:, :, :end]))
    return jnp.concatenate(outs, axis=2)

def diff_layer(h, w_in, lam_p, norm_g, w_out, mem_k, mem_v, slopes, layer_idx):
    B, S, _ = h.shape
    H, Dh = DIFF_HEADS, DIFF_HEAD_DIM
    proj = h @ w_in
    q = proj[..., :DIFF_QK].reshape(B, S, H, 2, Dh).transpose(0, 2, 3, 1, 4)
    k = proj[..., DIFF_QK:2 * DIFF_QK].reshape(B, S, H, 2, Dh).transpose(0, 2, 3, 1, 4)
    v = proj[..., 2 * DIFF_QK:2 * DIFF_QK + DIFF_V].reshape(B, S, H, 2 * Dh).transpose(0, 2, 1, 3)
    xq = proj[..., 2 * DIFF_QK + DIFF_V:]
    lam_init = 0.8 - 0.6 * math.exp(-0.3 * layer_idx)
    lp = lam_p.astype(jnp.float32)
    lam = jnp.exp(jnp.sum(lp[0] * lp[1])) - jnp.exp(jnp.sum(lp[2] * lp[3])) + lam_init
    o = diff_attention(q, k, v, lam, slopes)
    o = rmsnorm(o, norm_g, eps=SUBLN_EPS) * (1.0 - lam_init)
    o = o.transpose(0, 2, 1, 3).reshape(B, S, H * 2 * Dh)
    xo = memory_attention(xq, mem_k, mem_v)
    return jnp.concatenate([o, xo], axis=-1) @ w_out

def mlstm_chunkwise(q, k, v, i_pre, f_pre):
    B, H, S, Dk = q.shape
    Dv = v.shape[-1]
    L = MLSTM_CHUNK
    q = q * (Dk ** -0.5)
    lf = jax.nn.log_sigmoid(f_pre)
    causal = jnp.tril(jnp.ones((L, L), dtype=bool))

    def step(carry, inp):
        C, n, m = carry
        qc, kc, vc, ic, lfc = inp
        b = jnp.cumsum(lfc, axis=-1)
        dmat = jnp.where(causal, b[..., :, None] - b[..., None, :] + ic[..., None, :], -jnp.inf)
        inter = b + m[..., None]
        m_t = jnp.maximum(inter, jnp.max(dmat, axis=-1))
        dec = jnp.exp(inter - m_t)
        sqk = jnp.einsum('bhtd,bhsd->bhts', qc, kc) * jnp.exp(dmat - m_t[..., None])
        num = dec[..., None] * jnp.einsum('bhtd,bhde->bhte', qc, C) + jnp.einsum('bhts,bhse->bhte', sqk, vc)
        den = dec * jnp.einsum('bhtd,bhd->bht', qc, n) + jnp.sum(sqk, axis=-1)
        hc = num / jnp.maximum(jnp.abs(den), jnp.exp(-m_t))[..., None]
        bL = b[..., -1]
        gs = bL[..., None] - b + ic
        m_new = jnp.maximum(bL + m, jnp.max(gs, axis=-1))
        ws = jnp.exp(gs - m_new[..., None])
        carry_dec = jnp.exp(bL + m - m_new)
        C_new = carry_dec[..., None, None] * C + jnp.einsum('bhs,bhsd,bhse->bhde', ws, kc, vc)
        n_new = carry_dec[..., None] * n + jnp.einsum('bhs,bhsd->bhd', ws, kc)
        return (C_new, n_new, m_new), hc

    init = (jnp.zeros((B, H, Dk, Dv), jnp.float32), jnp.zeros((B, H, Dk), jnp.float32),
            jnp.zeros((B, H), jnp.float32))
    xs = (_chunks(q, L), _chunks(k, L), _chunks(v, L), _chunks(i_pre, L), _chunks(lf, L))
    _, hs = lax.scan(step, init, xs)
    return _unchunk(hs)

def mlstm_layer(h, w_in, conv_w, gate_b, norm_g, w_out, mem_k, mem_v):
    B, S, _ = h.shape
    H, Dh, D = MLSTM_HEADS, MLSTM_HEAD_DIM, D_MODEL
    proj = h @ w_in
    qk = jax.nn.silu(causal_conv(proj[..., :2 * D], conv_w))
    q, k = qk[..., :D], qk[..., D:]
    v = proj[..., 2 * D:3 * D]
    o = proj[..., 3 * D:4 * D]
    gates = proj[..., 4 * D:4 * D + 2 * H].astype(jnp.float32).reshape(B, S, 2, H) + gate_b.astype(jnp.float32)
    xq = proj[..., 4 * D + 2 * H:]

    def heads(a):
        return a.reshape(B, S, H, Dh).transpose(0, 2, 1, 3).astype(jnp.float32)

    hh = mlstm_chunkwise(heads(q), heads(k), heads(v),
                         gates[:, :, 0].transpose(0, 2, 1), gates[:, :, 1].transpose(0, 2, 1))
    hh = rmsnorm(hh.transpose(0, 2, 1, 3).astype(h.dtype), norm_g.reshape(H, Dh)).reshape(B, S, D)
    hh = hh * jax.nn.sigmoid(o)
    xo = memory_attention(xq, mem_k, mem_v)
    return jnp.concatenate([hh, xo], axis=-1) @ w_out

def gla_chunkwise(q, k, v, log_a):
    B, H, S, Dk = q.shape
    Dv = v.shape[-1]
    L = GLA_CHUNK
    q = q * (Dk ** -0.5)
    causal = jnp.tril(jnp.ones((L, L), dtype=bool))

    def step(state, inp):
        qc, kc, vc, ac = inp
        b = jnp.cumsum(ac, axis=2)
        inter = jnp.einsum('bhtd,bhde->bhte', qc * jnp.exp(b), state)
        diff = b[:, :, :, None, :] - b[:, :, None, :, :]
        decay = jnp.exp(jnp.where(causal[:, :, None], diff, -jnp.inf))
        amat = jnp.einsum('bhtd,bhsd,bhtsd->bhts', qc, kc, decay)
        intra = jnp.einsum('bhts,bhse->bhte', amat, vc)
        bL = b[:, :, -1]
        k_dec = kc * jnp.exp(bL[:, :, None, :] - b)
        new_state = jnp.exp(bL)[..., None] * state + jnp.einsum('bhsd,bhse->bhde', k_dec, vc)
        return new_state, inter + intra

    init = jnp.zeros((B, H, Dk, Dv), jnp.float32)
    xs = (_chunks(q, L), _chunks(k, L), _chunks(v, L), _chunks(log_a, L))
    _, os_ = lax.scan(step, init, xs)
    return _unchunk(os_)

def gla_layer(h, w_in, gate_w2, gate_b, norm_g, w_out, mem_k, mem_v):
    B, S, _ = h.shape
    H, Dk, Dv = GLA_HEADS, GLA_KEY_DIM, GLA_VALUE_DIM
    kw = H * Dk
    proj = h @ w_in
    q = proj[..., :kw]
    k = proj[..., kw:2 * kw]
    v = proj[..., 2 * kw:2 * kw + D_MODEL]
    g = proj[..., 2 * kw + D_MODEL:2 * kw + 2 * D_MODEL]
    z = proj[..., 2 * kw + 2 * D_MODEL:2 * kw + 2 * D_MODEL + GLA_GATE_RANK]
    xq = proj[..., 2 * kw + 2 * D_MODEL + GLA_GATE_RANK:]
    log_a = jax.nn.log_sigmoid((z @ gate_w2 + gate_b).astype(jnp.float32)) / GLA_TAU

    def heads(a, d):
        return a.reshape(B, S, H, d).transpose(0, 2, 1, 3).astype(jnp.float32)

    o = gla_chunkwise(heads(q, Dk), heads(k, Dk), heads(v, Dv), heads(log_a, Dk))
    o = rmsnorm(o.transpose(0, 2, 1, 3).astype(h.dtype), norm_g.reshape(H, Dv)).reshape(B, S, D_MODEL)
    o = o * jax.nn.silu(g)
    xo = memory_attention(xq, mem_k, mem_v)
    return jnp.concatenate([o, xo], axis=-1) @ w_out

def _layers_of(kind):
    return len(range(kind, DEPTH, N_MIXERS))

def first_inputs(seed: int = 0) -> dict:
    key = jax.random.key(seed)
    keys = iter(jax.random.split(key, 40))

    def nrm(shape, scale):
        return jax.random.normal(next(keys), shape, jnp.float32) * scale

    def gain(shape):
        return 1.0 + nrm(shape, 0.05)

    nA, nB, nC, nD = (_layers_of(kd) for kd in range(N_MIXERS))
    D = D_MODEL
    x = nrm((BATCH, SEQ, D), 1.0)
    mem = nrm((BATCH, MEM_LEN, D), 1.0)
    norm_g = gain((DEPTH, 3, D))
    ffn_w_up = nrm((DEPTH, 2, D, 2 * D_FF), D ** -0.5)
    ffn_w_down = nrm((DEPTH, 2, D_FF, D), D_FF ** -0.5)
    mem_norm_g = gain((D,))
    mem_w_kv = nrm((DEPTH, D, 2 * X_WIDTH), D ** -0.5)
    pool_w_in = nrm((nA, D, POOL_IN), D ** -0.5)
    pool_w_group = nrm((nA, POOL_GROUPS, POOL_GROUP_DIM, POOL_GROUP_DIM), POOL_GROUP_DIM ** -0.5)
    pool_scale = gain((nA, D))
    pool_w_out = nrm((nA, MIX_OUT, D), MIX_OUT ** -0.5)
    diff_w_in = nrm((nB, D, DIFF_IN), D ** -0.5)
    diff_lambda = nrm((nB, 4, DIFF_HEAD_DIM), 0.1)
    diff_norm_g = gain((nB, 2 * DIFF_HEAD_DIM))
    diff_w_out = nrm((nB, MIX_OUT, D), MIX_OUT ** -0.5)
    mlstm_w_in = nrm((nC, D, MLSTM_IN), D ** -0.5)
    mlstm_conv_w = nrm((nC, MLSTM_CONV, 2 * D), MLSTM_CONV ** -0.5)
    i_bias = nrm((nC, MLSTM_HEADS), 0.1)
    f_bias = jnp.linspace(3.0, 6.0, MLSTM_HEADS, dtype=jnp.float32)[None] + nrm((nC, MLSTM_HEADS), 0.01)
    mlstm_gate_b = jnp.stack([i_bias, f_bias], axis=1)
    mlstm_norm_g = gain((nC, D))
    mlstm_w_out = nrm((nC, MIX_OUT, D), MIX_OUT ** -0.5)
    gla_w_in = nrm((nD, D, GLA_IN), D ** -0.5)
    gla_gate_w2 = nrm((nD, GLA_GATE_RANK, GLA_HEADS * GLA_KEY_DIM), GLA_GATE_RANK ** -0.5)
    gla_gate_b = nrm((nD, GLA_HEADS * GLA_KEY_DIM), 0.1)
    gla_norm_g = gain((nD, D))
    gla_w_out = nrm((nD, MIX_OUT, D), MIX_OUT ** -0.5)
    final_norm_g = gain((D,))
    return {'x': x, 'mem': mem, 'norm_g': norm_g, 'ffn_w_up': ffn_w_up, 'ffn_w_down': ffn_w_down,
            'mem_norm_g': mem_norm_g, 'mem_w_kv': mem_w_kv,
            'pool_w_in': pool_w_in, 'pool_w_group': pool_w_group, 'pool_scale': pool_scale, 'pool_w_out': pool_w_out,
            'diff_w_in': diff_w_in, 'diff_lambda': diff_lambda, 'diff_norm_g': diff_norm_g, 'diff_w_out': diff_w_out,
            'mlstm_w_in': mlstm_w_in, 'mlstm_conv_w': mlstm_conv_w, 'mlstm_gate_b': mlstm_gate_b,
            'mlstm_norm_g': mlstm_norm_g, 'mlstm_w_out': mlstm_w_out,
            'gla_w_in': gla_w_in, 'gla_gate_w2': gla_gate_w2, 'gla_gate_b': gla_gate_b,
            'gla_norm_g': gla_norm_g, 'gla_w_out': gla_w_out, 'final_norm_g': final_norm_g}

def first_block(x, mem, norm_g, ffn_w_up, ffn_w_down, mem_norm_g, mem_w_kv,
              pool_w_in, pool_w_group, pool_scale, pool_w_out,
              diff_w_in, diff_lambda, diff_norm_g, diff_w_out,
              mlstm_w_in, mlstm_conv_w, mlstm_gate_b, mlstm_norm_g, mlstm_w_out,
              gla_w_in, gla_gate_w2, gla_gate_b, gla_norm_g, gla_w_out, final_norm_g):
    B, M, _ = mem.shape
    mem_n = rmsnorm(mem, mem_norm_g)
    slopes = alibi_slopes(DIFF_HEADS)
    for i in range(DEPTH):
        kind, j = i % N_MIXERS, i // N_MIXERS
        kv = mem_n @ mem_w_kv[i]
        mem_k = kv[..., :X_WIDTH].reshape(B, M, X_HEADS, X_HEAD_DIM)
        mem_v = kv[..., X_WIDTH:].reshape(B, M, X_HEADS, X_HEAD_DIM)
        x = x + 0.5 * swiglu(rmsnorm(x, norm_g[i, 0]), ffn_w_up[i, 0], ffn_w_down[i, 0])
        h = rmsnorm(x, norm_g[i, 1])
        if kind == 0:
            mix = pool_layer(h, pool_w_in[j], pool_w_group[j], pool_scale[j], pool_w_out[j], mem_k, mem_v)
        elif kind == 1:
            mix = diff_layer(h, diff_w_in[j], diff_lambda[j], diff_norm_g[j], diff_w_out[j], mem_k, mem_v, slopes, i)
        elif kind == 2:
            mix = mlstm_layer(h, mlstm_w_in[j], mlstm_conv_w[j], mlstm_gate_b[j], mlstm_norm_g[j], mlstm_w_out[j],
                              mem_k, mem_v)
        else:
            mix = gla_layer(h, gla_w_in[j], gla_gate_w2[j], gla_gate_b[j], gla_norm_g[j], gla_w_out[j], mem_k, mem_v)
        x = x + mix
        x = x + 0.5 * swiglu(rmsnorm(x, norm_g[i, 2]), ffn_w_up[i, 1], ffn_w_down[i, 1])
    return rmsnorm(x, final_norm_g)


DEPTH_2 = 1

HEAD_DIM = 64
MOBA_HEADS = 8
DSA_HEADS = 8
N_HEADS = MOBA_HEADS + DSA_HEADS
MIX_WIDTH = N_HEADS * HEAD_DIM
MOBA_WIDTH = MOBA_HEADS * HEAD_DIM
DSA_WIDTH = DSA_HEADS * HEAD_DIM
MOBA_BLOCK = 256
MOBA_TOPK = 3
IDX_HEADS = 4
IDX_DIM = 64
DSA_TOPK_MAX = 256
N_BUCKETS = 32
MAX_DISTANCE = 4096
PEER_HEADS = 8
PEER_NKEYS = 128
PEER_EXPERTS = PEER_NKEYS * PEER_NKEYS
PEER_DKEY = 256
PEER_TOPK = 16
Q_CHUNK = 128
T_CHUNK = 128
EPS = 1e-6
PROJ_SIZES = (MOBA_WIDTH, MOBA_WIDTH, MOBA_WIDTH, DSA_WIDTH, DSA_WIDTH, DSA_WIDTH,
              IDX_HEADS * IDX_DIM, IDX_DIM, IDX_HEADS)
PROJ_WIDTH = 3 * MOBA_WIDTH + 3 * DSA_WIDTH + IDX_HEADS * IDX_DIM + IDX_DIM + IDX_HEADS


def rms_norm(x, g):
    xf = x.astype(jnp.float32)
    y = xf * lax.rsqrt(jnp.mean(xf * xf, axis=-1, keepdims=True) + EPS)
    return (y * g).astype(x.dtype)

def modulate(h, shift, scale):
    return h * (1 + scale[:, None, :]) + shift[:, None, :]

def t5_bucket(dist):
    max_exact = N_BUCKETS // 2
    d = jnp.maximum(dist, 0)
    df = jnp.maximum(d, 1).astype(jnp.float32)
    large = max_exact + (jnp.log(df / max_exact) / math.log(MAX_DISTANCE / max_exact)
                         * (N_BUCKETS - max_exact)).astype(jnp.int32)
    return jnp.where(d < max_exact, d, jnp.minimum(large, N_BUCKETS - 1))

def moba_attention(q, k, v, tab):
    B, H, S, Dh = q.shape
    nb = -(-S // MOBA_BLOCK)
    pad = nb * MOBA_BLOCK - S
    kp = jnp.pad(k, ((0, 0), (0, 0), (0, pad), (0, 0))).reshape(B, H, nb, MOBA_BLOCK, Dh)
    vp = jnp.pad(v, ((0, 0), (0, 0), (0, pad), (0, 0))).reshape(B, H, nb, MOBA_BLOCK, Dh)
    k_mean = jnp.mean(kp.astype(jnp.float32), axis=3)
    n_sel = max(min(MOBA_TOPK, nb - 1), 1)
    scale = HEAD_DIM ** -0.5
    bi = jnp.arange(B)[:, None, None, None]
    hi = jnp.arange(H)[None, :, None, None]
    blk = jnp.arange(MOBA_BLOCK)

    def one_chunk(ci):
        t0 = ci * Q_CHUNK
        t = t0 + jnp.arange(Q_CHUNK)
        b0 = t0 // MOBA_BLOCK
        qc = lax.dynamic_slice_in_dim(q, t0, Q_CHUNK, axis=2)
        gate = jnp.einsum('bhqd,bhnd->bhqn', qc.astype(jnp.float32), k_mean)
        gate = jnp.where(jnp.arange(nb) < b0, gate, -jnp.inf)
        _, sel = lax.top_k(gate, n_sel)
        sel_ok = sel < b0
        kg = kp[bi, hi, sel]
        vg = vp[bi, hi, sel]
        s_sel = jnp.einsum('bhqd,bhqjkd->bhqjk', qc, kg).astype(jnp.float32) * scale
        pos_sel = sel[..., None] * MOBA_BLOCK + blk
        s_sel = s_sel + tab[hi[..., None], t5_bucket(t[:, None, None] - pos_sel)]
        s_sel = jnp.where(sel_ok[..., None], s_sel, -jnp.inf).reshape(B, H, Q_CHUNK, n_sel * MOBA_BLOCK)
        ko = lax.dynamic_index_in_dim(kp, b0, axis=2, keepdims=False)
        vo = lax.dynamic_index_in_dim(vp, b0, axis=2, keepdims=False)
        pos_own = b0 * MOBA_BLOCK + blk
        s_own = jnp.einsum('bhqd,bhkd->bhqk', qc, ko).astype(jnp.float32) * scale
        s_own = s_own + jnp.take(tab, t5_bucket(t[:, None] - pos_own[None, :]), axis=1)[None]
        s_own = jnp.where(pos_own[None, :] <= t[:, None], s_own, -jnp.inf)
        p = jax.nn.softmax(jnp.concatenate([s_sel, s_own], axis=-1), axis=-1).astype(v.dtype)
        p_sel = p[..., :n_sel * MOBA_BLOCK].reshape(B, H, Q_CHUNK, n_sel, MOBA_BLOCK)
        p_own = p[..., n_sel * MOBA_BLOCK:]
        return (jnp.einsum('bhqjk,bhqjkd->bhqd', p_sel, vg)
                + jnp.einsum('bhqk,bhkd->bhqd', p_own, vo))

    out = lax.map(one_chunk, jnp.arange(S // Q_CHUNK))
    return jnp.transpose(out, (1, 2, 0, 3, 4)).reshape(B, H, S, Dh)

def dsa_attention(q, k, v, q_idx, k_idx, w_idx, tab):
    B, S, H, Dh = q.shape
    topk = min(DSA_TOPK_MAX, S // 4)
    scale = HEAD_DIM ** -0.5
    keys = jnp.arange(S)
    bi = jnp.arange(B)[:, None, None]

    def one_chunk(ci):
        t0 = ci * Q_CHUNK
        t = t0 + jnp.arange(Q_CHUNK)
        qi = lax.dynamic_slice_in_dim(q_idx, t0, Q_CHUNK, axis=1)
        wi = lax.dynamic_slice_in_dim(w_idx, t0, Q_CHUNK, axis=1)
        qc = lax.dynamic_slice_in_dim(q, t0, Q_CHUNK, axis=1)
        rel = jax.nn.relu(jnp.einsum('bqhd,bsd->bqhs', qi, k_idx).astype(jnp.float32))
        score = jnp.einsum('bqh,bqhs->bqs', wi.astype(jnp.float32), rel)
        score = jnp.where(keys[None, None, :] <= t[None, :, None], score, -jnp.inf)
        _, idx = lax.top_k(score, topk)
        kg = k[bi, idx]
        vg = v[bi, idx]
        s = jnp.einsum('bqhd,bqkhd->bhqk', qc, kg).astype(jnp.float32) * scale
        bias = jnp.moveaxis(jnp.take(tab, t5_bucket(t[None, :, None] - idx), axis=1), 0, 1)
        s = jnp.where((idx <= t[None, :, None])[:, None], s + bias, -jnp.inf)
        p = jax.nn.softmax(s, axis=-1).astype(v.dtype)
        return jnp.einsum('bhqk,bqkhd->bqhd', p, vg)

    out = lax.map(one_chunk, jnp.arange(S // Q_CHUNK))
    return jnp.transpose(out, (1, 0, 2, 3, 4)).reshape(B, S, H * Dh)

def hybrid_mixer(h, w_in, w_out, rel_bias):
    B, S, _ = h.shape
    proj = h @ w_in
    parts = []
    off = 0
    for size in PROJ_SIZES:
        parts.append(proj[..., off:off + size])
        off += size
    mq, mk, mv, dq, dk, dv, iq, ik, iw = parts
    to_bhsd = lambda t, nh: jnp.transpose(t.reshape(B, S, nh, HEAD_DIM), (0, 2, 1, 3))
    to_bshd = lambda t, nh: t.reshape(B, S, nh, HEAD_DIM)
    y_moba = moba_attention(to_bhsd(mq, MOBA_HEADS), to_bhsd(mk, MOBA_HEADS),
                            to_bhsd(mv, MOBA_HEADS), rel_bias[:MOBA_HEADS])
    y_moba = jnp.transpose(y_moba, (0, 2, 1, 3)).reshape(B, S, MOBA_WIDTH)
    ikf = ik.astype(jnp.float32)
    ik_n = (ikf * lax.rsqrt(jnp.mean(ikf * ikf, axis=-1, keepdims=True) + EPS)).astype(ik.dtype)
    y_dsa = dsa_attention(to_bshd(dq, DSA_HEADS), to_bshd(dk, DSA_HEADS), to_bshd(dv, DSA_HEADS),
                          iq.reshape(B, S, IDX_HEADS, IDX_DIM), ik_n, iw * IDX_HEADS ** -0.5,
                          rel_bias[MOBA_HEADS:])
    y = jnp.concatenate([y_moba, y_dsa], axis=-1)
    return y @ w_out

def peer_ffn(h, w_query, sub_keys, u_emb, v_emb):
    B, S, D = h.shape

    def one_chunk(ci):
        hc = lax.dynamic_slice_in_dim(h, ci * T_CHUNK, T_CHUNK, axis=1)
        q = (hc @ w_query).reshape(B, T_CHUNK, PEER_HEADS, 2, PEER_DKEY // 2)
        s = jnp.einsum('bthpd,hpnd->bthpn', q, sub_keys).astype(jnp.float32)
        s_top, i_top = lax.top_k(s, PEER_TOPK)
        cand = (s_top[..., 0, :, None] + s_top[..., 1, None, :]).reshape(B, T_CHUNK, PEER_HEADS, PEER_TOPK * PEER_TOPK)
        cand_idx = (i_top[..., 0, :, None] * PEER_NKEYS + i_top[..., 1, None, :]).reshape(cand.shape)
        g_s, pos = lax.top_k(cand, PEER_TOPK)
        e_idx = jnp.take_along_axis(cand_idx, pos, axis=-1)
        g = jax.nn.softmax(g_s, axis=-1)
        u = u_emb[e_idx]
        act = jax.nn.gelu(jnp.einsum('btd,bthkd->bthk', hc, u).astype(jnp.float32), approximate=False)
        return jnp.einsum('bthk,bthkd->btd', (g * act).astype(h.dtype), v_emb[e_idx])

    out = lax.map(one_chunk, jnp.arange(S // T_CHUNK))
    return jnp.transpose(out, (1, 0, 2, 3)).reshape(B, S, D)

def second_inputs(seed: int = 0) -> dict:
    key = jax.random.key(seed)
    ks = jax.random.split(key, 14)
    f32 = jnp.float32
    nrm = lambda k, shape, s: jax.random.normal(k, shape, f32) * s
    return {
        'x': nrm(ks[0], (BATCH, SEQ, D_MODEL), 1.0),
        'c': nrm(ks[1], (BATCH, D_MODEL), 1.0),
        'w_ada': nrm(ks[2], (DEPTH_2, D_MODEL, 6 * D_MODEL), 0.5 * D_MODEL ** -0.5),
        'b_ada': nrm(ks[3], (DEPTH_2, 6 * D_MODEL), 0.02),
        'norm_attn': 1.0 + nrm(ks[4], (DEPTH_2, D_MODEL), 0.02),
        'norm_ffn': 1.0 + nrm(ks[5], (DEPTH_2, D_MODEL), 0.02),
        'w_in': nrm(ks[6], (DEPTH_2, D_MODEL, PROJ_WIDTH), D_MODEL ** -0.5),
        'w_out': nrm(ks[7], (DEPTH_2, MIX_WIDTH, D_MODEL), MIX_WIDTH ** -0.5),
        'rel_bias': nrm(ks[8], (N_HEADS, N_BUCKETS), 0.5),
        'peer_wq': nrm(ks[9], (DEPTH_2, D_MODEL, PEER_HEADS * PEER_DKEY), D_MODEL ** -0.5),
        'peer_subkeys': nrm(ks[10], (DEPTH_2, PEER_HEADS, 2, PEER_NKEYS, PEER_DKEY // 2), (PEER_DKEY // 2) ** -0.5),
        'peer_u': nrm(ks[11], (DEPTH_2, PEER_EXPERTS, D_MODEL), D_MODEL ** -0.5),
        'peer_v': nrm(ks[12], (DEPTH_2, PEER_EXPERTS, D_MODEL), PEER_HEADS ** -0.5),
        'norm_final': 1.0 + nrm(ks[13], (D_MODEL,), 0.02),
    }

def second_block(x, c, w_ada, b_ada, norm_attn, norm_ffn, w_in, w_out, rel_bias,
              peer_wq, peer_subkeys, peer_u, peer_v, norm_final):
    mod = jnp.einsum('bd,lde->lbe', jax.nn.silu(c), w_ada) + b_ada[:, None, :]
    for l in range(DEPTH_2):
        sh1, sc1, g1, sh2, sc2, g2 = jnp.split(mod[l], 6, axis=-1)
        h = modulate(rms_norm(x, norm_attn[l]), sh1, sc1)
        x = x + g1[:, None, :] * hybrid_mixer(h, w_in[l], w_out[l], rel_bias)
        h = modulate(rms_norm(x, norm_ffn[l]), sh2, sc2)
        x = x + g2[:, None, :] * peer_ffn(h, peer_wq[l], peer_subkeys[l], peer_u[l], peer_v[l])
    return rms_norm(x, norm_final)


def setup_inputs(seed=0):
    out = dict(first_inputs(seed))
    for name, value in second_inputs(seed + 1).items():
        if name != "x":
            out[name + "_2"] = value
    return out


def reference(
    x, mem, norm_g, ffn_w_up, ffn_w_down, mem_norm_g, mem_w_kv, pool_w_in, pool_w_group,
    pool_scale, pool_w_out, diff_w_in, diff_lambda, diff_norm_g, diff_w_out, mlstm_w_in,
    mlstm_conv_w, mlstm_gate_b, mlstm_norm_g, mlstm_w_out, gla_w_in, gla_gate_w2, gla_gate_b,
    gla_norm_g, gla_w_out, final_norm_g, c_2, w_ada_2, b_ada_2, norm_attn_2, norm_ffn_2, w_in_2,
    w_out_2, rel_bias_2, peer_wq_2, peer_subkeys_2, peer_u_2, peer_v_2, norm_final_2,
):
    x = first_block(
        x, mem, norm_g, ffn_w_up, ffn_w_down, mem_norm_g, mem_w_kv, pool_w_in, pool_w_group,
        pool_scale, pool_w_out, diff_w_in, diff_lambda, diff_norm_g, diff_w_out, mlstm_w_in,
        mlstm_conv_w, mlstm_gate_b, mlstm_norm_g, mlstm_w_out, gla_w_in, gla_gate_w2,
        gla_gate_b, gla_norm_g, gla_w_out, final_norm_g,
    )
    return second_block(
        x, c_2, w_ada_2, b_ada_2, norm_attn_2, norm_ffn_2, w_in_2, w_out_2, rel_bias_2,
        peer_wq_2, peer_subkeys_2, peer_u_2, peer_v_2, norm_final_2,
    )


_drawn_inputs = setup_inputs


def setup_inputs(seed=0):
    import zlib

    import numpy as np

    out = dict(_drawn_inputs(seed))
    spreads = {}
    factors = {'mem_norm_g': 6.435,
     'b_ada_2': 3.271,
     'norm_attn_2': 6.142,
     'norm_ffn_2': 6.134,
     'norm_final_2': 2.776}
    for name, (base, spread) in spreads.items():
        noise = np.random.default_rng([zlib.crc32(name.encode()), seed]).standard_normal(out[name].shape)
        drawn = base * np.exp(spread * noise) if base else spread * noise
        out[name] = __import__('jax').numpy.asarray(drawn.astype(out[name].dtype))
    for name, factor in factors.items():
        out[name] = (out[name] * factor).astype(out[name].dtype)
    return out
```

```python
import math

import concourse.bass as bass
from concourse import mybir
from contextlib import ExitStack

F32 = mybir.dt.float32
F32R = mybir.dt.float32r
I32 = mybir.dt.int32
U32 = mybir.dt.uint32
ALU = mybir.AluOpType
ACT = mybir.ActivationFunctionType
AX = mybir.AxisListType

D = 1024
T = 256
KT = D // 128
FF = 2816
FT = FF // 128
NEG = -1.0e30
TAKEN = -3.0e38
BUCKET_START = [*range(16), 23, 32, 46, 64, 91, 128, 182]
TOPK = min(256, T // 4)
NG = 8
GROUPS = 128 // NG
STOP = 99


def bucket_ranges():
    starts = [*range(16), 16, 23, 32, 46, 64, 91, 128, 182]
    return [(b, s, (starts[b + 1] if b + 1 < len(starts) else T)) for b, s in enumerate(starts)]


def program(nc, a, out):
    ctx = ExitStack()
    stage_a = ExitStack()

    def sb(name, shape, dt=F32, where=None):
        return (where or ctx).enter_context(nc.sbuf_tensor(name, shape, dt))

    def sem(name):
        return ctx.enter_context(nc.semaphore(name))

    xT = sb("xT", [128, KT, T])
    ident = sb("ident", [128, 128])
    ones = sb("ones", [128, 128])
    cols = sb("cols", [128, 104])
    modc = sb("modc", [128, 48])
    badac = sb("badac", [128, 48])
    silc = sb("silc", [128, KT])
    eps = sb("eps", [128, 4])
    gmod = sb("gmod", [128, 2 * KT])
    rstd = sb("rstd", [128, T])
    small = sb("small", [128, 64])
    lam = sb("lam", [128, 384])
    st = sb("st", [128, 32])
    M = sb("M", [128, 3072 + 8704])
    WR = sb("WR", [128, 2, 4096], F32, stage_a)
    WH = sb("WH", [128, 2, 2048], F32R, stage_a)
    WL = sb("WL", [128, 2, 2048], F32R, stage_a)
    hTh = sb("hTh", [128, KT, T], F32R, stage_a)
    hTl = sb("hTl", [128, KT, T], F32R, stage_a)
    actH = sb("actH", [128, FT, T], F32R, stage_a)
    actL = sb("actL", [128, FT, T], F32R, stage_a)
    adaW = sb("adaW", [128, KT, 128], F32, stage_a)
    adaS = sb("adaS", [128, 2, 512], F32, stage_a)
    memK = sb("memK", [128, 2, 4, T], F32, stage_a)
    memV = sb("memV", [128, 2, 2, 512], F32, stage_a)
    stage_a.close()
    GU = sb("GU", [128, 2, NG, D])
    GV = sb("GV", [128, 2, NG, D])
    xtok = sb("xtok", [128, 2, D])
    htok = sb("htok", [128, 2, D])
    P = [ctx.enter_context(nc.psum_tensor(f"P{i}", [128, 512], F32)) for i in range(8)]
    rel_rows = nc.dram_tensor("rel_rows", (16, 128 * 512), F32, kind="Internal").ap()

    def view(at, *shape):
        n = math.prod(shape)
        v = M[:, at:at + n]
        if len(shape) == 1:
            return v
        names = "abcd"[:len(shape)]
        return v.rearrange(f"p ({' '.join(names)}) -> p {' '.join(names)}",
                           **dict(zip(names[1:], shape[1:])))

    NT = view(0, KT, T)
    LB = view(0, 2, 4, T)
    SIL = view(2048, 2, T)
    PRD = view(2560, 2, T)
    PTS = view(2048, 2, 2, T)
    MX = 3072
    xin, memin, memT = view(MX, 2, D), view(MX + 2048, 2, D), view(MX + 4096, KT, T)
    rows1 = view(MX + 6144, 128)
    rows2 = view(MX + 6272, 128)
    relr = view(MX + 6400, 512)
    relz = view(MX + 6912, 512)
    reltab = view(MX + 7424, 32)
    PADW = T + 16
    uT = view(MX, KT, PADW)
    wa = view(MX + 2176, 2, PADW)
    wb = view(MX + 2720, 2, PADW)
    inv = view(MX + 3264, 4, T)
    xq0 = view(MX + 4288, 4, T)
    ptmp = view(MX + 5312, KT, T)
    dQ, dK, dV = view(MX, 8, T), view(MX + 2048, 8, T), view(MX + 4096, 2, D)
    xq1 = view(MX + 6144, 4, T)
    dist = view(MX + 7168, 2, T)
    bias1 = view(MX + 7680, 2, 2, T)
    lamw = lam[:, 0:256].rearrange("p (a b) -> p a b", a=4)
    lamp = lam[:, 256:384].rearrange("p (a b) -> p a b", a=2)
    hQ, hK, hV = view(MX, 8, T), view(MX + 2048, 8, T), view(MX + 4096, 2, 1024)
    iQ, iK = view(MX + 6144, 2, T), view(MX + 6656, T)
    pen = view(MX + 6912, 2, T)
    bias2 = view(MX + 7424, 2, 2, T)
    iw = small[:, 32:40].rearrange("p (a b) -> p a b", a=2)
    score, work, relu2 = view(0, 2, T), view(512, 2, T), view(1024, 2, 2, T)
    pQ = view(MX, 16, T)
    skT = view(MX + 4096, 16, 128)
    skin = view(MX + 6144, 16, 128)

    diag = view(MX, 2, NG, 128)
    tmpf = view(MX + 2048, D)
    zro = view(MX + 3072, 128)
    dots = view(MX + 3200, 2, NG)
    gel8 = view(MX + 3232, 2, NG)
    coef8 = view(MX + 3264, 2, NG)
    eidx = view(MX + 8192, 256).bitcast(I32)
    gate = view(MX + 8448, 2, 8, 16)
    gatec = view(MX + 8448, 256)
    idxu = view(MX + 3840, 2, NG).bitcast(I32)
    idxv = view(MX + 3872, 2, NG).bitcast(I32)
    gfin = view(MX + 6144, D)
    g2bc = view(MX + 7168, D)
    gvf = GV[:].rearrange("p a b c -> p (a b c)")
    sks = gvf[:, 0:4096].rearrange("p (t h n) -> p t h n", t=2, h=16)
    skw = gvf[:, 4096:6144].rearrange("p (h n) -> p h n", h=16)
    cand = gvf[:, 6144:8192].rearrange("p (h i j) -> p h i j", h=8, i=16)
    candw = gvf[:, 4096:6144].rearrange("p (h n) -> p h n", h=8)
    hot = gvf[:, 8192:10240].rearrange("p (h k i) -> p h k i", h=8, k=16)
    posd = gvf[:, 10240:10496].rearrange("p (a n) -> p a n", a=2)
    posf = gvf[:, 10496:10752].rearrange("p (a n) -> p a n", a=2)
    psel = gvf[:, 10752:11008].rearrange("p (a n) -> p a n", a=2)
    iota16 = gvf[:, 11008:11024]
    v16 = gvf[:, 11264:11776].rearrange("p (t h n) -> p t h n", t=2, h=16)
    i16 = gvf[:, 11776:12288].rearrange("p (t h n) -> p t h n", t=2, h=16).bitcast(U32)
    i16f = gvf[:, 12288:12800].rearrange("p (t h n) -> p t h n", t=2, h=16)
    gs = gvf[:, 12800:13056].rearrange("p (t h n) -> p t h n", t=2, h=8)
    pos = gvf[:, 13056:13312].rearrange("p (t h n) -> p t h n", t=2, h=8).bitcast(U32)

    G_NORM, G_MEM, G_POOL, G_ATT, G_FFN, G_C, G_FIN, G_DIFF = 0, 48, 56, 64, 72, 80, 88, 96

    names = """x_landed mem_landed rows_landed rel_landed rel_stored iden_ready const_ready x_tr x_in mem_tr mem_in
        cols_tr cols_ready silc_ready hi_ready lo_ready half_used bank_free sq_ready ss_ready std_ready rstd_ready
        hn_ready hh_ready hl_ready sil_ready act_hi act_lo x_ready dve_chain pool_chain ada_landed ada_sum
        ada_done mod_ready gmod_ready lam_landed lam_ready lam_exp neglam_ready inv_ready pad_ready pooled_ready pool_hi pool_lo
        group_done mix_hi mix_lo score_done logits_ready neg_max exp_done rsum_ready prob_ready
        diffp_ready tr_done pt_ready o_done o_hi o_ready bias_ready dist_ready osq_ready oss_ready ostd_ready
        on_ready on_hi on_lo ik_sq ik_ss ik_std ik_ready idx_products idx_relu idx_summed masked_ready iota_ready pen_ready bias_landed
        sk_landed sk_tr sk_ready htok_tr htok_ready xtok_tr xtok_ready sk_scores s_ready gdiff_ready gexp_ready gate_ready
        index_ready dots_ready gelu_ready coef_ready diag_ready v_used iu_ready iv_ready g2_diag g2_tr g2_ready gfin_landed
        acc_done xf_ready fss_ready fstd_ready y_ready stored peer_free zero_ready""".split()
    S = {n: sem(n) for n in names}
    raw_landed = [sem("raw_landed0"), sem("raw_landed1")]
    u_landed = [sem("u_landed0"), sem("u_landed1")]
    v_landed = [sem("v_landed0"), sem("v_landed1")]
    b_landed = [sem("b_landed0"), sem("b_landed1")]

    def kview(w):
        return w.rearrange("(k p) n -> p k n", p=128)

    chunks = []

    def raw(slot, kind, h):
        r = WR[:, slot, :]
        if kind == "cols":
            return r.rearrange("p (k n) -> p k n", k=KT)[:, :, h * 256:h * 256 + 256]
        if kind == "pair":
            return r.rearrange("p (k g j n) -> p k g j n", k=KT, g=2, j=2)[:, :, :, h, :]
        return r[:, h * 2048:h * 2048 + 2048]

    def raw_dst(slot, kind, part):
        r = WR[:, slot, :]
        if kind in ("cols", "pair"):
            return r.rearrange("p (k n) -> p k n", k=KT)[:, :, part * 256:part * 256 + 256]
        return r[:, part * 2048:part * 2048 + 2048].rearrange("p (k n) -> p k n", k=2)

    def split_view(buf, u, kind):
        b = buf[:, u, :]
        if kind == "cols":
            return b.rearrange("p (k n) -> p k n", k=KT)
        if kind == "pair":
            return b.rearrange("p (k g n) -> p k g n", k=KT, g=2)
        return b

    def add_cols(w, n0, special=None):
        chunks.append(("cols", 2, [kview(w)[:, :, n0 + 256 * q:n0 + 256 * q + 256] for q in range(2)], special))

    def add_rows(w, kts):
        for k in range(0, kts, 4):
            parts = [kview(w)[:, k + 2 * q:k + 2 * q + 2, :] for q in range(2) if k + 2 * q < kts]
            chunks.append(("rows", len(parts), parts, None))

    phases = {}
    state = dict(U=0, C=0, E=0)

    def phase(name, add):
        c0 = len(chunks)
        add()
        n = sum(c[1] for c in chunks[c0:])
        phases[name] = dict(U=state["U"], C=c0, n=n, nc=len(chunks) - c0)
        state["U"] += n

    def cols_phase(name, w, n_chunks, n0=0):
        phase(name, lambda: [add_cols(w, n0 + 512 * i) for i in range(n_chunks)])
        phases[name]["E"] = state["E"]
        state["E"] += phases[name]["n"]

    def ffn(i, f):
        def up():
            w = kview(a["ffn_w_up"][i, f])
            for c in range(FF // 256):
                chunks.append(("pair", 2, [w[:, :, g * FF + c * 256:g * FF + c * 256 + 256] for g in range(2)], None))
        phase(f"up{i}{f}", up)
        phases[f"up{i}{f}"]["E"] = state["E"]
        state["E"] += phases[f"up{i}{f}"]["n"]
        phase(f"down{i}{f}", lambda: add_rows(a["ffn_w_down"][i, f], FT))

    cols_phase("kv0", a["mem_w_kv"][0], 2)
    cols_phase("kv1", a["mem_w_kv"][1], 2)
    ffn(0, 0)
    cols_phase("pool_in", a["pool_w_in"][0], 3)

    def pool_group():
        w = a["pool_w_group"][0].rearrange("g (c p) n -> p (g c) n", p=128)
        chunks.append(("group", 2, [w[:, 4 * q:4 * q + 4, :] for q in range(2)], None))
    phase("group", pool_group)
    phases["group"]["E"] = state["E"]
    state["E"] += 4
    phase("pool_out", lambda: add_rows(a["pool_w_out"][0], 12))
    ffn(0, 1)
    ffn(1, 0)
    cols_phase("diff_in", a["diff_w_in"][0], 7)
    phase("diff_out", lambda: add_rows(a["diff_w_out"][0], 12))
    ffn(1, 1)
    w2 = a["w_in_2"][0]
    cols_phase("in2", w2, 6)
    phase("in2x", lambda: chunks.append(("cols", 2, [kview(w2)[:, :, 3072:3328]], "index")))
    phases["in2x"]["E"] = state["E"]
    state["E"] += 2
    phase("out2", lambda: add_rows(a["w_out_2"][0], KT))
    cols_phase("wq", a["peer_wq_2"][0], 4)

    half_of = []
    for c, ch in enumerate(chunks):
        half_of += [(c, h) for h in range(ch[1])]
    last_half = [max(u for u, (cc, _) in enumerate(half_of) if cc == c) for c in range(len(chunks))]
    slot_loads = []
    total = [0, 0]
    for c, ch in enumerate(chunks):
        total[c % 2] += 16 * (4 if ch[3] == "index" else len(ch[2]))
        slot_loads.append(total[c % 2])

    block = ctx.enter_context(nc.Block())

    X_AFTER = {n: 4 * (i + 1) for i, n in enumerate(
        ["input", "down00", "pool_out", "down01", "down10", "diff_out", "down11", "final", "out2"])}
    ATT = dict(mem0=0, diff=4, mem1=12, moba=16, dsa=24)
    NORMS = dict(mem=(0, G_MEM, 0), up00=(1, G_NORM, 1), pool_in=(2, G_NORM + 8, 2), up01=(3, G_NORM + 16, 3),
                 up10=(4, G_NORM + 24, 4), diff_in=(5, G_NORM + 32, 5), up11=(6, G_NORM + 40, 6), final=(7, G_FIN, None),
                 in2=(8, None, 7), wq=(9, None, 8))
    LAM_INIT = 0.8 - 0.6 * math.exp(-0.3 * 1)

    def heads_of(kind):
        if kind in ("mem0", "mem1"):
            l = int(kind[3])
            xq = xq1 if l else xq0
            return [dict(a=ATT[kind] + h, qk=[(xq[:, h], memK[:, l, h])], v=lambda s, h=h: memV[:, l, s, h * 128:h * 128 + 128],
                         scale=128.0 ** -0.5, rows=(0, 128), tile=8 + h, bias=None, split=True) for h in range(4)]
        if kind == "diff":
            return [dict(a=ATT[kind] + h, qk=[(dQ[64 * c:64 * c + 64, h], dK[64 * c:64 * c + 64, h]) for c in range(2)],
                         v=lambda s, h=h: dV[:, s, h * 128:h * 128 + 128], scale=0.125, rows=(0, 128), tile=h,
                         bias=bias1[:, h % 2], bias_sem=(S["bias_ready"], h + 1), split=False, head=h) for h in range(8)]
        out = []
        for h in range(16):
            r = slice(64 * (h % 2), 64 * (h % 2) + 64)
            s = (S["bias_ready"], h + 1) if h >= 8 else (b_landed[h % 2], 32 * (h // 2 + 1))
            out.append(dict(a=ATT["moba"] + h, qk=[(hQ[r, h // 2], hK[r, h // 2])], v=lambda s, h=h: hV[:, s, h * 64:h * 64 + 64],
                            scale=0.125, rows=(r.start, r.stop), tile=h // 2, bias=bias2[:, h % 2], bias_sem=s,
                            split=True))
        return out

    ADA = {}
    for i, (name, h) in enumerate([("down00", 0), ("down00", 4), ("down00", 8), ("pool_in", 1), ("pool_in", 3), ("pool_in", 5),
                                   ("down01", 0), ("down01", 4), ("down01", 8), ("down10", 0), ("down10", 4), ("down10", 8)]):
        ADA[(name, h)] = i

    def rb(x):
        return 16 * (x % 2)

    def nmax(x, j):
        return st[:, rb(x) + j:rb(x) + j + 1]

    def rsum(x, j):
        return st[:, rb(x) + 4 + j:rb(x) + 5 + j]

    def rinv(x, j):
        return st[:, rb(x) + 8 + j:rb(x) + 9 + j]

    class Chain:
        def __init__(self, eng, s):
            self.eng, self.s, self.n = eng, s, 0

        def __call__(self, ins):
            self.n += 1
            ins.then_inc(self.s, 1)
            self.eng.wait_ge(self.s, self.n)

    @block.sync
    def _(sp):
        sp.dma_start(xin, a["x"][0].rearrange("(a p) n -> p a n", p=128)).then_inc(S["x_landed"], 16)
        sp.dma_start(memin, a["mem"][0].rearrange("(a p) n -> p a n", p=128)).then_inc(S["mem_landed"], 16)

        def vec(w):
            return w.rearrange("(a n) -> a n", n=128)
        loads = [(rows1, 0, a["norm_g"].rearrange("l s (a n) -> (l s a) n", n=128), 48), (rows1, G_MEM, vec(a["mem_norm_g"]), 8),
                 (rows1, G_POOL, vec(a["pool_scale"][0]), 8), (rows1, G_ATT, vec(a["norm_attn_2"][0]), 8),
                 (rows1, G_FFN, vec(a["norm_ffn_2"][0]), 8), (rows1, G_C, vec(a["c_2"][0]), 8),
                 (rows1, G_FIN, vec(a["final_norm_g"]), 8), (rows1, G_DIFF, a["diff_norm_g"], 1),
                 (rows2, 0, vec(a["b_ada_2"][0]), 48)]
        for r, at, src, n in loads:
            sp.dma_start(r[at:at + n, :], src).then_inc(S["rows_landed"], 16)

        def load(c):
            kind, n, parts, special = chunks[c]
            if c >= 2:
                sp.wait_ge(S["lo_ready"], last_half[c - 2] + 1)
            for q, src in enumerate(parts):
                sp.dma_start(raw_dst_of(c % 2, kind, q), src).then_inc(raw_landed[c % 2], 16)
            if special == "index":
                r = WR[:, c % 2, :].rearrange("p (k n) -> p k n", k=KT)
                for at, n0, n in ((256, 3328, 64), (320, 3328, 64), (384, 3392, 4)):
                    sp.dma_start(r[:, :, at:at + n], kview(w2)[:, :, n0:n0 + n]).then_inc(raw_landed[c % 2], 16)

        def raw_dst_of(slot, kind, part):
            if kind == "group":
                return WR[:, slot, part * 1024:part * 1024 + 1024].rearrange("p (k n) -> p k n", k=4)
            return raw_dst(slot, kind, part)

        def load_up(i, f):
            p = phases[f"up{i}{f}"]
            for c in range(3):
                load(p["C"] + c)
            w = kview(a["ffn_w_up"][i, f])
            with sp.Fori(0, 4) as r:
                for j in range(2):
                    c = 3 + j
                    sp.wait_ge(S["lo_ready"], r * 4 + last_half[p["C"] + c - 2] + 1)
                    for g in range(2):
                        sp.dma_start(raw_dst_of((p["C"] + c) % 2, "pair", g),
                                     w[:, :, bass.ds(r * 512 + (g * FF + c * 256), 256)]).then_inc(raw_landed[(p["C"] + c) % 2], 16)

        for name, p in phases.items():
            if name.startswith("up"):
                load_up(int(name[2]), int(name[3]))
            else:
                for c in range(p["C"], p["C"] + p["nc"]):
                    load(c)
        for t in range(2):
            sp.wait_ge(S["y_ready"], t + 1)
            sp.dma_start(out[0, t * 128:t * 128 + 128, :], xtok[:, t, :]).then_inc(S["stored"], 16)
        sp.wait_ge(S["stored"], 32)

    @block.gpsimd
    def _(pool):
        chain = Chain(pool, S["pool_chain"])
        pool.dma_start(reltab[0:16, :], a["rel_bias_2"]).then_inc(S["rel_landed"], 16)
        chain(nc.gpsimd.memset(ident[:], 0.0))
        nc.gpsimd.affine_select(out=ident[:], in_=ident[:], compare_op=ALU.not_equal, fill=1.0, base=0,
                                pattern=[[-1, 128]], channel_multiplier=1).then_inc(S["iden_ready"], 1)
        nc.gpsimd.memset(small[:, :], 0.0)
        nc.gpsimd.memset(eps[:, 0:1], 1e-6)
        nc.gpsimd.memset(eps[:, 1:2], 1e-5)
        nc.gpsimd.memset(ones[:], 1.0).then_inc(S["const_ready"], 1)
        nc.gpsimd.memset(relz[0:16, :], 0.0)
        chain(nc.gpsimd.memset(relr[0:16, :], NEG))
        pool.wait_ge(S["rel_landed"], 16)
        for b, lo, hi in bucket_ranges():
            if hi > lo:
                last = nc.gpsimd.tensor_scalar(relr[0:16, T - hi:T - lo], relz[0:16, T - hi:T - lo], reltab[0:16, b:b + 1],
                                               None, ALU.add)
        chain(last)
        pool.dma_start(rel_rows.rearrange("h (r n) -> h r n", n=512), relr[0:16, :].unsqueeze(1).broadcast_to([16, 128, 512])).then_inc(S["rel_stored"], 16)

        pool.wait_ge(S["silc_ready"], 1)
        wada = kview(a["w_ada_2"][0])
        cb = silc[:, :].unsqueeze(2).broadcast_to([128, KT, 128])
        base = chain.n

        def ada_piece(dram, buf, steps, landed, sums):
            for q in range(4):
                pool.dma_start(adaW[:], dram(q)).then_inc(S["ada_landed"], 16)
                pool.wait_ge(S["ada_landed"], landed(q))
                nc.gpsimd.tensor_tensor(adaW[:], adaW[:], cb, ALU.mult).then_inc(S["pool_chain"], 1)
                pool.wait_ge(S["pool_chain"], steps(3 * q + 1))
                nc.gpsimd.tensor_tensor(adaW[:, 0:4], adaW[:, 0:4], adaW[:, 4:8], ALU.add).then_inc(S["pool_chain"], 1)
                pool.wait_ge(S["pool_chain"], steps(3 * q + 2))
                nc.gpsimd.tensor_tensor(adaW[:, 0:2], adaW[:, 0:2], adaW[:, 2:4], ALU.add).then_inc(S["pool_chain"], 1)
                pool.wait_ge(S["pool_chain"], steps(3 * q + 3))
                nc.gpsimd.tensor_tensor(adaS[:, buf, q * 128:q * 128 + 128], adaW[:, 0], adaW[:, 1], ALU.add)\
                    .then_inc(S["ada_sum"], 1)
                pool.wait_ge(S["ada_sum"], sums(q + 1))

        for n in range(2):
            ada_piece(lambda q: wada[:, :, n * 512 + q * 128:n * 512 + q * 128 + 128], n,
                      lambda k: base + n * 12 + k, lambda q: n * 64 + 16 * q + 16, lambda k: 4 * n + k)

        def ada_pairs(first, n):
            with pool.Fori(0, n) as r:
                for m in range(2):
                    i = 2 * first + m
                    pool.wait_ge(S["ada_done"], r * 2 + (i - 1))
                    nc.gpsimd.tensor_tensor(small[:, 61:62], ones[:, 0:1], ones[:, 0:1], ALU.add)
                    ada_piece(lambda q: wada[:, :, bass.ds(r * 1024 + (i * 512 + q * 128), 128)], m,
                              lambda k: r * 24 + (base + 12 * i + k), lambda q: r * 128 + (i * 64 + 16 * q + 16),
                              lambda k: r * 8 + (4 * i + k))
        ada_pairs(1, 1)

        pool.wait_ge(S["x_ready"], X_AFTER["down00"])
        nc.gpsimd.memset(uT[:, :, 0:16], 0.0)
        nc.gpsimd.memset(wa[:, :, 0:16], 0.0)
        nc.gpsimd.memset(wb[:, :, 0:16], 0.0)
        nc.gpsimd.iota(inv[:], pattern=[[0, 4], [1, T]], base=1, channel_multiplier=0,
                       allow_small_or_imprecise_dtypes=True).then_inc(S["pad_ready"], 1)

        ada_pairs(2, 2)

        pool.wait_ge(S["x_ready"], X_AFTER["pool_out"])
        chain.n = base + 12 * 8
        chain(nc.gpsimd.iota(dist[:], pattern=[[128, 2], [-1, T]], base=0, channel_multiplier=1,
                             allow_small_or_imprecise_dtypes=True))
        chain(nc.gpsimd.affine_select(out=dist[:], in_=dist[:], compare_op=ALU.is_ge, fill=-NEG, base=0,
                                      pattern=[[128, 2], [-1, T]], channel_multiplier=1))
        base += 2
        ada_pairs(4, 2)
        chain.n = base + 12 * 12
        for h in range(8):
            if h >= 2:
                pool.wait_ge(S["logits_ready"], ATT["diff"] + h - 1)
            nc.gpsimd.tensor_scalar(bias1[:, h % 2], dist[:], -(2.0 ** -(h + 1)), None, ALU.mult).then_inc(S["bias_ready"], 1)

        pool.wait_ge(S["idx_summed"], 8)
        nc.gpsimd.affine_select(out=score[:], in_=score[:], compare_op=ALU.is_ge, fill=NEG, base=0,
                                pattern=[[128, 2], [-1, T]], channel_multiplier=1).then_inc(S["masked_ready"], 1)
        pool.wait_ge(S["rel_stored"], 16)
        for h in range(16):
            if h >= 2:
                pool.wait_ge(S["logits_ready"], ATT["moba"] + h - 1)
            for t in range(2):
                pool.dma_start(bias2[:, h % 2, t], bass.AP(rel_rows.tensor, h * 65536 + 255 - 128 * t, [[511, 128], [1, T]]))\
                    .then_inc(b_landed[h % 2], 16)
            if h >= 8:
                pool.wait_ge(b_landed[h % 2], 32 * (h // 2 + 1))
                pool.wait_ge(S["pen_ready"], 2)
                nc.gpsimd.tensor_tensor(bias2[:, h % 2], bias2[:, h % 2], pen[:], ALU.add).then_inc(S["bias_ready"], 1)

        ub, vb = a["peer_u_2"][0], a["peer_v_2"][0]
        pool.wait_ge(S["sk_ready"], 4)
        pool.dma_start(gfin, a["norm_final_2"].partition_broadcast(128)).then_inc(S["gfin_landed"], 16)

        def gathers(buf, idx, table, landed, par):
            for i in range(NG):
                pool.indirect_dma_start(buf[:, par, i, :], None, table,
                                        bass.IndirectOffsetOnAxis(ap=idx[:, par, i:i + 1], axis=0)).then_inc(landed[par], 16)
        pool.wait_ge(S["s_ready"], 2)
        nc.gpsimd.memset(zro, 0.0).then_inc(S["zero_ready"], 1)
        nc.gpsimd.iota(iota16, pattern=[[1, 16]], base=0, channel_multiplier=0,
                       allow_small_or_imprecise_dtypes=True).then_inc(S["iota_ready"], 1)
        pool.wait_ge(S["index_ready"], 2)
        for g in range(2):
            nc.gpsimd.tensor_copy(idxu[:, g, :], eidx[:, g * NG:g * NG + NG]).then_inc(S["iu_ready"], 1)
            pool.wait_ge(S["iu_ready"], g + 1)
            gathers(GU, idxu, ub, u_landed, g)
        for g in range(2):
            nc.gpsimd.tensor_copy(idxv[:, g, :], eidx[:, g * NG:g * NG + NG]).then_inc(S["iv_ready"], 1)
            pool.wait_ge(S["iv_ready"], g + 1)
            gathers(GV, idxv, vb, v_landed, g)
        with pool.Fori(0, GROUPS - 1) as r:
            for g in range(2):
                pool.wait_ge(S["dots_ready"], r * 2 + (g + 1))
                nc.gpsimd.tensor_tensor(small[:, 50 + g:51 + g], small[:, 58:59], small[:, 58:59], ALU.add)
                nc.gpsimd.tensor_copy(idxu[:, g, :], eidx[:, bass.ds(r * 2 * NG + ((2 + g) * NG), NG)]).then_inc(S["iu_ready"], 1)
                pool.wait_ge(S["iu_ready"], r * 2 + (g + 3))
                nc.gpsimd.tensor_tensor(small[:, 52 + g:53 + g], small[:, 58:59], small[:, 58:59], ALU.add)
                gathers(GU, idxu, ub, u_landed, g)
                pool.wait_ge(S["v_used"], r * 2 + (g + 1))
                nc.gpsimd.tensor_tensor(small[:, 54 + g:55 + g], small[:, 58:59], small[:, 58:59], ALU.add)
                nc.gpsimd.tensor_copy(idxv[:, g, :], eidx[:, bass.ds(r * 2 * NG + ((2 + g) * NG), NG)]).then_inc(S["iv_ready"], 1)
                pool.wait_ge(S["iv_ready"], r * 2 + (g + 3))
                nc.gpsimd.tensor_tensor(small[:, 56 + g:57 + g], small[:, 58:59], small[:, 58:59], ALU.add)
                gathers(GV, idxv, vb, v_landed, g)

    @block.tensor
    def _(pe):
        mm = nc.tensor.matmul

        def product(o, wh, wl, xh, xl, first, last, skip=False):
            mm(o, wh, xh, start=first, stop=False, skip_group_check=skip)
            mm(o, wh, xl, start=False, stop=False, skip_group_check=skip)
            return mm(o, wl, xh, start=False, stop=last, skip_group_check=skip)

        def cols_half(U, u, E, e, wait_bank=True):
            pe.wait_ge(S["lo_ready"], U + 1)
            if wait_bank:
                pe.wait_ge(S["bank_free"], E - 1)
            for b in range(2):
                for k in range(KT):
                    c = k * 256 + b * 128
                    last = product(P[4 + e][:, b * 256:b * 256 + 256], WH[:, u, c:c + 128], WL[:, u, c:c + 128],
                                   hTh[:, k], hTl[:, k], k == 0, k == KT - 1)
            last.then_inc(S["half_used"], 1)

        def values_half(U, E):
            u, e = U % 2, E % 2
            pe.wait_ge(S["lo_ready"], U + 1)
            pe.wait_ge(S["bank_free"], E - 1)
            for t in range(2):
                o = P[4 + e][:, t * 256:t * 256 + 256]
                for k in range(KT):
                    w = slice(k * 256, k * 256 + 256)
                    xh, xl = hTh[:, k, t * 128:t * 128 + 128], hTl[:, k, t * 128:t * 128 + 128]
                    mm(o, xh, WH[:, u, w], start=(k == 0), stop=False)
                    mm(o, xh, WL[:, u, w], start=False, stop=False)
                    last = mm(o, xl, WH[:, u, w], start=False, stop=(k == KT - 1))
            last.then_inc(S["half_used"], 1)

        def rows_half(U, kt0, nkt):
            pe.wait_ge(S["lo_ready"], U + 1)
            for kk in range(2):
                for d in range(KT):
                    k = kt0 + kk
                    c = kk * 1024 + d * 128
                    last = product(P[d // 2][:, (d % 2) * 256:(d % 2) * 256 + 256], WH[:, U % 2, c:c + 128],
                                   WL[:, U % 2, c:c + 128], actH[:, k], actL[:, k], k == 0 and d % 2 == 0, k == nkt - 1, True)
            last.then_inc(S["half_used"], 1)

        def ada(name, h):
            i = ADA.get((name, h))
            if i is None:
                return
            pe.wait_ge(S["ada_sum"], 4 * i + 4)
            if i:
                pe.wait_ge(S["mod_ready"], i)
            for j in range(4):
                last = mm(P[7][:, j:j + 1], adaS[:, i % 2, j * 128:j * 128 + 128], ones[:, 0:1], start=True, stop=True)
            last.then_inc(S["ada_done"], 1)

        def norm(name):
            n = NORMS[name][0]
            if n:
                pe.wait_ge(S["std_ready"], n)
            for q in range(4):
                pe.wait_ge(S["sq_ready"], 4 * n + q + 1)
                for k in (2 * q, 2 * q + 1):
                    last = mm(P[6][:, 0:T], ones[:], NT[:, k], start=(k == 0), stop=(k == KT - 1))
            last.then_inc(S["ss_ready"], 1)

        def split_ready(name):
            pe.wait_ge(S["hl_ready"], 4 * (NORMS[name][2] + 1))

        def ffn(i, f):
            norm(f"up{i}{f}")
            split_ready(f"up{i}{f}")
            p = phases[f"up{i}{f}"]
            U, E = p["U"], p["E"]
            with pe.Fori(0, 5) as r:
                for j in range(4):
                    cols_half(r * 4 + (U + j), (U + j) % 2, r * 4 + (E + j), (E + j) % 2)
            for j in range(20, 22):
                cols_half(U + j, (U + j) % 2, E + j, (E + j) % 2)
            p = phases[f"down{i}{f}"]
            for v in range(p["n"]):
                pe.wait_ge(S["act_lo"], FT * (2 * i + f) + 2 * v + 2)
                rows_half(p["U"] + v, 2 * v, FT)
                ada(f"down{i}{f}", v)

        def attention(units):
            def scores(x):
                a, b = x["a"], 4 * (x["a"] % 2)
                if a >= 2:
                    pe.wait_ge(S["logits_ready"], a - 1)
                for c, (q, k) in enumerate(x["qk"]):
                    for t in range(2):
                        last = mm(P[b + c][:, t * T:t * T + T], q[:, t * 128:t * 128 + 128], k, start=True, stop=True)
                last.then_inc(S["score_done"], 1)

            def transposes(x):
                a = x["a"]
                if len(x["qk"]) == 2:
                    pe.wait_ge(S["diffp_ready"], x["head"] + 1)
                pe.wait_ge(S["prob_ready"], a + 1)
                if a >= 2:
                    pe.wait_ge(S["pt_ready"], a - 1)
                for s in range(2):
                    for t in range(2):
                        last = nc.tensor.transpose(P[2 + a % 2][:, s * T + t * 128:s * T + t * 128 + 128],
                                                   LB[:, a % 2, t, s * 128:s * 128 + 128], ident[:])
                last.then_inc(S["tr_done"], 1)

            def weighted(x):
                a = x["a"]
                pe.wait_ge(S["pt_ready"], a + 1)
                if a >= 2:
                    pe.wait_ge(S["o_ready"], a - 1)
                for s in range(2):
                    last = mm(P[6 + a % 2][x["rows"][0]:x["rows"][1], 0:T], x["v"](s), PTS[:, a % 2, s],
                              start=(s == 0), stop=(s == 1))
                last.then_inc(S["o_done"], 1)

            scores(units[0])
            for i in range(len(units) + 1):
                if i + 1 < len(units):
                    scores(units[i + 1])
                if i < len(units):
                    transposes(units[i])
                if i >= 1:
                    weighted(units[i - 1])

        pe.wait_ge(S["iden_ready"], 1)
        pe.wait_ge(S["const_ready"], 1)
        for b0, src, landed, done in ((4, memin, "mem_landed", "mem_tr"), (0, xin, "x_landed", "x_tr")):
            pe.wait_ge(S[landed], 16)
            for q in range(4):
                for kk in range(2):
                    for t in range(2):
                        k = 2 * q + kk
                        last = nc.tensor.transpose(P[b0 + q][:, kk * T + t * 128:kk * T + t * 128 + 128],
                                                   src[:, t, k * 128:k * 128 + 128], ident[:])
                last.then_inc(S[done], 1)
        pe.wait_ge(S["rows_landed"], 9 * 16)
        pe.wait_ge(S["x_ready"], 1)
        nc.tensor.transpose(P[0][:, 0:97], rows1[0:97, :], ident[0:97, 0:97])
        nc.tensor.transpose(P[0][:, 128:176], rows2[0:48, :], ident[0:48, 0:48]).then_inc(S["cols_tr"], 1)

        norm("mem")
        split_ready("mem")
        for l in range(2):
            p = phases[f"kv{l}"]
            for j in range(2):
                U, E = p["U"] + j, p["E"] + j
                cols_half(U, U % 2, E, E % 2, wait_bank=E >= 2)
            for j in range(2, 4):
                values_half(p["U"] + j, p["E"] + j)
        ffn(0, 0)

        norm("pool_in")
        split_ready("pool_in")
        p = phases["pool_in"]
        for j in range(6):
            cols_half(p["U"] + j, (p["U"] + j) % 2, p["E"] + j, (p["E"] + j) % 2)
            ada("pool_in", j)
        pe.wait_ge(S["bank_free"], p["E"] + 6)
        pe.wait_ge(S["mod_ready"], 6)
        attention(heads_of("mem0"))
        p = phases["group"]
        pe.wait_ge(S["logits_ready"], 4)
        pe.wait_ge(S["pool_lo"], 4)
        for g in range(4):
            U, E = p["U"] + g // 2, p["E"] + g
            pe.wait_ge(S["lo_ready"], U + 1)
            pe.wait_ge(S["bank_free"], E - 1)
            for b in range(2):
                for c in range(2):
                    w = ((g % 2) * 2 + c) * 256 + b * 128
                    last = product(P[4 + E % 2][:, b * 256:b * 256 + 256], WH[:, U % 2, w:w + 128], WL[:, U % 2, w:w + 128],
                                   hTh[:, 2 * g + c], hTl[:, 2 * g + c], c == 0, c == 1)
            last.then_inc(S["group_done" if g % 2 == 0 else "half_used"], 1)
        p = phases["pool_out"]
        pe.wait_ge(S["o_ready"], 4)
        pe.wait_ge(S["mix_lo"], 4)
        for v in range(6):
            rows_half(p["U"] + v, 2 * v, 12)
        ffn(0, 1)
        ffn(1, 0)

        norm("diff_in")
        split_ready("diff_in")
        p = phases["diff_in"]
        for j in range(14):
            if 8 <= j < 12:
                values_half(p["U"] + j, p["E"] + j)
            else:
                cols_half(p["U"] + j, (p["U"] + j) % 2, p["E"] + j, (p["E"] + j) % 2)
        pe.wait_ge(S["bank_free"], p["E"] + 14)
        attention(heads_of("diff") + heads_of("mem1"))
        pe.wait_ge(S["osq_ready"], 1)
        for q in range(4):
            mm(P[q][:], ones[:], M[:, 512 * q:512 * q + 512], start=True, stop=True).then_inc(S["oss_ready"], 1)
        p = phases["diff_out"]
        pe.wait_ge(S["o_ready"], ATT["moba"])
        pe.wait_ge(S["on_lo"], 4)
        for v in range(6):
            rows_half(p["U"] + v, 2 * v, 12)
        ffn(1, 1)
        norm("final")

        norm("in2")
        split_ready("in2")
        p = phases["in2"]
        for j in range(12):
            if j in (4, 5, 10, 11):
                values_half(p["U"] + j, p["E"] + j)
            else:
                cols_half(p["U"] + j, (p["U"] + j) % 2, p["E"] + j, (p["E"] + j) % 2)
        p = phases["in2x"]
        cols_half(p["U"], p["U"] % 2, p["E"], p["E"] % 2)
        U, E = p["U"] + 1, p["E"] + 1
        u, o = U % 2, P[4 + E % 2]
        pe.wait_ge(S["lo_ready"], U + 1)
        pe.wait_ge(S["bank_free"], E - 1)
        for k in range(KT):
            c = k * 256
            product(o[:, 0:T], WH[:, u, c:c + 128], WL[:, u, c:c + 128], hTh[:, k], hTl[:, k], k == 0, k == KT - 1)
        for t in range(2):
            for k in range(KT):
                w = slice(k * 256 + 128, k * 256 + 132)
                xh, xl = hTh[:, k, t * 128:t * 128 + 128], hTl[:, k, t * 128:t * 128 + 128]
                ot = o[:, T + 4 * t:T + 4 * t + 4]
                mm(ot, xh, WH[:, u, w], start=(k == 0), stop=False)
                mm(ot, xh, WL[:, u, w], start=False, stop=False)
                last = mm(ot, xl, WH[:, u, w], start=False, stop=(k == KT - 1))
        last.then_inc(S["half_used"], 1)
        pe.wait_ge(S["ik_sq"], 1)
        mm(P[6][:, 0:T], ones[:], relu2[:, 0, 0], start=True, stop=True).then_inc(S["ik_ss"], 1)
        pe.wait_ge(S["bank_free"], p["E"] + 2)
        for t in range(2):
            for h in range(4):
                r = slice(64 * (h % 2), 64 * (h % 2) + 64)
                n = 4 * t + h
                if n >= 2:
                    pe.wait_ge(S["idx_relu"], n - 1)
                mm(P[n % 2][:, 0:T], iQ[r, h // 2, t * 128:t * 128 + 128], iK[r, :], start=True, stop=True)\
                    .then_inc(S["idx_products"], 1)
        pe.wait_ge(S["idx_relu"], 8)
        attention(heads_of("heads"))
        p = phases["out2"]
        pe.wait_ge(S["o_ready"], ATT["moba"] + 16)
        for v in range(4):
            rows_half(p["U"] + v, 2 * v, KT)

        norm("wq")
        pe.wait_ge(S["hn_ready"], 4 * 9)
        for t in range(2):
            for q in range(2):
                for k in range(4):
                    last = nc.tensor.transpose(P[2 * t + q][:, k * 128:k * 128 + 128],
                                               NT[:, 4 * q + k, t * 128:t * 128 + 128], ident[:])
                last.then_inc(S["htok_tr"], 1)
        split_ready("wq")
        p = phases["wq"]
        for j in range(8):
            cols_half(p["U"] + j, (p["U"] + j) % 2, p["E"] + j, (p["E"] + j) % 2)
        pe.wait_ge(S["sk_landed"], 16)
        for q in range(4):
            pe.wait_ge(S["htok_ready"], q + 1)
            for k in range(4):
                last = nc.tensor.transpose(P[q][:, k * 128:k * 128 + 128], skin[:, 4 * q + k], ident[:])
            last.then_inc(S["sk_tr"], 1)
        for t in range(2):
            for q in range(2):
                pe.wait_ge(S["sk_ready"], 2 * t + q + 1)
                for k in range(4):
                    last = nc.tensor.transpose(P[2 * t + q][:, k * 128:k * 128 + 128],
                                               xT[:, 4 * q + k, t * 128:t * 128 + 128], ident[:])
                last.then_inc(S["xtok_tr"], 1)
        pe.wait_ge(S["xtok_ready"], 4)
        pe.wait_ge(S["bank_free"], p["E"] + 8)
        for t in range(2):
            for h in range(16):
                last = mm(P[4 * t + h // 4][:, (h % 4) * 128:(h % 4) * 128 + 128], pQ[:, h, t * 128:t * 128 + 128], skT[:, h],
                          start=True, stop=True)
            last.then_inc(S["sk_scores"], 1)
        pe.wait_ge(S["s_ready"], 2)
        pe.wait_ge(S["g2_diag"], 1)
        for k in range(KT):
            last = mm(P[4 + k // 4][:, (k % 4) * 128:(k % 4) * 128 + 128], ones[:], diag[:, 0, k], start=True, stop=True)
        last.then_inc(S["g2_tr"], 1)
        pe.wait_ge(S["zero_ready"], 1)
        for b in range(4):
            mm(P[b][:], zro, xtok[:, 0, 0:512], start=True, stop=False, skip_group_check=True)

        def experts(t, r, g):
            pe.wait_ge(S["diag_ready"], r * 2 + (t * GROUPS + g + 1))
            pe.wait_ge(v_landed[g], r * (16 * NG) + (t * GROUPS // 2 + 1) * 16 * NG)
            for i in range(NG):
                for q in range(2):
                    last = mm(P[2 * t + q][:], diag[:, g, i], GV[:, g, i, q * 512:q * 512 + 512], start=False, stop=False,
                              skip_group_check=True)
            last.then_inc(S["v_used"], 1)
        for t in range(2):
            with pe.Fori(0, GROUPS // 2) as r:
                for g in range(2):
                    experts(t, r, g)
            for q in range(2):
                last = mm(P[2 * t + q][:], zro, xtok[:, 1, 0:512], start=False, stop=True, skip_group_check=True)
            last.then_inc(S["acc_done"], 1)

    @block.scalar
    def _(act):
        copy = ACT.Copy

        def split(U):
            if U >= len(half_of):
                return
            c, h = half_of[U]
            kind = chunks[c][0]
            if U >= 2:
                act.wait_ge(S["half_used"], U - 1)
            act.wait_ge(raw_landed[c % 2], slot_loads[c])
            if kind == "group":
                nc.scalar.activation(WH[:, U % 2, 0:1024], WR[:, c % 2, h * 1024:h * 1024 + 1024], copy).then_inc(S["hi_ready"], 1)
            else:
                nc.scalar.activation(split_view(WH, U % 2, kind), raw(c % 2, kind, h), copy).then_inc(S["hi_ready"], 1)

        def split_loop(U, r, par):
            c, h = half_of[U]
            act.wait_ge(S["half_used"], r * 4 + (U - 1))
            act.wait_ge(raw_landed[c % 2], r * 32 + slot_loads[c])
            nc.scalar.activation(split_view(WH, U % 2, "pair"), raw(c % 2, "pair", h), copy).then_inc(S["hi_ready"], 1)

        def norm(name, src, ready, base, shift=False):
            n, _, m = NORMS[name]
            if n == 1:
                act.wait_ge(S["hl_ready"], 4)
            for q in range(4):
                act.wait_ge(S[ready], base + q + 1)
                nc.scalar.activation(NT[:, 2 * q:2 * q + 2], src[:, 2 * q:2 * q + 2], ACT.Square).then_inc(S["sq_ready"], 1)
            act.wait_ge(S["ss_ready"], n + 1)
            nc.scalar.activation(rstd[:], P[6][:, 0:T], ACT.Sqrt, bias=eps[:, 0:1], scale=1.0 / D).then_inc(S["std_ready"], 1)
            if m is None:
                return
            nxt = {"mem": "kv0"}.get(name, name)
            if phases[nxt]["U"]:
                act.wait_ge(S["half_used"], phases[nxt]["U"])
            for q in range(4):
                act.wait_ge(S["hn_ready"], 4 * m + q + 1)
                nc.scalar.activation(hTh[:, 2 * q:2 * q + 2], NT[:, 2 * q:2 * q + 2], copy).then_inc(S["hh_ready"], 1)

        def gate_silu(Ue, E, j):
            act.wait_ge(S["half_used"], Ue + 1)
            nc.scalar.activation(SIL[:, j % 2], P[4 + E % 2][:, 0:T], ACT.Silu).then_inc(S["sil_ready"], 1)

        def hi_act(al, j, tile):
            act.wait_ge(S["bank_free"], al)
            nc.scalar.activation(tile, PRD[:, j % 2], copy).then_inc(S["act_hi"], 1)

        def ffn(i, f, base):
            norm(f"up{i}{f}", xT, "x_ready", base)
            p = phases[f"up{i}{f}"]
            U, E = p["U"], p["E"]

            def step(j):
                split(U + j + 2)
                gate_silu(U + j, E + j, j)
                if j:
                    hi_act(E + j, j - 1, actH[:, j - 1])
            step(0)
            with act.Fori(0, 4) as r:
                for j in range(1, 5):
                    split_loop(U + j + 2, r, j)
                    gate_silu(r * 4 + (U + j), E + j, j)
                    hi_act(r * 4 + (E + j), j - 1, actH[:, bass.ds(r * 4 + (j - 1), 1), :].rearrange("p a t -> p (a t)"))
            for j in range(17, 22):
                step(j)
            hi_act(E + 22, 21, actH[:, 21])
            p = phases[f"down{i}{f}"]
            for v in range(p["n"]):
                split(p["U"] + v + 2)

        def attention(units):
            def exps(x):
                a, n = x["a"], 2 * len(x["qk"])
                act.wait_ge(S["neg_max"], a + 1)
                for j in range(n):
                    last = nc.scalar.activation(LB[:, a % 2, j], LB[:, a % 2, j], ACT.Exp, bias=nmax(a, j), scale=1.0,
                                                accum_out=rsum(a, j))
                last.then_inc(S["exp_done"], 1)

            def normalise(x):
                a = x["a"]
                act.wait_ge(S["rsum_ready"], a + 1)
                for t in range(2):
                    last = nc.scalar.activation(LB[:, a % 2, t], LB[:, a % 2, t], copy, scale=rinv(a, t))
                last.then_inc(S["prob_ready"], 1)

            def pt(x):
                a = x["a"]
                act.wait_ge(S["tr_done"], a + 1)
                if a >= 2:
                    act.wait_ge(S["o_done"], a - 1)
                nc.scalar.activation(PTS[:, a % 2].rearrange("p a b -> p (a b)"), P[2 + a % 2][:], copy).then_inc(S["pt_ready"], 1)

            def result(x):
                if not x["split"]:
                    return
                a, (r0, r1) = x["a"], x["rows"]
                act.wait_ge(S["o_done"], a + 1)
                nc.scalar.activation(actH[r0:r1, x["tile"]], P[6 + a % 2][r0:r1, 0:T], copy).then_inc(S["o_hi"], 1)

            exps(units[0])
            for i in range(len(units) + 1):
                if i < len(units):
                    normalise(units[i])
                if i + 1 < len(units):
                    exps(units[i + 1])
                if i < len(units):
                    pt(units[i])
                if i >= 1:
                    result(units[i - 1])

        act.dma_start(lamw, a["diff_lambda"][0].partition_broadcast(128)).then_inc(S["lam_landed"], 16)
        for q in range(4):
            act.wait_ge(S["mem_tr"], q + 1)
            nc.scalar.activation(memT[:, 2 * q:2 * q + 2].rearrange("p a b -> p (a b)"), P[4 + q][:], copy).then_inc(S["mem_in"], 1)
        split(0)
        split(1)
        act.wait_ge(S["const_ready"], 1)
        act.wait_ge(S["cols_ready"], 1)
        nc.scalar.activation(silc[:], cols[:, G_C:G_C + KT], ACT.Silu).then_inc(S["silc_ready"], 1)
        norm("mem", memT, "mem_in", 0)
        for U in range(8):
            split(U + 2)
        ffn(0, 0, 0)
        norm("pool_in", xT, "x_ready", X_AFTER["down00"] - 4)
        p = phases["pool_in"]
        for j in range(6):
            split(p["U"] + j + 2)
        for g in range(4):
            act.wait_ge(S["pooled_ready"], g + 1)
            nc.scalar.activation(hTh[:, 2 * g:2 * g + 2], ptmp[:, 2 * g:2 * g + 2], copy).then_inc(S["pool_hi"], 1)
        attention(heads_of("mem0"))
        p = phases["group"]
        for j in range(2):
            for g in (2 * j, 2 * j + 1):
                if g % 2:
                    split(p["U"] + j + 2)
                act.wait_ge(S["bank_free"], p["E"] + g + 1)
                nc.scalar.activation(actH[:, 2 * g:2 * g + 2], ptmp[:, 2 * g:2 * g + 2], copy).then_inc(S["mix_hi"], 1)
        p = phases["pool_out"]
        for v in range(p["n"]):
            split(p["U"] + v + 2)
        ffn(0, 1, X_AFTER["pool_out"] - 4)
        ffn(1, 0, X_AFTER["down01"] - 4)

        act.wait_ge(S["lam_ready"], 1)
        nc.scalar.activation(small[:, 2:4], small[:, 0:2], ACT.Exp).then_inc(S["lam_exp"], 1)
        norm("diff_in", xT, "x_ready", X_AFTER["down10"] - 4)
        p = phases["diff_in"]
        for j in range(14):
            split(p["U"] + j + 2)
        attention(heads_of("diff") + heads_of("mem1"))
        act.wait_ge(S["tr_done"], ATT["mem1"] + 4)
        nc.scalar.activation(M[:, 0:2048], M[:, MX:MX + 2048], ACT.Square).then_inc(S["osq_ready"], 1)
        for q in range(4):
            act.wait_ge(S["oss_ready"], q + 1)
            nc.scalar.activation(M[:, MX + 2048 + 512 * q:MX + 2560 + 512 * q], P[q][:], ACT.Sqrt, bias=eps[:, 1:2],
                                 scale=1.0 / 128).then_inc(S["ostd_ready"], 1)
        for q in range(4):
            act.wait_ge(S["on_ready"], q + 1)
            nc.scalar.activation(actH[:, 2 * q:2 * q + 2], dQ[:, 2 * q:2 * q + 2], copy).then_inc(S["on_hi"], 1)
        p = phases["diff_out"]
        for v in range(p["n"]):
            split(p["U"] + v + 2)
        ffn(1, 1, X_AFTER["diff_out"] - 4)
        norm("final", xT, "x_ready", X_AFTER["down11"] - 4)

        norm("in2", xT, "x_ready", X_AFTER["final"] - 4)
        for name in ("in2", "in2x"):
            for j in range(phases[name]["n"]):
                split(phases[name]["U"] + j + 2)
        act.wait_ge(S["half_used"], phases["in2x"]["U"] + 2)
        nc.scalar.activation(relu2[:, 0, 0], P[4 + (phases["in2x"]["E"] + 1) % 2][:, 0:T], ACT.Square).then_inc(S["ik_sq"], 1)
        act.wait_ge(S["ik_ss"], 1)
        nc.scalar.activation(rstd[:], P[6][:, 0:T], ACT.Sqrt, bias=eps[:, 0:1], scale=1.0 / 128).then_inc(S["ik_std"], 1)
        for n in range(8):
            act.wait_ge(S["idx_products"], n + 1)
            if n >= 2:
                act.wait_ge(S["idx_summed"], n - 1)
            nc.scalar.activation(relu2[:, n % 2, 0], P[n % 2][:, 0:T], ACT.Relu).then_inc(S["idx_relu"], 1)
        attention(heads_of("heads"))
        p = phases["out2"]
        for v in range(p["n"]):
            split(p["U"] + v + 2)

        act.wait_ge(S["x_ready"], X_AFTER["out2"])
        act.dma_start(skin, a["peer_subkeys_2"][0].rearrange("h q n d -> n (h q) d")).then_inc(S["sk_landed"], 16)
        norm("wq", xT, "x_ready", X_AFTER["out2"] - 4)
        for t in range(2):
            for q in range(2):
                act.wait_ge(S["htok_tr"], 2 * t + q + 1)
                nc.scalar.activation(htok[:, t, q * 512:q * 512 + 512], P[2 * t + q][:], copy).then_inc(S["htok_ready"], 1)
        p = phases["wq"]
        for j in range(p["n"]):
            split(p["U"] + j + 2)
        for q in range(4):
            act.wait_ge(S["sk_tr"], q + 1)
            nc.scalar.activation(skT[:, 4 * q:4 * q + 4].rearrange("p a b -> p (a b)"), P[q][:], copy).then_inc(S["sk_ready"], 1)
        for t in range(2):
            for q in range(2):
                act.wait_ge(S["xtok_tr"], 2 * t + q + 1)
                nc.scalar.activation(xtok[:, t, q * 512:q * 512 + 512], P[2 * t + q][:], copy).then_inc(S["xtok_ready"], 1)
        act.wait_ge(S["sk_scores"], 1)
        for q in range(4):
            last = nc.scalar.activation(gvf[:, 512 * q:512 * q + 512], P[q][:], copy)
        last.then_inc(S["s_ready"], 1)
        act.wait_ge(S["sk_scores"], 2)
        for q in range(4):
            last = nc.scalar.activation(gvf[:, 2048 + 512 * q:2560 + 512 * q], P[4 + q][:], copy)
        last.then_inc(S["s_ready"], 1)
        for k in range(KT):
            last = nc.scalar.activation(diag[:, 0, k], ident[:], copy, scale=modc[:, 40 + k:41 + k])
        last.then_inc(S["g2_diag"], 1)
        act.wait_ge(S["g2_tr"], 1)
        for q in range(2):
            last = nc.scalar.activation(g2bc[:, q * 512:q * 512 + 512], P[4 + q][:], copy)
        last.then_inc(S["g2_ready"], 1)
        for t in range(2):
            act.wait_ge(S["gdiff_ready"], t + 1)
            nc.scalar.activation(gate[:, t], gate[:, t], ACT.Exp).then_inc(S["gexp_ready"], 1)

        def experts(t, r, g, first=False):
            n = t * GROUPS + g
            act.wait_ge(S["dots_ready"], r * 2 + (n + 1))
            if not first:
                act.wait_ge(S["coef_ready"], r * 2 + (n - 1))
            nc.scalar.activation(gel8[:, g], dots[:, g], ACT.Gelu).then_inc(S["gelu_ready"], 1)
            act.wait_ge(S["coef_ready"], r * 2 + (n + 1))
            if not first:
                act.wait_ge(S["v_used"], r * 2 + (n - 1))
            for i in range(NG):
                last = nc.scalar.activation(diag[:, g, i], ident[:], copy, scale=coef8[:, g, i:i + 1])
            last.then_inc(S["diag_ready"], 1)
        for g in range(2):
            experts(0, 0, g, True)
        with act.Fori(1, GROUPS // 2) as r:
            for g in range(2):
                experts(0, r, g)
        with act.Fori(0, GROUPS // 2) as r:
            for g in range(2):
                experts(1, r, g)
        for t in range(2):
            act.wait_ge(S["xf_ready"], t + 1)
            nc.scalar.activation(tmpf, xtok[:, t], ACT.Square, accum_out=small[:, 44 + t:45 + t]).then_inc(S["fss_ready"], 1)
            act.wait_ge(S["fss_ready"], t + 1)
            nc.scalar.activation(small[:, 46 + t:47 + t], small[:, 44 + t:45 + t], ACT.Sqrt, bias=eps[:, 0:1], scale=1.0 / D)\
                .then_inc(S["fstd_ready"], 1)

    @block.vector
    def _(dve):
        chain = Chain(dve, S["dve_chain"])
        tt, ts, stt = nc.vector.tensor_tensor, nc.vector.tensor_scalar, nc.vector.scalar_tensor_tensor

        def split(U):
            if U >= len(half_of):
                return
            c, h = half_of[U]
            kind = chunks[c][0]
            dve.wait_ge(S["hi_ready"], U + 1)
            if kind == "group":
                tt(WL[:, U % 2, 0:1024], WR[:, c % 2, h * 1024:h * 1024 + 1024], WH[:, U % 2, 0:1024].bitcast(F32), ALU.subtract)\
                    .then_inc(S["lo_ready"], 1)
            else:
                tt(split_view(WL, U % 2, kind), raw(c % 2, kind, h), split_view(WH, U % 2, kind).bitcast(F32), ALU.subtract)\
                    .then_inc(S["lo_ready"], 1)

        def split_loop(U, r):
            c, h = half_of[U]
            dve.wait_ge(S["hi_ready"], r * 4 + (U + 1))
            tt(split_view(WL, U % 2, "pair"), raw(c % 2, "pair", h), split_view(WH, U % 2, "pair").bitcast(F32), ALU.subtract)\
                .then_inc(S["lo_ready"], 1)

        def norm(name, src, gain, shift=None, dst=None):
            n, _, m = NORMS[name]
            dst = NT if dst is None else dst
            dve.wait_ge(S["std_ready"], n + 1)
            chain(nc.vector.reciprocal(rstd[:], rstd[:]))
            for k in range(KT):
                last = stt(dst[:, k], src[:, k], gain(k), rstd[:], ALU.mult, ALU.mult)
                if shift is None and k % 2:
                    last.then_inc(S["x_ready" if m is None else "hn_ready"], 1)
            if shift is not None:
                chain(last)
                for k in range(KT):
                    last = ts(dst[:, k], dst[:, k], shift(k), None, ALU.add)
                    if k % 2:
                        last.then_inc(S["hn_ready"], 1)
            if m is None:
                return
            for q in range(4):
                dve.wait_ge(S["hh_ready"], 4 * m + q + 1)
                tt(hTl[:, 2 * q:2 * q + 2], NT[:, 2 * q:2 * q + 2], hTh[:, 2 * q:2 * q + 2].bitcast(F32), ALU.subtract)\
                    .then_inc(S["hl_ready"], 1)

        def col(at):
            return lambda k: cols[:, at + k:at + k + 1]

        def post_copy(U, E, dst):
            dve.wait_ge(S["half_used"], U + 1)
            nc.vector.tensor_copy(dst, P[4 + E % 2][:].rearrange("p (a b) -> p a b", a=2)).then_inc(S["bank_free"], 1)

        def ada(name, h):
            i = ADA.get((name, h))
            if i is not None:
                dve.wait_ge(S["ada_done"], i + 1)
                tt(modc[:, 4 * i:4 * i + 4], P[7][:, 0:4], badac[:, 4 * i:4 * i + 4], ALU.add).then_inc(S["mod_ready"], 1)

        def add_update(U, gain=None):
            dve.wait_ge(S["half_used"], U)
            for q in range(4):
                if callable(gain):
                    for k in range(2):
                        last = stt(xT[:, 2 * q + k], P[q][:, k * T:k * T + T], gain(2 * q + k), xT[:, 2 * q + k], ALU.mult, ALU.add)
                else:
                    x = xT[:, 2 * q:2 * q + 2].rearrange("p a b -> p (a b)")
                    last = stt(x, P[q][:], gain, x, ALU.mult, ALU.add)
                last.then_inc(S["x_ready"], 1)

        def ffn(i, f, g):
            norm(f"up{i}{f}", xT, col(g))
            p = phases[f"up{i}{f}"]
            U, E = p["U"], p["E"]

            def product(sil, e, j):
                if j:
                    dve.wait_ge(S["act_lo"], sil - 2)
                dve.wait_ge(S["sil_ready"], sil)
                tt(PRD[:, j % 2], SIL[:, j % 2], P[4 + e % 2][:, T:2 * T], ALU.mult).then_inc(S["bank_free"], 1)

            def lo_act(hi, j, lo, hitile):
                dve.wait_ge(S["act_hi"], hi)
                tt(lo, PRD[:, j % 2], hitile.bitcast(F32), ALU.subtract).then_inc(S["act_lo"], 1)
            s0 = FT * (2 * i + f)

            def step(j):
                split(U + j + 2)
                product(s0 + j + 1, E + j, j)
                if j:
                    lo_act(s0 + j, j - 1, actL[:, j - 1], actH[:, j - 1])
            step(0)
            with dve.Fori(0, 4) as r:
                for j in range(1, 5):
                    split_loop(U + j + 2, r)
                    product(r * 4 + (s0 + j + 1), E + j, j)
                    one = [b[:, bass.ds(r * 4 + (j - 1), 1), :].rearrange("p a t -> p (a t)") for b in (actL, actH)]
                    lo_act(r * 4 + (s0 + j), j - 1, one[0], one[1])
            for j in range(17, 22):
                step(j)
            lo_act(s0 + 22, 21, actL[:, 21], actH[:, 21])
            p = phases[f"down{i}{f}"]
            for v in range(p["n"]):
                split(p["U"] + v + 2)
                ada(f"down{i}{f}", v)
            add_update(p["U"] + p["n"], 0.5)

        def mix_lo(g):
            dve.wait_ge(S["mix_hi"], g + 1)
            tt(actL[:, 2 * g:2 * g + 2], ptmp[:, 2 * g:2 * g + 2], actH[:, 2 * g:2 * g + 2].bitcast(F32), ALU.subtract)\
                .then_inc(S["mix_lo"], 1)

        def choose(t):
            sk = sks[:, t]
            dve.wait_ge(S["s_ready"], t + 1)
            for h in range(16):
                last = nc.vector.max(v16[:, t, h, 0:8], sk[:, h])
            chain(last)
            for h in range(16):
                nc.vector.max_index(i16[:, t, h, 0:8], v16[:, t, h, 0:8], sk[:, h])
            for h in range(16):
                last = nc.vector.match_replace(skw[:, h], v16[:, t, h, 0:8], sk[:, h], TAKEN)
            chain(last)
            for h in range(16):
                last = nc.vector.max(v16[:, t, h, 8:16], skw[:, h])
            chain(last)
            for h in range(16):
                last = nc.vector.max_index(i16[:, t, h, 8:16], v16[:, t, h, 8:16], skw[:, h])
            chain(last)
            nc.vector.tensor_copy(i16f[:, t], i16[:, t])
            v = v16[:, t].rearrange("p (h q) i -> p h q i", q=2)
            wide = [128, 8, 16, 16]
            chain(tt(cand, v[:, :, 0].unsqueeze(3).broadcast_to(wide), v[:, :, 1].unsqueeze(2).broadcast_to(wide), ALU.add))
            flat = cand.rearrange("p h i j -> p h (i j)")
            for h in range(8):
                last = nc.vector.max(gs[:, t, h, 0:8], flat[:, h])
            chain(last)
            for h in range(8):
                nc.vector.max_index(pos[:, t, h, 0:8], gs[:, t, h, 0:8], flat[:, h])
            for h in range(8):
                last = nc.vector.match_replace(candw[:, h], gs[:, t, h, 0:8], flat[:, h], TAKEN)
            chain(last)
            for h in range(8):
                last = nc.vector.max(gs[:, t, h, 8:16], candw[:, h])
            chain(last)
            tt(gate[:, t], gs[:, t], gs[:, t, :, 0:1].broadcast_to([128, 8, 16]), ALU.subtract).then_inc(S["gdiff_ready"], 1)
            for h in range(8):
                last = nc.vector.max_index(pos[:, t, h, 8:16], gs[:, t, h, 8:16], candw[:, h])
            chain(last)
            p = pos[:, t].rearrange("p h k -> p (h k)")
            pd = posd.bitcast(U32)
            ts(pd[:, 0], p, 4, None, ALU.logical_shift_right)
            chain(ts(pd[:, 1], p, 15, None, ALU.bitwise_and))
            chain(nc.vector.tensor_copy(posf, pd))
            ix = i16f[:, t].rearrange("p (h q) i -> p h q i", q=2)
            if t == 0:
                dve.wait_ge(S["iota_ready"], 1)
            for q in range(2):
                pf = posf[:, q].rearrange("p (h k) -> p h k", h=8)
                chain(tt(hot, pf.unsqueeze(3).broadcast_to(wide), iota16.unsqueeze(1).unsqueeze(1).broadcast_to(wide), ALU.is_equal))
                chain(tt(hot, hot, ix[:, :, q].unsqueeze(2).broadcast_to(wide), ALU.mult))
                chain(nc.vector.tensor_reduce(psel[:, q].rearrange("p (h k) -> p h k", h=8), hot, AX.X, ALU.add))
            stt(eidx[:, t * 128:t * 128 + 128], psel[:, 0], float(128), psel[:, 1], ALU.mult, ALU.add).then_inc(S["index_ready"], 1)
            dve.wait_ge(S["gexp_ready"], t + 1)
            gsum = small[:, 8:16]
            chain(nc.vector.tensor_reduce(gsum, gate[:, t], AX.X, ALU.add))
            chain(nc.vector.reciprocal(gsum, gsum))
            chain(tt(gate[:, t], gate[:, t], gsum.unsqueeze(2).broadcast_to([128, 8, 16]), ALU.mult))

        def attention(units):
            def logits(x):
                a, b, n = x["a"], 4 * (x["a"] % 2), len(x["qk"])
                dve.wait_ge(S["score_done"], a + 1)
                if a >= 2:
                    dve.wait_ge(S["tr_done"], a - 1)
                if x["bias"] is not None:
                    dve.wait_ge(*x["bias_sem"])
                for c in range(n):
                    o = LB[:, a % 2, 2 * c:2 * c + 2]
                    i = P[b + c][:].rearrange("p (a b) -> p a b", a=2)
                    if x["bias"] is None:
                        last = ts(o, i, x["scale"], None, ALU.mult)
                    else:
                        last = stt(o, i, x["scale"], x["bias"], ALU.mult, ALU.add)
                last.then_inc(S["logits_ready"], 1)
                dve.wait_ge(S["logits_ready"], a + 1)
                nc.vector.tensor_reduce(st[:, rb(a):rb(a) + 2 * n], LB[:, a % 2, 0:2 * n], AX.X, ALU.max, negate=True)\
                    .then_inc(S["neg_max"], 1)

            def rsums(x):
                a, n = x["a"], 2 * len(x["qk"])
                dve.wait_ge(S["exp_done"], a + 1)
                if n == 4:
                    chain(nc.vector.reciprocal(st[:, rb(a) + 8:rb(a) + 8 + n], st[:, rb(a) + 4:rb(a) + 4 + n]))
                    ts(st[:, rb(a) + 10:rb(a) + 12], st[:, rb(a) + 10:rb(a) + 12], small[:, 5:6], None, ALU.mult)\
                        .then_inc(S["rsum_ready"], 1)
                else:
                    nc.vector.reciprocal(st[:, rb(a) + 8:rb(a) + 8 + n], st[:, rb(a) + 4:rb(a) + 4 + n]).then_inc(S["rsum_ready"], 1)

            def diffs(x):
                a = x["a"]
                dve.wait_ge(S["prob_ready"], a + 1)
                for t in range(2):
                    last = stt(LB[:, a % 2, t], LB[:, a % 2, 2 + t], rinv(a, 2 + t), LB[:, a % 2, t], ALU.mult, ALU.add)
                last.then_inc(S["diffp_ready"], 1)

            def result(x):
                a, (r0, r1) = x["a"], x["rows"]
                if not x["split"]:
                    dve.wait_ge(S["o_done"], a + 1)
                    nc.vector.tensor_copy(dQ[:, x["head"]], P[6 + a % 2][:, 0:T]).then_inc(S["o_ready"], 1)
                    return
                ohi = a + 1 - (8 if a >= ATT["mem1"] else 0)
                dve.wait_ge(S["o_hi"], ohi)
                tt(actL[r0:r1, x["tile"]], P[6 + a % 2][r0:r1, 0:T], actH[r0:r1, x["tile"]].bitcast(F32), ALU.subtract)\
                    .then_inc(S["o_ready"], 1)

            logits(units[0])
            for i in range(len(units) + 1):
                if i + 1 < len(units):
                    logits(units[i + 1])
                if i < len(units):
                    rsums(units[i])
                    if len(units[i]["qk"]) == 2:
                        diffs(units[i])
                if i >= 1:
                    result(units[i - 1])

        for q in range(4):
            dve.wait_ge(S["x_tr"], q + 1)
            nc.vector.tensor_copy(xT[:, 2 * q:2 * q + 2].rearrange("p a b -> p (a b)"), P[q][:]).then_inc(S["x_ready"], 1)
        dve.wait_ge(S["cols_tr"], 1)
        nc.vector.tensor_copy(badac[:], P[0][:, 128:176])
        nc.vector.tensor_copy(cols[:, 0:97], P[0][:, 0:97]).then_inc(S["cols_ready"], 1)
        dve.wait_ge(S["cols_ready"], 1)
        split(0)
        split(1)
        norm("mem", memT, col(G_MEM))
        for l in range(2):
            p = phases[f"kv{l}"]
            for j in range(4):
                split(p["U"] + j + 2)
                dst = memK[:, l, 2 * j:2 * j + 2] if j < 2 else memV[:, l, :, (j - 2) * 256:(j - 2) * 256 + 256]
                post_copy(p["U"] + j, p["E"] + j, dst)
        ffn(0, 0, G_NORM)

        norm("pool_in", xT, col(G_NORM + 8))
        p = phases["pool_in"]
        dve.wait_ge(S["pad_ready"], 1)
        for j in range(6):
            split(p["U"] + j + 2)
            dst = uT[:, 2 * j:2 * j + 2, 16:] if j < 4 else xq0[:, 2 * (j - 4):2 * (j - 4) + 2]
            post_copy(p["U"] + j, p["E"] + j, dst)
            ada("pool_in", j)
        for g in range(4):
            last = nc.vector.tensor_scalar_min(inv[:, g], inv[:, g], float(2 << g))
        chain(last)
        dve.wait_ge(S["bank_free"], p["E"] + 6)
        chain(nc.vector.reciprocal(inv[:], inv[:]))
        for g in range(4):
            src, w = uT[:, 2 * g:2 * g + 2], 1
            for s in range(g + 1):
                dst = wa if s % 2 == 0 else wb
                chain(tt(dst[:, :, 16:], src[:, :, 16:], src[:, :, 16 - w:PADW - w], ALU.add))
                src, w = dst, 2 * w
            iv = inv[:, g].unsqueeze(1).broadcast_to([128, 2, T])
            pg = ptmp[:, 2 * g:2 * g + 2]
            chain(tt(pg, src[:, :, 16:], iv, ALU.mult))
            tt(pg, pg, uT[:, 2 * g:2 * g + 2, 16:], ALU.subtract).then_inc(S["pooled_ready"], 1)
        for g in range(4):
            dve.wait_ge(S["pool_hi"], g + 1)
            tt(hTl[:, 2 * g:2 * g + 2], ptmp[:, 2 * g:2 * g + 2], hTh[:, 2 * g:2 * g + 2].bitcast(F32), ALU.subtract)\
                .then_inc(S["pool_lo"], 1)
        attention(heads_of("mem0"))
        p = phases["group"]
        for g in range(4):
            if g % 2:
                split(p["U"] + g // 2 + 2)
                dve.wait_ge(S["half_used"], p["U"] + g // 2 + 1)
            else:
                dve.wait_ge(S["group_done"], g // 2 + 1)
            for b in range(2):
                k = 2 * g + b
                last = ts(ptmp[:, k], P[4 + (p["E"] + g) % 2][:, b * T:b * T + T], cols[:, G_POOL + k:G_POOL + k + 1], None, ALU.mult)
            last.then_inc(S["bank_free"], 1)
            if g:
                mix_lo(g - 1)
        mix_lo(3)
        p = phases["pool_out"]
        for v in range(p["n"]):
            split(p["U"] + v + 2)
        add_update(p["U"] + p["n"], 1.0)
        ffn(0, 1, G_NORM + 16)
        dve.wait_ge(S["lam_landed"], 16)
        lw = lamw.rearrange("p (a b) n -> p a b n", a=2)
        chain(tt(lamp, lw[:, :, 0], lw[:, :, 1], ALU.mult))
        nc.vector.tensor_reduce(small[:, 0:2], lamp, AX.X, ALU.add).then_inc(S["lam_ready"], 1)
        ffn(1, 0, G_NORM + 24)
        dve.wait_ge(S["lam_exp"], 1)
        chain(tt(small[:, 4:5], small[:, 3:4], small[:, 2:3], ALU.subtract))
        chain(ts(small[:, 5:6], small[:, 4:5], -LAM_INIT, None, ALU.add))
        chain(ts(cols[:, 97:98], cols[:, G_DIFF:G_DIFF + 1], 1.0 - LAM_INIT, None, ALU.mult))

        norm("diff_in", xT, col(G_NORM + 32))
        p = phases["diff_in"]
        for j in range(14):
            split(p["U"] + j + 2)
            if j < 8:
                dst = (dQ if j < 4 else dK)[:, 2 * (j % 4):2 * (j % 4) + 2]
            elif j < 12:
                dst = dV[:, :, (j - 8) * 256:(j - 8) * 256 + 256]
            else:
                dst = xq1[:, 2 * (j - 12):2 * (j - 12) + 2]
            post_copy(p["U"] + j, p["E"] + j, dst)
        attention(heads_of("diff") + heads_of("mem1"))
        for q in range(4):
            r = M[:, MX + 2048 + 512 * q:MX + 2560 + 512 * q]
            dve.wait_ge(S["ostd_ready"], q + 1)
            chain(nc.vector.reciprocal(r, r))
            o = M[:, MX + 512 * q:MX + 512 * q + 512]
            stt(o, o, cols[:, 97:98], r, ALU.mult, ALU.mult).then_inc(S["on_ready"], 1)
        for q in range(4):
            dve.wait_ge(S["on_hi"], q + 1)
            tt(actL[:, 2 * q:2 * q + 2], dQ[:, 2 * q:2 * q + 2], actH[:, 2 * q:2 * q + 2].bitcast(F32), ALU.subtract)\
                .then_inc(S["on_lo"], 1)
        p = phases["diff_out"]
        for v in range(p["n"]):
            split(p["U"] + v + 2)
        add_update(p["U"] + p["n"], 1.0)
        ffn(1, 1, G_NORM + 40)
        norm("final", xT, col(G_FIN), dst=xT)

        dve.wait_ge(S["mod_ready"], 12)
        for j, (g, s) in enumerate(((G_ATT, 8), (G_FFN, 32))):
            last = stt(gmod[:, 8 * j:8 * j + 8], modc[:, s:s + 8], 1.0, cols[:, g:g + 8], ALU.add, ALU.mult)
        chain(last)
        norm("in2", xT, lambda k: gmod[:, k:k + 1], lambda k: modc[:, k:k + 1])
        p = phases["in2"]
        for j in range(12):
            split(p["U"] + j + 2)
            jj, half = j % 6, j // 6
            if jj < 2:
                dst = hQ[:, 4 * half + 2 * jj:4 * half + 2 * jj + 2]
            elif jj < 4:
                dst = hK[:, 4 * half + 2 * (jj - 2):4 * half + 2 * (jj - 2) + 2]
            else:
                dst = hV[:, :, half * 512 + (jj - 4) * 256:half * 512 + (jj - 4) * 256 + 256]
            post_copy(p["U"] + j, p["E"] + j, dst)
        p = phases["in2x"]
        split(p["U"] + 2)
        post_copy(p["U"], p["E"], iQ)
        split(p["U"] + 3)
        dve.wait_ge(S["ik_std"], 1)
        b = P[4 + (p["E"] + 1) % 2]
        chain(ts(iw, b[:, T:T + 8].rearrange("p (a b) -> p a b", a=2), 0.5, None, ALU.mult))
        chain(nc.vector.reciprocal(rstd[:], rstd[:]))
        tt(iK, b[:, 0:T], rstd[:], ALU.mult).then_inc(S["bank_free"], 1)
        for t in range(2):
            for h in range(4):
                n = 4 * t + h
                dve.wait_ge(S["idx_relu"], n + 1)
                w, r = iw[:, t, h:h + 1], relu2[:, n % 2, 0]
                if h:
                    dve.wait_ge(S["idx_summed"], n)
                    last = stt(score[:, t], r, w, score[:, t], ALU.mult, ALU.add)
                else:
                    last = ts(score[:, t], r, w, None, ALU.mult)
                last.then_inc(S["idx_summed"], 1)
        dve.wait_ge(S["masked_ready"], 1)
        for i in range(TOPK // 8):
            for t in range(2):
                last = nc.vector.max(small[:, 16 + 8 * t:24 + 8 * t], score[:, t] if i == 0 else work[:, t])
            chain(last)
            for t in range(2):
                last = nc.vector.match_replace(work[:, t], small[:, 16 + 8 * t:24 + 8 * t], score[:, t] if i == 0 else work[:, t],
                                               TAKEN)
            chain(last)
        for t in range(2):
            ts(pen[:, t], work[:, t], TAKEN / 2, NEG, ALU.is_gt, ALU.mult).then_inc(S["pen_ready"], 1)
        dve.wait_ge(S["pen_ready"], 2)
        attention(heads_of("heads"))
        p = phases["out2"]
        for v in range(p["n"]):
            split(p["U"] + v + 2)
        add_update(p["U"] + p["n"], lambda k: modc[:, 16 + k:17 + k])

        norm("wq", xT, lambda k: gmod[:, 8 + k:9 + k], lambda k: modc[:, 24 + k:25 + k])
        p = phases["wq"]
        for j in range(p["n"]):
            split(p["U"] + j + 2)
            post_copy(p["U"] + j, p["E"] + j, pQ[:, 2 * j:2 * j + 2])
        for t in range(2):
            choose(t)

        def experts(t, r, g, first=False):
            n = t * GROUPS + g
            dve.wait_ge(u_landed[g], r * (16 * NG) + (t * GROUPS // 2 + 1) * 16 * NG)
            if not first:
                dve.wait_ge(S["gelu_ready"], r * 2 + (n - 1))
            for i in range(NG):
                last = nc.vector.tensor_tensor_reduce(out=GU[:, g, i], in0=GU[:, g, i], in1=htok[:, t], scale=1.0, scalar=0.0,
                                                      op0=ALU.mult, op1=ALU.add, accum_out=dots[:, g, i:i + 1])
            last.then_inc(S["dots_ready"], 1)
            dve.wait_ge(S["gelu_ready"], r * 2 + (n + 1))
            if not first:
                dve.wait_ge(S["diag_ready"], r * 2 + (n - 1))
            if isinstance(r, int):
                gt = gatec[:, (2 * r + n) * NG:(2 * r + n + 1) * NG]
            else:
                gt = gatec[:, bass.ds(r * (2 * NG) + n * NG, NG)]
            tt(coef8[:, g], gel8[:, g], gt, ALU.mult).then_inc(S["coef_ready"], 1)
        for g in range(2):
            experts(0, 0, g, True)
        with dve.Fori(1, GROUPS // 2) as r:
            for g in range(2):
                experts(0, r, g)
        with dve.Fori(0, GROUPS // 2) as r:
            for g in range(2):
                experts(1, r, g)
        dve.wait_ge(S["g2_ready"], 1)
        dve.wait_ge(S["gfin_landed"], 16)
        for t in range(2):
            dve.wait_ge(S["acc_done"], t + 1)
            if t:
                dve.wait_ge(S["fss_ready"], 1)
            for q in range(2):
                last = tt(tmpf[:, q * 512:q * 512 + 512], P[2 * t + q][:], g2bc[:, q * 512:q * 512 + 512], ALU.mult)
            chain(last)
            tt(xtok[:, t], xtok[:, t], tmpf, ALU.add).then_inc(S["xf_ready"], 1)
        for t in range(2):
            dve.wait_ge(S["fstd_ready"], t + 1)
            chain(nc.vector.reciprocal(small[:, 48 + t:49 + t], small[:, 46 + t:47 + t]))
            stt(xtok[:, t], xtok[:, t], small[:, 48 + t:49 + t], gfin, ALU.mult, ALU.mult).then_inc(S["y_ready"], 1)


INPUTS = ["x", "mem", "norm_g", "ffn_w_up", "ffn_w_down", "mem_norm_g", "mem_w_kv", "pool_w_in", "pool_w_group", "pool_scale",
          "pool_w_out", "diff_w_in", "diff_lambda", "diff_norm_g", "diff_w_out", "final_norm_g", "c_2", "w_ada_2", "b_ada_2",
          "norm_attn_2", "norm_ffn_2", "w_in_2", "w_out_2", "rel_bias_2", "peer_wq_2", "peer_subkeys_2", "peer_u_2",
          "peer_v_2", "norm_final_2"]


def kernel(**inputs):
    import numpy as np
    import concourse.bacc as bacc
    from concourse.bass_utils import run_bass_kernel_spmd as run

    nc = bacc.Bacc("TRN2", target_bir_lowering=False, num_devices=1)
    arrays, aps = {}, {}
    for name in INPUTS:
        v = np.ascontiguousarray(inputs[name])
        arrays["in_" + name] = v
        aps[name] = nc.dram_tensor("in_" + name, v.shape, mybir.dt.from_np(v.dtype), kind="ExternalInput").ap()
    out = nc.dram_tensor("out_0", (1, T, D), F32, kind="ExternalOutput").ap()
    program(nc, aps, out)
    r = run(nc, [arrays], core_ids=[0])
    return r.results[0]["out_0"]
```

```python
import math

import concourse.bass as bass
from concourse import mybir
from contextlib import ExitStack

F32 = mybir.dt.float32
F32R = mybir.dt.float32r
I32 = mybir.dt.int32
U32 = mybir.dt.uint32
ALU = mybir.AluOpType
ACT = mybir.ActivationFunctionType
AX = mybir.AxisListType

D = 1024
T = 256
KT = D // 128
FF = 2816
FT = FF // 128
NEG = -1.0e30
TAKEN = -3.0e38
BUCKET_START = [*range(16), 23, 32, 46, 64, 91, 128, 182]
TOPK = min(256, T // 4)
NG = 8
GROUPS = 128 // NG
STOP = 99


def bucket_ranges():
    starts = [*range(16), 16, 23, 32, 46, 64, 91, 128, 182]
    return [(b, s, (starts[b + 1] if b + 1 < len(starts) else T)) for b, s in enumerate(starts)]


def program(nc, a, out):
    ctx = ExitStack()
    stage_a = ExitStack()

    def sb(name, shape, dt=F32, where=None):
        return (where or ctx).enter_context(nc.sbuf_tensor(name, shape, dt))

    def sem(name):
        return ctx.enter_context(nc.semaphore(name))

    xT = sb("xT", [128, KT, T])
    ident = sb("ident", [128, 128])
    ones = sb("ones", [128, 128])
    cols = sb("cols", [128, 104])
    modc = sb("modc", [128, 48])
    badac = sb("badac", [128, 48])
    silc = sb("silc", [128, KT])
    eps = sb("eps", [128, 4])
    gmod = sb("gmod", [128, 2 * KT])
    rstd = sb("rstd", [128, T])
    small = sb("small", [128, 64])
    lam = sb("lam", [128, 384])
    st = sb("st", [128, 32])
    M = sb("M", [128, 3072 + 8704])
    WR = sb("WR", [128, 2, 4096], F32, stage_a)
    WH = sb("WH", [128, 2, 2048], F32R, stage_a)
    WL = sb("WL", [128, 2, 2048], F32R, stage_a)
    hTh = sb("hTh", [128, KT, T], F32R, stage_a)
    hTl = sb("hTl", [128, KT, T], F32R, stage_a)
    actH = sb("actH", [128, FT, T], F32R, stage_a)
    actL = sb("actL", [128, FT, T], F32R, stage_a)
    adaW = sb("adaW", [128, KT, 128], F32, stage_a)
    adaS = sb("adaS", [128, 2, 512], F32, stage_a)
    memK = sb("memK", [128, 2, 4, T], F32, stage_a)
    memV = sb("memV", [128, 2, 2, 512], F32, stage_a)
    stage_a.close()
    GU = sb("GU", [128, 2, NG, D])
    GV = sb("GV", [128, 2, NG, D])
    xtok = sb("xtok", [128, 2, D])
    htok = sb("htok", [128, 2, D])
    P = [ctx.enter_context(nc.psum_tensor(f"P{i}", [128, 512], F32)) for i in range(8)]
    rel_rows = nc.dram_tensor("rel_rows", (16, 128 * 512), F32, kind="Internal").ap()

    def view(at, *shape):
        n = math.prod(shape)
        v = M[:, at:at + n]
        if len(shape) == 1:
            return v
        names = "abcd"[:len(shape)]
        return v.rearrange(f"p ({' '.join(names)}) -> p {' '.join(names)}",
                           **dict(zip(names[1:], shape[1:])))

    NT = view(0, KT, T)
    LB = view(0, 2, 4, T)
    GUP = view(0, 2, 2, T)
    SIL = view(2048, 2, T)
    PRD = view(2560, 2, T)
    PTS = view(2048, 2, 2, T)
    MX = 3072
    xin, memin, memT = view(MX, 2, D), view(MX + 2048, 2, D), view(MX + 4096, KT, T)
    rows1 = view(MX + 6144, 128)
    rows2 = view(MX + 6272, 128)
    relr = view(MX + 6400, 512)
    relz = view(MX + 6912, 512)
    reltab = view(MX + 7424, 32)
    PADW = T + 16
    uT = view(MX, KT, PADW)
    wa = view(MX + 2176, 2, PADW)
    wb = view(MX + 2720, 2, PADW)
    inv = view(MX + 3264, 4, T)
    xq0 = view(MX + 4288, 4, T)
    ptmp = view(MX + 5312, KT, T)
    dQ, dK, dV = view(MX, 8, T), view(MX + 2048, 8, T), view(MX + 4096, 2, D)
    xq1 = view(MX + 6144, 4, T)
    dist = view(MX + 7168, 2, T)
    bias1 = view(MX + 7680, 2, 2, T)
    lamw = lam[:, 0:256].rearrange("p (a b) -> p a b", a=4)
    lamp = lam[:, 256:384].rearrange("p (a b) -> p a b", a=2)
    hQ, hK, hV = view(MX, 8, T), view(MX + 2048, 8, T), view(MX + 4096, 2, 1024)
    iQ, iK = view(MX + 6144, 2, T), view(MX + 6656, T)
    pen = view(MX + 6912, 2, T)
    bias2 = view(MX + 7424, 2, 2, T)
    iw = small[:, 32:40].rearrange("p (a b) -> p a b", a=2)
    score, work, relu2 = view(0, 2, T), view(512, 2, T), view(1024, 2, 2, T)
    NT2, rstd2 = view(MX, KT, T), view(MX + 2048, T)
    rcol = small[:, 40:42]
    sks = [view(0, 16, 128), view(MX + 2048, 16, 128)]
    v16, i16, i16f = (view(at, 16, 16) for at in (2048, 2304, 2560))
    i16 = i16.bitcast(U32)
    gs, pos = view(2816, 8, 16), view(2944, 8, 16).bitcast(U32)
    pQ = view(MX, 4, 2, T)
    cand = view(MX, 8, 16, 16)
    diag = view(MX, 2, NG, 128)
    tmpf = view(MX + 2048, D)
    skT = view(MX + 4096, 16, 128)
    posd, posf, psel = (view(MX + at, 2, 128) for at in (4096, 4352, 4608))
    iota16 = view(MX + 4864, 16)
    zro = view(MX + 5120, 128)
    dots, gel8, coef8 = (view(MX + at, 2, NG) for at in (5248, 5264, 5280))
    idxu, idxv = (view(MX + at, 2, NG).bitcast(I32) for at in (5296, 5312))
    skin = view(MX + 6144, 16, 128)
    skw = view(MX + 6144, 16, 128)
    candw = view(MX + 6144, 8, 256)
    hot = view(MX + 6144, 8, 16, 16)
    gfin, g2bc = view(MX + 6144, D), view(MX + 7168, D)
    eidx = view(MX + 8192, 256).bitcast(I32)
    gate = view(MX + 8448, 2, 8, 16)
    gatec = view(MX + 8448, 256)

    G_NORM, G_MEM, G_POOL, G_ATT, G_FFN, G_C, G_FIN, G_DIFF = 0, 48, 56, 64, 72, 80, 88, 96

    names = """x_landed mem_landed rows_landed rel_landed rel_stored iden_ready const_ready x_tr x_in mem_tr mem_in
        cols_tr cols_ready silc_ready hi_ready lo_ready half_used bank_free sq_ready ss_ready std_ready
        hn_ready hh_ready hl_ready sil_ready act_hi act_lo x_ready dve_chain pool_chain ada_landed ada_sum
        ada_done mod_ready gmod_ready lam_landed lam_ready lam_exp neglam_ready inv_ready pad_ready pooled_ready pool_hi pool_lo
        group_done mix_hi mix_lo score_done logits_ready neg_max exp_done rsum_ready prob_ready
        diffp_ready tr_done pt_ready o_done o_hi o_ready bias_ready dist_ready osq_ready oss_ready ostd_ready
        on_ready on_hi on_lo ik_sq ik_ss ik_std ik_ready idx_products idx_relu idx_summed masked_ready iota_ready pen_ready bias_landed
        sk_landed sk_tr sk_ready htok_tr htok_ready xtok_tr xtok_ready sk_scores s_ready gdiff_ready gexp_ready gate_ready
        index_ready dots_ready gelu_ready coef_ready diag_ready v_used iu_ready iv_ready g2_diag g2_tr g2_ready gfin_landed
        acc_done rstd_made prod_ready rcol_tr rcol_ready m2_ready xf_ready fss_ready fstd_ready y_ready stored peer_free zero_ready""".split()
    S = {n: sem(n) for n in names}
    raw_landed = [sem("raw_landed0"), sem("raw_landed1")]
    u_landed = [sem("u_landed0"), sem("u_landed1")]
    v_landed = [sem("v_landed0"), sem("v_landed1")]
    b_landed = [sem("b_landed0"), sem("b_landed1")]

    def kview(w):
        return w.rearrange("(k p) n -> p k n", p=128)

    chunks = []

    def raw(slot, kind, h):
        r = WR[:, slot, :]
        if kind == "cols":
            return r.rearrange("p (k n) -> p k n", k=KT)[:, :, h * 256:h * 256 + 256]
        if kind == "pair":
            return r.rearrange("p (k g j n) -> p k g j n", k=KT, g=2, j=2)[:, :, :, h, :]
        return r[:, h * 2048:h * 2048 + 2048]

    def raw_dst(slot, kind, part):
        r = WR[:, slot, :]
        if kind in ("cols", "pair"):
            return r.rearrange("p (k n) -> p k n", k=KT)[:, :, part * 256:part * 256 + 256]
        return r[:, part * 2048:part * 2048 + 2048].rearrange("p (k n) -> p k n", k=2)

    def split_view(buf, u, kind):
        b = buf[:, u, :]
        if kind == "cols":
            return b.rearrange("p (k n) -> p k n", k=KT)
        if kind == "pair":
            return b.rearrange("p (k g n) -> p k g n", k=KT, g=2)
        return b

    def add_cols(w, n0, special=None):
        chunks.append(("cols", 2, [kview(w)[:, :, n0 + 256 * q:n0 + 256 * q + 256] for q in range(2)], special))

    def add_rows(w, kts):
        for k in range(0, kts, 4):
            parts = [kview(w)[:, k + 2 * q:k + 2 * q + 2, :] for q in range(2) if k + 2 * q < kts]
            chunks.append(("rows", len(parts), parts, None))

    phases = {}
    state = dict(U=0, C=0, E=0)

    def phase(name, add):
        c0 = len(chunks)
        add()
        n = sum(c[1] for c in chunks[c0:])
        phases[name] = dict(U=state["U"], C=c0, n=n, nc=len(chunks) - c0)
        state["U"] += n

    def cols_phase(name, w, n_chunks, n0=0):
        phase(name, lambda: [add_cols(w, n0 + 512 * i) for i in range(n_chunks)])
        phases[name]["E"] = state["E"]
        state["E"] += phases[name]["n"]

    def ffn(i, f):
        def up():
            w = kview(a["ffn_w_up"][i, f])
            for c in range(FF // 256):
                chunks.append(("pair", 2, [w[:, :, g * FF + c * 256:g * FF + c * 256 + 256] for g in range(2)], None))
        phase(f"up{i}{f}", up)
        phases[f"up{i}{f}"]["E"] = state["E"]
        state["E"] += phases[f"up{i}{f}"]["n"]
        phase(f"down{i}{f}", lambda: add_rows(a["ffn_w_down"][i, f], FT))

    cols_phase("kv0", a["mem_w_kv"][0], 2)
    cols_phase("kv1", a["mem_w_kv"][1], 2)
    ffn(0, 0)
    cols_phase("pool_in", a["pool_w_in"][0], 3)

    def pool_group():
        w = a["pool_w_group"][0].rearrange("g (c p) n -> p (g c) n", p=128)
        chunks.append(("group", 2, [w[:, 4 * q:4 * q + 4, :] for q in range(2)], None))
    phase("group", pool_group)
    phases["group"]["E"] = state["E"]
    state["E"] += 4
    phase("pool_out", lambda: add_rows(a["pool_w_out"][0], 12))
    ffn(0, 1)
    ffn(1, 0)
    cols_phase("diff_in", a["diff_w_in"][0], 7)
    phase("diff_out", lambda: add_rows(a["diff_w_out"][0], 12))
    ffn(1, 1)
    w2 = a["w_in_2"][0]
    cols_phase("in2", w2, 6)
    phase("in2x", lambda: chunks.append(("cols", 2, [kview(w2)[:, :, 3072:3328]], "index")))
    phases["in2x"]["E"] = state["E"]
    state["E"] += 2
    phase("out2", lambda: add_rows(a["w_out_2"][0], KT))
    cols_phase("wq", a["peer_wq_2"][0], 4)

    half_of = []
    for c, ch in enumerate(chunks):
        half_of += [(c, h) for h in range(ch[1])]
    last_half = [max(u for u, (cc, _) in enumerate(half_of) if cc == c) for c in range(len(chunks))]
    slot_loads = []
    total = [0, 0]
    for c, ch in enumerate(chunks):
        total[c % 2] += 16 * (4 if ch[3] == "index" else len(ch[2]))
        slot_loads.append(total[c % 2])

    block = ctx.enter_context(nc.Block())

    X_AFTER = {n: 4 * (i + 1) for i, n in enumerate(
        ["input", "down00", "pool_out", "down01", "down10", "diff_out", "down11", "final", "out2"])}
    ATT = dict(mem0=0, diff=4, mem1=12, moba=16, dsa=24)
    NORMS = dict(mem=(0, G_MEM, 0), up00=(1, G_NORM, 1), pool_in=(2, G_NORM + 8, 2), up01=(3, G_NORM + 16, 3),
                 up10=(4, G_NORM + 24, 4), diff_in=(5, G_NORM + 32, 5), up11=(6, G_NORM + 40, 6), final=(7, G_FIN, None),
                 in2=(8, None, 7), wq=(9, None, 8))
    HN = dict(mem=0, in2=1, wq=2)
    LAM_INIT = 0.8 - 0.6 * math.exp(-0.3 * 1)

    def heads_of(kind):
        if kind in ("mem0", "mem1"):
            l = int(kind[3])
            xq = xq1 if l else xq0
            return [dict(a=ATT[kind] + h, qk=[(xq[:, h], memK[:, l, h])], v=lambda s, h=h: memV[:, l, s, h * 128:h * 128 + 128],
                         scale=128.0 ** -0.5, rows=(0, 128), tile=8 + h, bias=None, split=True) for h in range(4)]
        if kind == "diff":
            return [dict(a=ATT[kind] + h, qk=[(dQ[64 * c:64 * c + 64, h], dK[64 * c:64 * c + 64, h]) for c in range(2)],
                         v=lambda s, h=h: dV[:, s, h * 128:h * 128 + 128], scale=0.125, rows=(0, 128), tile=h,
                         bias=bias1[:, h % 2], bias_sem=(S["bias_ready"], h + 1), split=False, head=h) for h in range(8)]
        out = []
        for h in range(16):
            r = slice(64 * (h % 2), 64 * (h % 2) + 64)
            s = (S["bias_ready"], h + 1) if h >= 8 else (b_landed[h % 2], 32 * (h // 2 + 1))
            out.append(dict(a=ATT["moba"] + h, qk=[(hQ[r, h // 2], hK[r, h // 2])], v=lambda s, h=h: hV[:, s, h * 64:h * 64 + 64],
                            scale=0.125, rows=(r.start, r.stop), tile=h // 2, bias=bias2[:, h % 2], bias_sem=s,
                            split=True))
        return out

    ADA = {}
    for i, (name, h) in enumerate([("down00", 5), ("down00", 10), ("down01", 0), ("down01", 4), ("down01", 8), ("down10", 0),
                                   ("down10", 4), ("down10", 8), ("diff_in", 10), ("down11", 0), ("down11", 1), ("down11", 10)]):
        ADA[(name, h)] = i

    def rb(x):
        return 16 * (x % 2)

    def nmax(x, j):
        return st[:, rb(x) + j:rb(x) + j + 1]

    def rsum(x, j):
        return st[:, rb(x) + 4 + j:rb(x) + 5 + j]

    def rinv(x, j):
        return st[:, rb(x) + 8 + j:rb(x) + 9 + j]

    class Chain:
        def __init__(self, eng, s):
            self.eng, self.s, self.n = eng, s, 0

        def __call__(self, ins):
            self.n += 1
            ins.then_inc(self.s, 1)
            self.eng.wait_ge(self.s, self.n)

    @block.sync
    def _(sp):
        sp.dma_start(xin, a["x"][0].rearrange("(a p) n -> p a n", p=128)).then_inc(S["x_landed"], 16)
        sp.dma_start(memin, a["mem"][0].rearrange("(a p) n -> p a n", p=128)).then_inc(S["mem_landed"], 16)

        def vec(w):
            return w.rearrange("(a n) -> a n", n=128)
        loads = [(rows1, 0, a["norm_g"].rearrange("l s (a n) -> (l s a) n", n=128), 48), (rows1, G_MEM, vec(a["mem_norm_g"]), 8),
                 (rows1, G_POOL, vec(a["pool_scale"][0]), 8), (rows1, G_ATT, vec(a["norm_attn_2"][0]), 8),
                 (rows1, G_FFN, vec(a["norm_ffn_2"][0]), 8), (rows1, G_C, vec(a["c_2"][0]), 8),
                 (rows1, G_FIN, vec(a["final_norm_g"]), 8), (rows1, G_DIFF, a["diff_norm_g"], 1),
                 (rows2, 0, vec(a["b_ada_2"][0]), 48)]
        for r, at, src, n in loads:
            sp.dma_start(r[at:at + n, :], src).then_inc(S["rows_landed"], 16)

        def load(c):
            kind, n, parts, special = chunks[c]
            if c >= 2:
                sp.wait_ge(S["lo_ready"], last_half[c - 2] + 1)
            for q, src in enumerate(parts):
                sp.dma_start(raw_dst_of(c % 2, kind, q), src).then_inc(raw_landed[c % 2], 16)
            if special == "index":
                r = WR[:, c % 2, :].rearrange("p (k n) -> p k n", k=KT)
                for at, n0, n in ((256, 3328, 64), (320, 3328, 64), (384, 3392, 4)):
                    sp.dma_start(r[:, :, at:at + n], kview(w2)[:, :, n0:n0 + n]).then_inc(raw_landed[c % 2], 16)

        def raw_dst_of(slot, kind, part):
            if kind == "group":
                return WR[:, slot, part * 1024:part * 1024 + 1024].rearrange("p (k n) -> p k n", k=4)
            return raw_dst(slot, kind, part)

        def load_up(i, f):
            p = phases[f"up{i}{f}"]
            for c in range(3):
                load(p["C"] + c)
            w = kview(a["ffn_w_up"][i, f])
            with sp.Fori(0, 4) as r:
                for j in range(2):
                    c = 3 + j
                    sp.wait_ge(S["lo_ready"], r * 4 + last_half[p["C"] + c - 2] + 1)
                    for g in range(2):
                        sp.dma_start(raw_dst_of((p["C"] + c) % 2, "pair", g),
                                     w[:, :, bass.ds(r * 512 + (g * FF + c * 256), 256)]).then_inc(raw_landed[(p["C"] + c) % 2], 16)

        for name, p in phases.items():
            if name.startswith("up"):
                load_up(int(name[2]), int(name[3]))
            else:
                for c in range(p["C"], p["C"] + p["nc"]):
                    load(c)
        for t in range(2):
            sp.wait_ge(S["y_ready"], t + 1)
            sp.dma_start(out[0, t * 128:t * 128 + 128, :], xtok[:, t, :]).then_inc(S["stored"], 16)
        sp.wait_ge(S["stored"], 32)

    @block.gpsimd
    def _(pool):
        chain = Chain(pool, S["pool_chain"])
        pool.dma_start(reltab[0:16, :], a["rel_bias_2"]).then_inc(S["rel_landed"], 16)
        chain(nc.gpsimd.memset(ident[:], 0.0))
        nc.gpsimd.affine_select(out=ident[:], in_=ident[:], compare_op=ALU.not_equal, fill=1.0, base=0,
                                pattern=[[-1, 128]], channel_multiplier=1).then_inc(S["iden_ready"], 1)
        nc.gpsimd.memset(small[:, :], 0.0)
        nc.gpsimd.memset(eps[:, 0:1], 1e-6)
        nc.gpsimd.memset(eps[:, 1:2], 1e-5)
        nc.gpsimd.memset(ones[:], 1.0).then_inc(S["const_ready"], 1)
        nc.gpsimd.memset(relz[0:16, :], 0.0)
        chain(nc.gpsimd.memset(relr[0:16, :], NEG))
        pool.wait_ge(S["rel_landed"], 16)
        for b, lo, hi in bucket_ranges():
            if hi > lo:
                last = nc.gpsimd.tensor_scalar(relr[0:16, T - hi:T - lo], relz[0:16, T - hi:T - lo], reltab[0:16, b:b + 1],
                                               None, ALU.add)
        chain(last)
        pool.dma_start(rel_rows.rearrange("h (r n) -> h r n", n=512), relr[0:16, :].unsqueeze(1).broadcast_to([16, 128, 512])).then_inc(S["rel_stored"], 16)

        pool.wait_ge(S["silc_ready"], 1)
        wada = kview(a["w_ada_2"][0])
        cb = silc[:, :].unsqueeze(2).broadcast_to([128, KT, 128])
        base = chain.n

        def ada_piece(dram, buf, steps, landed, sums):
            for q in range(4):
                pool.dma_start(adaW[:], dram(q)).then_inc(S["ada_landed"], 16)
                pool.wait_ge(S["ada_landed"], landed(q))
                nc.gpsimd.tensor_tensor(adaW[:], adaW[:], cb, ALU.mult).then_inc(S["pool_chain"], 1)
                pool.wait_ge(S["pool_chain"], steps(3 * q + 1))
                nc.gpsimd.tensor_tensor(adaW[:, 0:4], adaW[:, 0:4], adaW[:, 4:8], ALU.add).then_inc(S["pool_chain"], 1)
                pool.wait_ge(S["pool_chain"], steps(3 * q + 2))
                nc.gpsimd.tensor_tensor(adaW[:, 0:2], adaW[:, 0:2], adaW[:, 2:4], ALU.add).then_inc(S["pool_chain"], 1)
                pool.wait_ge(S["pool_chain"], steps(3 * q + 3))
                nc.gpsimd.tensor_tensor(adaS[:, buf, q * 128:q * 128 + 128], adaW[:, 0], adaW[:, 1], ALU.add)\
                    .then_inc(S["ada_sum"], 1)
                pool.wait_ge(S["ada_sum"], sums(q + 1))

        for n in range(2):
            ada_piece(lambda q: wada[:, :, n * 512 + q * 128:n * 512 + q * 128 + 128], n,
                      lambda k: base + n * 12 + k, lambda q: n * 64 + 16 * q + 16, lambda k: 4 * n + k)

        def ada_pairs(first, n):
            with pool.Fori(0, n) as r:
                for m in range(2):
                    i = 2 * first + m
                    pool.wait_ge(S["ada_done"], r * 2 + (i - 1))
                    nc.gpsimd.tensor_tensor(small[:, 61:62], ones[:, 0:1], ones[:, 0:1], ALU.add)
                    ada_piece(lambda q: wada[:, :, bass.ds(r * 1024 + (i * 512 + q * 128), 128)], m,
                              lambda k: r * 24 + (base + 12 * i + k), lambda q: r * 128 + (i * 64 + 16 * q + 16),
                              lambda k: r * 8 + (4 * i + k))

        pool.wait_ge(S["x_ready"], X_AFTER["down00"])
        nc.gpsimd.memset(uT[:, :, 0:16], 0.0)
        nc.gpsimd.memset(wa[:, :, 0:16], 0.0)
        nc.gpsimd.memset(wb[:, :, 0:16], 0.0)
        nc.gpsimd.iota(inv[:], pattern=[[0, 4], [1, T]], base=1, channel_multiplier=0,
                       allow_small_or_imprecise_dtypes=True).then_inc(S["pad_ready"], 1)

        ada_pairs(1, 1)

        pool.wait_ge(S["x_ready"], X_AFTER["pool_out"])
        chain.n = base + 12 * 4
        chain(nc.gpsimd.iota(dist[:], pattern=[[128, 2], [-1, T]], base=0, channel_multiplier=1,
                             allow_small_or_imprecise_dtypes=True))
        chain(nc.gpsimd.affine_select(out=dist[:], in_=dist[:], compare_op=ALU.is_ge, fill=-NEG, base=0,
                                      pattern=[[128, 2], [-1, T]], channel_multiplier=1))
        base += 2
        ada_pairs(2, 3)
        for h in range(8):
            if h >= 2:
                pool.wait_ge(S["logits_ready"], ATT["diff"] + h - 1)
            nc.gpsimd.tensor_scalar(bias1[:, h % 2], dist[:], -(2.0 ** -(h + 1)), None, ALU.mult).then_inc(S["bias_ready"], 1)

        ada_pairs(5, 1)

        pool.wait_ge(S["idx_summed"], 8)
        nc.gpsimd.affine_select(out=score[:], in_=score[:], compare_op=ALU.is_ge, fill=NEG, base=0,
                                pattern=[[128, 2], [-1, T]], channel_multiplier=1).then_inc(S["masked_ready"], 1)
        pool.wait_ge(S["rel_stored"], 16)
        for h in range(16):
            if h >= 2:
                pool.wait_ge(S["logits_ready"], ATT["moba"] + h - 1)
            for t in range(2):
                pool.dma_start(bias2[:, h % 2, t], bass.AP(rel_rows.tensor, h * 65536 + 255 - 128 * t, [[511, 128], [1, T]]))\
                    .then_inc(b_landed[h % 2], 16)
            if h >= 8:
                pool.wait_ge(b_landed[h % 2], 32 * (h // 2 + 1))
                pool.wait_ge(S["pen_ready"], 2)
                nc.gpsimd.tensor_tensor(bias2[:, h % 2], bias2[:, h % 2], pen[:], ALU.add).then_inc(S["bias_ready"], 1)

        ub, vb = a["peer_u_2"][0], a["peer_v_2"][0]

        def gathers(buf, idx, table, landed, par):
            for i in range(NG):
                pool.indirect_dma_start(buf[:, par, i, :], None, table,
                                        bass.IndirectOffsetOnAxis(ap=idx[:, par, i:i + 1], axis=0)).then_inc(landed[par], 16)
        pool.wait_ge(S["s_ready"], 8)
        nc.gpsimd.memset(zro, 0.0).then_inc(S["zero_ready"], 1)
        nc.gpsimd.iota(iota16, pattern=[[1, 16]], base=0, channel_multiplier=0,
                       allow_small_or_imprecise_dtypes=True).then_inc(S["iota_ready"], 1)
        pool.wait_ge(S["index_ready"], 1)
        for g in range(2):
            nc.gpsimd.tensor_copy(idxu[:, g, :], eidx[:, g * NG:g * NG + NG]).then_inc(S["iu_ready"], 1)
            pool.wait_ge(S["iu_ready"], g + 1)
            gathers(GU, idxu, ub, u_landed, g)
        for g in range(2):
            nc.gpsimd.tensor_copy(idxv[:, g, :], eidx[:, g * NG:g * NG + NG]).then_inc(S["iv_ready"], 1)
            pool.wait_ge(S["iv_ready"], g + 1)
            gathers(GV, idxv, vb, v_landed, g)
        pool.wait_ge(S["index_ready"], 2)
        pool.dma_start(gfin, a["norm_final_2"].partition_broadcast(128)).then_inc(S["gfin_landed"], 16)
        with pool.Fori(0, GROUPS - 1) as r:
            for g in range(2):
                pool.wait_ge(S["dots_ready"], r * 2 + (g + 1))
                nc.gpsimd.tensor_tensor(small[:, 50 + g:51 + g], small[:, 58:59], small[:, 58:59], ALU.add)
                nc.gpsimd.tensor_copy(idxu[:, g, :], eidx[:, bass.ds(r * 2 * NG + ((2 + g) * NG), NG)]).then_inc(S["iu_ready"], 1)
                pool.wait_ge(S["iu_ready"], r * 2 + (g + 3))
                nc.gpsimd.tensor_tensor(small[:, 52 + g:53 + g], small[:, 58:59], small[:, 58:59], ALU.add)
                gathers(GU, idxu, ub, u_landed, g)
                pool.wait_ge(S["v_used"], r * 2 + (g + 1))
                nc.gpsimd.tensor_tensor(small[:, 54 + g:55 + g], small[:, 58:59], small[:, 58:59], ALU.add)
                nc.gpsimd.tensor_copy(idxv[:, g, :], eidx[:, bass.ds(r * 2 * NG + ((2 + g) * NG), NG)]).then_inc(S["iv_ready"], 1)
                pool.wait_ge(S["iv_ready"], r * 2 + (g + 3))
                nc.gpsimd.tensor_tensor(small[:, 56 + g:57 + g], small[:, 58:59], small[:, 58:59], ALU.add)
                gathers(GV, idxv, vb, v_landed, g)

    @block.tensor
    def _(pe):
        mm = nc.tensor.matmul

        def product(o, wh, wl, xh, xl, first, last, skip=False):
            mm(o, wh, xh, start=first, stop=False, skip_group_check=skip)
            mm(o, wh, xl, start=False, stop=False, skip_group_check=skip)
            return mm(o, wl, xh, start=False, stop=last, skip_group_check=skip)

        def cols_half(U, u, E, e, wait_bank=True, pieces=None):
            pe.wait_ge(S["lo_ready"], U + 1)
            if wait_bank:
                pe.wait_ge(S["bank_free"], E - 1)
            for b in range(2):
                for k in range(KT):
                    if pieces is not None and b == 0 and k % 2 == 0:
                        pe.wait_ge(S["hl_ready"], 4 * pieces + k // 2 + 1)
                    c = k * 256 + b * 128
                    last = product(P[4 + e][:, b * 256:b * 256 + 256], WH[:, u, c:c + 128], WL[:, u, c:c + 128],
                                   hTh[:, k], hTl[:, k], k == 0, k == KT - 1)
            last.then_inc(S["half_used"], 1)

        def values_half(U, E):
            u, e = U % 2, E % 2
            pe.wait_ge(S["lo_ready"], U + 1)
            pe.wait_ge(S["bank_free"], E - 1)
            for t in range(2):
                o = P[4 + e][:, t * 256:t * 256 + 256]
                for k in range(KT):
                    w = slice(k * 256, k * 256 + 256)
                    xh, xl = hTh[:, k, t * 128:t * 128 + 128], hTl[:, k, t * 128:t * 128 + 128]
                    mm(o, xh, WH[:, u, w], start=(k == 0), stop=False)
                    mm(o, xh, WL[:, u, w], start=False, stop=False)
                    last = mm(o, xl, WH[:, u, w], start=False, stop=(k == KT - 1))
            last.then_inc(S["half_used"], 1)

        def rows_half(U, kt0, nkt):
            pe.wait_ge(S["lo_ready"], U + 1)
            for kk in range(2):
                for d in range(KT):
                    k = kt0 + kk
                    c = kk * 1024 + d * 128
                    last = product(P[d // 2][:, (d % 2) * 256:(d % 2) * 256 + 256], WH[:, U % 2, c:c + 128],
                                   WL[:, U % 2, c:c + 128], actH[:, k], actL[:, k], k == 0 and d % 2 == 0, k == nkt - 1, True)
            last.then_inc(S["half_used"], 1)

        def ada(name, h):
            i = ADA.get((name, h))
            if i is None:
                return
            pe.wait_ge(S["ada_sum"], 4 * i + 4)
            if i == 8:
                pe.wait_ge(S["rcol_ready"], 1)
            if i:
                pe.wait_ge(S["mod_ready"], i)
            for j in range(4):
                last = mm(P[7][:, j:j + 1], adaS[:, i % 2, j * 128:j * 128 + 128], ones[:, 0:1], start=True, stop=True)
            last.then_inc(S["ada_done"], 1)

        def norm(name, squares=NT, bank=6):
            n = NORMS[name][0]
            if n and bank == 6:
                pe.wait_ge(S["std_ready"], n)
            for q in range(4):
                pe.wait_ge(S["sq_ready"], 4 * n + q + 1)
                for k in (2 * q, 2 * q + 1):
                    last = mm(P[bank][:, 0:T], ones[:], squares[:, k], start=(k == 0), stop=(k == KT - 1))
            last.then_inc(S["ss_ready"], 1)

        def split_ready(name):
            pe.wait_ge(S["hl_ready"], 4 * (NORMS[name][2] + 1))

        def first_half(name):
            U, E = phases[name]["U"], phases[name]["E"]
            cols_half(U, U % 2, E, E % 2, pieces=NORMS[name][2])
            norm(name)

        def ffn(i, f):
            first_half(f"up{i}{f}")
            p = phases[f"up{i}{f}"]
            U, E = p["U"], p["E"]
            cols_half(U + 1, (U + 1) % 2, E + 1, (E + 1) % 2)
            with pe.Fori(0, 5) as r:
                for j in range(2, 6):
                    cols_half(r * 4 + (U + j), (U + j) % 2, r * 4 + (E + j), (E + j) % 2)
            p = phases[f"down{i}{f}"]
            for v in range(p["n"]):
                pe.wait_ge(S["act_lo"], FT * (2 * i + f) + 2 * v + 2)
                rows_half(p["U"] + v, 2 * v, FT)
                ada(f"down{i}{f}", v)

        def attention(units):
            def scores(x):
                a, b = x["a"], 4 * (x["a"] % 2)
                if a >= 2:
                    pe.wait_ge(S["logits_ready"], a - 1)
                for c, (q, k) in enumerate(x["qk"]):
                    for t in range(2):
                        last = mm(P[b + c][:, t * T:t * T + T], q[:, t * 128:t * 128 + 128], k, start=True, stop=True)
                last.then_inc(S["score_done"], 1)

            def transposes(x):
                a = x["a"]
                if len(x["qk"]) == 2:
                    pe.wait_ge(S["diffp_ready"], x["head"] + 1)
                pe.wait_ge(S["prob_ready"], a + 1)
                if a >= 2:
                    pe.wait_ge(S["pt_ready"], a - 1)
                for s in range(2):
                    for t in range(2):
                        last = nc.tensor.transpose(P[2 + a % 2][:, s * T + t * 128:s * T + t * 128 + 128],
                                                   LB[:, a % 2, t, s * 128:s * 128 + 128], ident[:])
                last.then_inc(S["tr_done"], 1)

            def weighted(x):
                a = x["a"]
                pe.wait_ge(S["pt_ready"], a + 1)
                if a >= 2:
                    pe.wait_ge(S["o_ready"], a - 1)
                for s in range(2):
                    last = mm(P[6 + a % 2][x["rows"][0]:x["rows"][1], 0:T], x["v"](s), PTS[:, a % 2, s],
                              start=(s == 0), stop=(s == 1))
                last.then_inc(S["o_done"], 1)

            scores(units[0])
            for i in range(len(units) + 1):
                if i + 1 < len(units):
                    scores(units[i + 1])
                if i < len(units):
                    transposes(units[i])
                if i >= 1:
                    weighted(units[i - 1])

        pe.wait_ge(S["iden_ready"], 1)
        pe.wait_ge(S["const_ready"], 1)
        for b0, src, landed, done in ((4, memin, "mem_landed", "mem_tr"), (0, xin, "x_landed", "x_tr")):
            pe.wait_ge(S[landed], 16)
            for q in range(4):
                for kk in range(2):
                    for t in range(2):
                        k = 2 * q + kk
                        last = nc.tensor.transpose(P[b0 + q][:, kk * T + t * 128:kk * T + t * 128 + 128],
                                                   src[:, t, k * 128:k * 128 + 128], ident[:])
                last.then_inc(S[done], 1)
        pe.wait_ge(S["rows_landed"], 9 * 16)
        pe.wait_ge(S["x_ready"], 1)
        nc.tensor.transpose(P[0][:, 0:97], rows1[0:97, :], ident[0:97, 0:97])
        nc.tensor.transpose(P[0][:, 128:176], rows2[0:48, :], ident[0:48, 0:48]).then_inc(S["cols_tr"], 1)

        norm("mem")
        split_ready("mem")
        for l in range(2):
            p = phases[f"kv{l}"]
            for j in range(2):
                U, E = p["U"] + j, p["E"] + j
                cols_half(U, U % 2, E, E % 2, wait_bank=E >= 2)
            for j in range(2, 4):
                values_half(p["U"] + j, p["E"] + j)
        ffn(0, 0)

        first_half("pool_in")
        p = phases["pool_in"]
        for j in range(1, 6):
            cols_half(p["U"] + j, (p["U"] + j) % 2, p["E"] + j, (p["E"] + j) % 2)
        pe.wait_ge(S["bank_free"], p["E"] + 6)
        pe.wait_ge(S["mod_ready"], 2)
        attention(heads_of("mem0"))
        p = phases["group"]
        pe.wait_ge(S["logits_ready"], 4)
        pe.wait_ge(S["pool_lo"], 4)
        for g in range(4):
            U, E = p["U"] + g // 2, p["E"] + g
            pe.wait_ge(S["lo_ready"], U + 1)
            pe.wait_ge(S["bank_free"], E - 1)
            for b in range(2):
                for c in range(2):
                    w = ((g % 2) * 2 + c) * 256 + b * 128
                    last = product(P[4 + E % 2][:, b * 256:b * 256 + 256], WH[:, U % 2, w:w + 128], WL[:, U % 2, w:w + 128],
                                   hTh[:, 2 * g + c], hTl[:, 2 * g + c], c == 0, c == 1)
            last.then_inc(S["group_done" if g % 2 == 0 else "half_used"], 1)
        p = phases["pool_out"]
        pe.wait_ge(S["o_ready"], 4)
        pe.wait_ge(S["mix_lo"], 4)
        for v in range(6):
            rows_half(p["U"] + v, 2 * v, 12)
        ffn(0, 1)
        ffn(1, 0)

        first_half("diff_in")
        p = phases["diff_in"]
        for j in range(1, 14):
            if j == 3:
                pe.wait_ge(S["rstd_made"], NORMS["diff_in"][2])
                pe.wait_ge(S["mod_ready"], 8)
                for t in range(2):
                    last = nc.tensor.transpose(P[7][:, t * 128:t * 128 + 128], rstd[:, t * 128:t * 128 + 128], ident[:])
                last.then_inc(S["rcol_tr"], 1)
            if 8 <= j < 12:
                values_half(p["U"] + j, p["E"] + j)
            else:
                cols_half(p["U"] + j, (p["U"] + j) % 2, p["E"] + j, (p["E"] + j) % 2)
            ada("diff_in", j)
        pe.wait_ge(S["bank_free"], p["E"] + 14)
        pe.wait_ge(S["mod_ready"], 9)
        attention(heads_of("diff") + heads_of("mem1"))
        pe.wait_ge(S["osq_ready"], 1)
        for q in range(4):
            mm(P[q][:], ones[:], M[:, 512 * q:512 * q + 512], start=True, stop=True).then_inc(S["oss_ready"], 1)
        p = phases["diff_out"]
        pe.wait_ge(S["o_ready"], ATT["moba"])
        pe.wait_ge(S["on_lo"], 4)
        for v in range(6):
            rows_half(p["U"] + v, 2 * v, 12)
        ffn(1, 1)
        norm("final")

        pe.wait_ge(S["mod_ready"], 12)
        norm("in2", NT2, 7)
        split_ready("in2")
        p = phases["in2"]
        for j in range(12):
            if j in (4, 5, 10, 11):
                values_half(p["U"] + j, p["E"] + j)
            else:
                cols_half(p["U"] + j, (p["U"] + j) % 2, p["E"] + j, (p["E"] + j) % 2)
        p = phases["in2x"]
        cols_half(p["U"], p["U"] % 2, p["E"], p["E"] % 2)
        U, E = p["U"] + 1, p["E"] + 1
        u, o = U % 2, P[4 + E % 2]
        pe.wait_ge(S["lo_ready"], U + 1)
        pe.wait_ge(S["bank_free"], E - 1)
        for k in range(KT):
            c = k * 256
            product(o[:, 0:T], WH[:, u, c:c + 128], WL[:, u, c:c + 128], hTh[:, k], hTl[:, k], k == 0, k == KT - 1)
        for t in range(2):
            for k in range(KT):
                w = slice(k * 256 + 128, k * 256 + 132)
                xh, xl = hTh[:, k, t * 128:t * 128 + 128], hTl[:, k, t * 128:t * 128 + 128]
                ot = o[:, T + 4 * t:T + 4 * t + 4]
                mm(ot, xh, WH[:, u, w], start=(k == 0), stop=False)
                mm(ot, xh, WL[:, u, w], start=False, stop=False)
                last = mm(ot, xl, WH[:, u, w], start=False, stop=(k == KT - 1))
        last.then_inc(S["half_used"], 1)
        pe.wait_ge(S["ik_sq"], 1)
        mm(P[6][:, 0:T], ones[:], relu2[:, 0, 0], start=True, stop=True).then_inc(S["ik_ss"], 1)
        pe.wait_ge(S["bank_free"], p["E"] + 2)
        for t in range(2):
            for h in range(4):
                r = slice(64 * (h % 2), 64 * (h % 2) + 64)
                n = 4 * t + h
                if n >= 2:
                    pe.wait_ge(S["idx_relu"], n - 1)
                mm(P[n % 2][:, 0:T], iQ[r, h // 2, t * 128:t * 128 + 128], iK[r, :], start=True, stop=True)\
                    .then_inc(S["idx_products"], 1)
        pe.wait_ge(S["idx_relu"], 8)
        attention(heads_of("heads"))
        p = phases["out2"]
        pe.wait_ge(S["o_ready"], ATT["moba"] + 16)
        for v in range(4):
            rows_half(p["U"] + v, 2 * v, KT)

        norm("wq")
        for t in range(2):
            for q in range(2):
                for k in range(4):
                    last = nc.tensor.transpose(P[2 * t + q][:, k * 128:k * 128 + 128],
                                               xT[:, 4 * q + k, t * 128:t * 128 + 128], ident[:])
                last.then_inc(S["xtok_tr"], 1)
        pe.wait_ge(S["sk_landed"], 16)
        for q, b in enumerate((4, 5, 7, 0)):
            if q == 3:
                pe.wait_ge(S["xtok_ready"], 1)
            for k in range(4):
                last = nc.tensor.transpose(P[b][:, k * 128:k * 128 + 128], skin[:, 4 * q + k], ident[:])
            last.then_inc(S["sk_tr"], 1)
        pe.wait_ge(S["hn_ready"], 4 * 3)
        pe.wait_ge(S["xtok_ready"], 4)
        pe.wait_ge(S["sk_ready"], 3)
        for n, b in enumerate((1, 2, 3, 7)):
            for k in range(4):
                last = nc.tensor.transpose(P[b][:, k * 128:k * 128 + 128],
                                           NT[:, 4 * (n % 2) + k, (n // 2) * 128:(n // 2) * 128 + 128], ident[:])
            last.then_inc(S["htok_tr"], 1)
        split_ready("wq")
        p = phases["wq"]

        def subkey_scores(j):
            if j == 0:
                pe.wait_ge(S["sk_ready"], 4)
            if j == 1:
                pe.wait_ge(S["htok_ready"], 1)
            pe.wait_ge(S["bank_free"], p["E"] + j + 1)
            if j >= 2:
                pe.wait_ge(S["s_ready"], j - 1)
            for t in range(2):
                for b in range(2):
                    last = mm(P[j % 2][:, t * 256 + b * 128:t * 256 + b * 128 + 128], pQ[:, j % 4, b, t * 128:t * 128 + 128],
                              skT[:, 2 * j + b], start=True, stop=True)
            last.then_inc(S["sk_scores"], 1)
        for j in range(8):
            cols_half(p["U"] + j, (p["U"] + j) % 2, p["E"] + j, (p["E"] + j) % 2)
            if j:
                subkey_scores(j - 1)
        subkey_scores(7)
        pe.wait_ge(S["zero_ready"], 1)
        pe.wait_ge(S["htok_ready"], 4)
        for b in range(4):
            mm(P[b][:], zro, xtok[:, 0, 0:512], start=True, stop=False, skip_group_check=True)
        pe.wait_ge(S["g2_diag"], 1)
        for k in range(KT):
            last = mm(P[4 + k // 4][:, (k % 4) * 128:(k % 4) * 128 + 128], ones[:], diag[:, 0, k], start=True, stop=True)
        last.then_inc(S["g2_tr"], 1)

        def experts(t, r, g):
            pe.wait_ge(S["diag_ready"], r * 2 + (t * GROUPS + g + 1))
            pe.wait_ge(v_landed[g], r * (16 * NG) + (t * GROUPS // 2 + 1) * 16 * NG)
            for i in range(NG):
                for q in range(2):
                    last = mm(P[2 * t + q][:], diag[:, g, i], GV[:, g, i, q * 512:q * 512 + 512], start=False, stop=False,
                              skip_group_check=True)
            last.then_inc(S["v_used"], 1)
        for t in range(2):
            with pe.Fori(0, GROUPS // 2) as r:
                for g in range(2):
                    experts(t, r, g)
            for q in range(2):
                last = mm(P[2 * t + q][:], zro, xtok[:, 1, 0:512], start=False, stop=True, skip_group_check=True)
            last.then_inc(S["acc_done"], 1)

    @block.scalar
    def _(act):
        copy = ACT.Copy

        def split(U):
            if U >= len(half_of):
                return
            c, h = half_of[U]
            kind = chunks[c][0]
            if U >= 2:
                act.wait_ge(S["half_used"], U - 1)
            act.wait_ge(raw_landed[c % 2], slot_loads[c])
            if kind == "group":
                nc.scalar.activation(WH[:, U % 2, 0:1024], WR[:, c % 2, h * 1024:h * 1024 + 1024], copy).then_inc(S["hi_ready"], 1)
            else:
                nc.scalar.activation(split_view(WH, U % 2, kind), raw(c % 2, kind, h), copy).then_inc(S["hi_ready"], 1)

        def split_loop(U, r, par):
            c, h = half_of[U]
            act.wait_ge(S["half_used"], r * 4 + (U - 1))
            act.wait_ge(raw_landed[c % 2], r * 32 + slot_loads[c])
            nc.scalar.activation(split_view(WH, U % 2, "pair"), raw(c % 2, "pair", h), copy).then_inc(S["hi_ready"], 1)

        def norm(name, src, ready, base, between=None):
            n, _, m = NORMS[name]
            if n == 1:
                act.wait_ge(S["hl_ready"], 4)
            for q in range(4):
                act.wait_ge(S[ready], base + q + 1)
                nc.scalar.activation(NT[:, 2 * q:2 * q + 2], src[:, 2 * q:2 * q + 2], ACT.Square).then_inc(S["sq_ready"], 1)
            act.wait_ge(S["ss_ready"], n + 1)
            nc.scalar.activation(rstd[:], P[6][:, 0:T], ACT.Sqrt, bias=eps[:, 0:1], scale=1.0 / D).then_inc(S["std_ready"], 1)
            if m is None:
                return
            if between:
                between()
            nxt = {"mem": "kv0"}.get(name, name)
            if phases[nxt]["U"]:
                act.wait_ge(S["half_used"], phases[nxt]["U"])
            for q in range(4):
                act.wait_ge(S["hn_ready"], 4 * HN[name] + q + 1)
                nc.scalar.activation(hTh[:, 2 * q:2 * q + 2], NT[:, 2 * q:2 * q + 2], copy).then_inc(S["hh_ready"], 1)

        def late_norm(name, base):
            n, gain, m = NORMS[name]

            def squares():
                for q in range(4):
                    act.wait_ge(S["x_ready"], base + q + 1)
                    nc.scalar.activation(NT[:, 2 * q:2 * q + 2], xT[:, 2 * q:2 * q + 2], ACT.Square).then_inc(S["sq_ready"], 1)
            if n == 1:
                act.wait_ge(S["hl_ready"], 4)
                squares()
                act.wait_ge(S["half_used"], phases[name]["U"])
            for q in range(4):
                act.wait_ge(S["x_ready"], base + q + 1)
                for k in (2 * q, 2 * q + 1):
                    last = nc.scalar.activation(hTh[:, k], xT[:, k], copy, scale=cols[:, gain + k:gain + k + 1])
                last.then_inc(S["hh_ready"], 1)
            if n > 1:
                squares()

        def late_std(name):
            n = NORMS[name][0]
            act.wait_ge(S["ss_ready"], n + 1)
            nc.scalar.activation(rstd[:], P[6][:, 0:T], ACT.Sqrt, bias=eps[:, 0:1], scale=1.0 / D).then_inc(S["std_ready"], 1)

        def gate_silu(E, s, j):
            act.wait_ge(S["bank_free"], E + 1)
            if j >= 2:
                act.wait_ge(S["prod_ready"], s - 1)
            nc.scalar.activation(SIL[:, j % 2], GUP[:, j % 2, 0], ACT.Silu).then_inc(S["sil_ready"], 1)

        def hi_act(s, j, tile):
            act.wait_ge(S["prod_ready"], s)
            nc.scalar.activation(tile, PRD[:, j % 2], copy).then_inc(S["act_hi"], 1)

        def ffn(i, f, base):
            late_norm(f"up{i}{f}", base)
            p = phases[f"up{i}{f}"]
            U, E, s0 = p["U"], p["E"], FT * (2 * i + f)

            def step(j):
                split(U + j + 2)
                if j == 0:
                    late_std(f"up{i}{f}")
                gate_silu(E + j, s0 + j, j)
                if j:
                    hi_act(s0 + j, j - 1, actH[:, j - 1])
            step(0)
            step(1)
            with act.Fori(0, 4) as r:
                for j in range(2, 6):
                    split_loop(U + j + 2, r, j)
                    gate_silu(r * 4 + (E + j), r * 4 + (s0 + j), j)
                    hi_act(r * 4 + (s0 + j), j - 1, actH[:, bass.ds(r * 4 + (j - 1), 1), :].rearrange("p a t -> p (a t)"))
            for j in range(18, 22):
                step(j)
            hi_act(s0 + 22, 21, actH[:, 21])
            p = phases[f"down{i}{f}"]
            for v in range(p["n"]):
                split(p["U"] + v + 2)

        def attention(units):
            def exps(x):
                a, n = x["a"], 2 * len(x["qk"])
                act.wait_ge(S["neg_max"], a + 1)
                for j in range(n):
                    last = nc.scalar.activation(LB[:, a % 2, j], LB[:, a % 2, j], ACT.Exp, bias=nmax(a, j), scale=1.0,
                                                accum_out=rsum(a, j))
                last.then_inc(S["exp_done"], 1)

            def normalise(x):
                a = x["a"]
                act.wait_ge(S["rsum_ready"], a + 1)
                for t in range(2):
                    last = nc.scalar.activation(LB[:, a % 2, t], LB[:, a % 2, t], copy, scale=rinv(a, t))
                last.then_inc(S["prob_ready"], 1)

            def pt(x):
                a = x["a"]
                act.wait_ge(S["tr_done"], a + 1)
                if a >= 2:
                    act.wait_ge(S["o_done"], a - 1)
                nc.scalar.activation(PTS[:, a % 2].rearrange("p a b -> p (a b)"), P[2 + a % 2][:], copy).then_inc(S["pt_ready"], 1)

            def result(x):
                if not x["split"]:
                    return
                a, (r0, r1) = x["a"], x["rows"]
                act.wait_ge(S["o_done"], a + 1)
                nc.scalar.activation(actH[r0:r1, x["tile"]], P[6 + a % 2][r0:r1, 0:T], copy).then_inc(S["o_hi"], 1)

            exps(units[0])
            for i in range(len(units) + 1):
                if i < len(units):
                    normalise(units[i])
                if i + 1 < len(units):
                    exps(units[i + 1])
                if i < len(units):
                    pt(units[i])
                if i >= 1:
                    result(units[i - 1])

        act.dma_start(lamw, a["diff_lambda"][0].partition_broadcast(128)).then_inc(S["lam_landed"], 16)
        for q in range(4):
            act.wait_ge(S["mem_tr"], q + 1)
            nc.scalar.activation(memT[:, 2 * q:2 * q + 2].rearrange("p a b -> p (a b)"), P[4 + q][:], copy).then_inc(S["mem_in"], 1)
        split(0)
        split(1)
        act.wait_ge(S["const_ready"], 1)
        act.wait_ge(S["cols_ready"], 1)
        nc.scalar.activation(silc[:], cols[:, G_C:G_C + KT], ACT.Silu).then_inc(S["silc_ready"], 1)
        norm("mem", memT, "mem_in", 0)
        for U in range(8):
            split(U + 2)
        ffn(0, 0, 0)
        late_norm("pool_in", X_AFTER["down00"] - 4)
        p = phases["pool_in"]
        for j in range(6):
            split(p["U"] + j + 2)
            if j == 0:
                late_std("pool_in")
        for g in range(4):
            act.wait_ge(S["pooled_ready"], g + 1)
            nc.scalar.activation(hTh[:, 2 * g:2 * g + 2], ptmp[:, 2 * g:2 * g + 2], copy).then_inc(S["pool_hi"], 1)
        attention(heads_of("mem0"))
        p = phases["group"]
        for j in range(2):
            for g in (2 * j, 2 * j + 1):
                if g % 2:
                    split(p["U"] + j + 2)
                act.wait_ge(S["bank_free"], p["E"] + g + 1)
                nc.scalar.activation(actH[:, 2 * g:2 * g + 2], ptmp[:, 2 * g:2 * g + 2], copy).then_inc(S["mix_hi"], 1)
        p = phases["pool_out"]
        for v in range(p["n"]):
            split(p["U"] + v + 2)
        ffn(0, 1, X_AFTER["pool_out"] - 4)
        ffn(1, 0, X_AFTER["down01"] - 4)

        act.wait_ge(S["lam_ready"], 1)
        nc.scalar.activation(small[:, 2:4], small[:, 0:2], ACT.Exp).then_inc(S["lam_exp"], 1)
        late_norm("diff_in", X_AFTER["down10"] - 4)
        p = phases["diff_in"]
        for j in range(14):
            split(p["U"] + j + 2)
            if j == 0:
                late_std("diff_in")
        attention(heads_of("diff") + heads_of("mem1"))
        act.wait_ge(S["tr_done"], ATT["mem1"] + 4)
        nc.scalar.activation(M[:, 0:2048], M[:, MX:MX + 2048], ACT.Square).then_inc(S["osq_ready"], 1)
        for q in range(4):
            act.wait_ge(S["oss_ready"], q + 1)
            nc.scalar.activation(M[:, MX + 2048 + 512 * q:MX + 2560 + 512 * q], P[q][:], ACT.Sqrt, bias=eps[:, 1:2],
                                 scale=1.0 / 128).then_inc(S["ostd_ready"], 1)
        for q in range(4):
            act.wait_ge(S["on_ready"], q + 1)
            nc.scalar.activation(actH[:, 2 * q:2 * q + 2], dQ[:, 2 * q:2 * q + 2], copy).then_inc(S["on_hi"], 1)
        p = phases["diff_out"]
        for v in range(p["n"]):
            split(p["U"] + v + 2)
        ffn(1, 1, X_AFTER["diff_out"] - 4)

        for q in range(4):
            act.wait_ge(S["x_ready"], X_AFTER["down11"] - 4 + q + 1)
            nc.scalar.activation(NT[:, 2 * q:2 * q + 2], xT[:, 2 * q:2 * q + 2], ACT.Square).then_inc(S["sq_ready"], 1)
        for q in range(4):
            for k in (2 * q, 2 * q + 1):
                last = nc.scalar.activation(NT2[:, k], xT[:, k], ACT.Square, scale=cols[:, G_FIN + k:G_FIN + k + 1])
            last.then_inc(S["sq_ready"], 1)
        late_std("final")
        act.wait_ge(S["m2_ready"], 1)
        nc.scalar.activation(rstd2, rstd2, ACT.Sqrt, bias=eps[:, 0:1], scale=1.0 / D).then_inc(S["std_ready"], 1)
        for q in range(4):
            act.wait_ge(S["hn_ready"], 4 * HN["in2"] + q + 1)
            nc.scalar.activation(hTh[:, 2 * q:2 * q + 2], NT[:, 2 * q:2 * q + 2], copy).then_inc(S["hh_ready"], 1)
        for name in ("in2", "in2x"):
            for j in range(phases[name]["n"]):
                split(phases[name]["U"] + j + 2)
        act.wait_ge(S["half_used"], phases["in2x"]["U"] + 2)
        nc.scalar.activation(relu2[:, 0, 0], P[4 + (phases["in2x"]["E"] + 1) % 2][:, 0:T], ACT.Square).then_inc(S["ik_sq"], 1)
        act.wait_ge(S["ik_ss"], 1)
        nc.scalar.activation(rstd[:], P[6][:, 0:T], ACT.Sqrt, bias=eps[:, 0:1], scale=1.0 / 128).then_inc(S["ik_std"], 1)
        for n in range(8):
            act.wait_ge(S["idx_products"], n + 1)
            if n >= 2:
                act.wait_ge(S["idx_summed"], n - 1)
            nc.scalar.activation(relu2[:, n % 2, 0], P[n % 2][:, 0:T], ACT.Relu).then_inc(S["idx_relu"], 1)
        attention(heads_of("heads"))
        p = phases["out2"]
        for v in range(p["n"]):
            split(p["U"] + v + 2)

        act.wait_ge(S["x_ready"], X_AFTER["out2"])
        act.dma_start(skin, a["peer_subkeys_2"][0].rearrange("h q n d -> n (h q) d")).then_inc(S["sk_landed"], 16)

        def peer_tiles():
            for n in range(4):
                act.wait_ge(S["xtok_tr"], n + 1)
                nc.scalar.activation(xtok[:, n // 2, (n % 2) * 512:(n % 2) * 512 + 512], P[n][:], copy).then_inc(S["xtok_ready"], 1)
            for q, b in enumerate((4, 5, 7, 0)):
                act.wait_ge(S["sk_tr"], q + 1)
                nc.scalar.activation(skT[:, 4 * q:4 * q + 4].rearrange("p a b -> p (a b)"), P[b][:], copy).then_inc(S["sk_ready"], 1)
        norm("wq", xT, "x_ready", X_AFTER["out2"] - 4, peer_tiles)
        for n, b in enumerate((1, 2, 3, 7)):
            act.wait_ge(S["htok_tr"], n + 1)
            nc.scalar.activation(htok[:, n // 2, (n % 2) * 512:(n % 2) * 512 + 512], P[b][:], copy).then_inc(S["htok_ready"], 1)
        p = phases["wq"]

        def scores_out(j):
            act.wait_ge(S["sk_scores"], j + 1)
            for t in range(2):
                last = nc.scalar.activation(sks[t][:, 2 * j:2 * j + 2].rearrange("p a b -> p (a b)"),
                                            P[j % 2][:, t * 256:t * 256 + 256], copy)
            last.then_inc(S["s_ready"], 1)
        for j in range(p["n"]):
            split(p["U"] + j + 2)
            if j >= 2:
                scores_out(j - 2)
        scores_out(6)
        scores_out(7)
        act.wait_ge(S["gdiff_ready"], 1)
        nc.scalar.activation(gate[:, 0], gate[:, 0], ACT.Exp).then_inc(S["gexp_ready"], 1)
        act.wait_ge(S["gdiff_ready"], 2)
        nc.scalar.activation(gate[:, 1], gate[:, 1], ACT.Exp).then_inc(S["gexp_ready"], 1)
        act.wait_ge(S["index_ready"], 2)
        for k in range(KT):
            last = nc.scalar.activation(diag[:, 0, k], ident[:], copy, scale=modc[:, 40 + k:41 + k])
        last.then_inc(S["g2_diag"], 1)
        act.wait_ge(S["g2_tr"], 1)
        for q in range(2):
            last = nc.scalar.activation(g2bc[:, q * 512:q * 512 + 512], P[4 + q][:], copy)
        last.then_inc(S["g2_ready"], 1)

        def experts(t, r, g, first=False):
            n = t * GROUPS + g
            act.wait_ge(S["dots_ready"], r * 2 + (n + 1))
            if not first:
                act.wait_ge(S["coef_ready"], r * 2 + (n - 1))
            nc.scalar.activation(gel8[:, g], dots[:, g], ACT.Gelu).then_inc(S["gelu_ready"], 1)
            act.wait_ge(S["coef_ready"], r * 2 + (n + 1))
            if not first:
                act.wait_ge(S["v_used"], r * 2 + (n - 1))
            for i in range(NG):
                last = nc.scalar.activation(diag[:, g, i], ident[:], copy, scale=coef8[:, g, i:i + 1])
            last.then_inc(S["diag_ready"], 1)
        for g in range(2):
            experts(0, 0, g, True)
        with act.Fori(1, GROUPS // 2) as r:
            for g in range(2):
                experts(0, r, g)
        with act.Fori(0, GROUPS // 2) as r:
            for g in range(2):
                experts(1, r, g)
        for t in range(2):
            act.wait_ge(S["xf_ready"], t + 1)
            nc.scalar.activation(tmpf, xtok[:, t], ACT.Square, accum_out=small[:, 44 + t:45 + t]).then_inc(S["fss_ready"], 1)
            act.wait_ge(S["fss_ready"], t + 1)
            nc.scalar.activation(small[:, 46 + t:47 + t], small[:, 44 + t:45 + t], ACT.Sqrt, bias=eps[:, 0:1], scale=1.0 / D)\
                .then_inc(S["fstd_ready"], 1)

    @block.vector
    def _(dve):
        chain = Chain(dve, S["dve_chain"])
        tt, ts, stt = nc.vector.tensor_tensor, nc.vector.tensor_scalar, nc.vector.scalar_tensor_tensor

        def split(U):
            if U >= len(half_of):
                return
            c, h = half_of[U]
            kind = chunks[c][0]
            dve.wait_ge(S["hi_ready"], U + 1)
            if kind == "group":
                tt(WL[:, U % 2, 0:1024], WR[:, c % 2, h * 1024:h * 1024 + 1024], WH[:, U % 2, 0:1024].bitcast(F32), ALU.subtract)\
                    .then_inc(S["lo_ready"], 1)
            else:
                tt(split_view(WL, U % 2, kind), raw(c % 2, kind, h), split_view(WH, U % 2, kind).bitcast(F32), ALU.subtract)\
                    .then_inc(S["lo_ready"], 1)

        def split_loop(U, r):
            c, h = half_of[U]
            dve.wait_ge(S["hi_ready"], r * 4 + (U + 1))
            tt(split_view(WL, U % 2, "pair"), raw(c % 2, "pair", h), split_view(WH, U % 2, "pair").bitcast(F32), ALU.subtract)\
                .then_inc(S["lo_ready"], 1)

        def norm(name, src, gain, shift=None, r=None):
            n, _, m = NORMS[name]
            dst, r = NT, rstd[:] if r is None else r
            dve.wait_ge(S["std_ready"], n + 1)
            chain(nc.vector.reciprocal(r, r))
            for k in range(KT):
                last = stt(dst[:, k], src[:, k], gain(k), r, ALU.mult, ALU.mult)
                if shift is None and k % 2:
                    last.then_inc(S["hn_ready"], 1)
            if shift is not None:
                chain(last)
                for k in range(KT):
                    last = ts(dst[:, k], dst[:, k], shift(k), None, ALU.add)
                    if k % 2:
                        last.then_inc(S["hn_ready"], 1)
            for q in range(4):
                dve.wait_ge(S["hh_ready"], 4 * m + q + 1)
                tt(hTl[:, 2 * q:2 * q + 2], NT[:, 2 * q:2 * q + 2], hTh[:, 2 * q:2 * q + 2].bitcast(F32), ALU.subtract)\
                    .then_inc(S["hl_ready"], 1)

        def col(at):
            return lambda k: cols[:, at + k:at + k + 1]

        def late_lo(name, q):
            _, gain, m = NORMS[name]
            dve.wait_ge(S["hh_ready"], 4 * m + q + 1)
            for k in (2 * q, 2 * q + 1):
                last = stt(hTl[:, k], xT[:, k], cols[:, gain + k:gain + k + 1], hTh[:, k].bitcast(F32), ALU.mult, ALU.subtract)
            last.then_inc(S["hl_ready"], 1)

        def late_rstd(name):
            dve.wait_ge(S["std_ready"], NORMS[name][0] + 1)
            nc.vector.reciprocal(rstd[:], rstd[:]).then_inc(S["rstd_made"], 1)
            dve.wait_ge(S["rstd_made"], NORMS[name][2])

        def post_scaled(U, E, dst):
            dve.wait_ge(S["half_used"], U + 1)
            tt(dst, P[4 + E % 2][:].rearrange("p (a b) -> p a b", a=2), rstd[:].unsqueeze(1).broadcast_to([128, 2, T]), ALU.mult)\
                .then_inc(S["bank_free"], 1)

        def post_values(U, E, dst):
            dve.wait_ge(S["half_used"], U + 1)
            for t in range(2):
                last = ts(dst[:, t], P[4 + E % 2][:, t * 256:t * 256 + 256], rcol[:, t:t + 1], None, ALU.mult)
            last.then_inc(S["bank_free"], 1)

        def post_copy(U, E, dst):
            dve.wait_ge(S["half_used"], U + 1)
            nc.vector.tensor_copy(dst, P[4 + E % 2][:].rearrange("p (a b) -> p a b", a=2)).then_inc(S["bank_free"], 1)

        def ada(name, h):
            i = ADA.get((name, h))
            if i is not None:
                dve.wait_ge(S["ada_done"], i + 1)
                tt(modc[:, 4 * i:4 * i + 4], P[7][:, 0:4], badac[:, 4 * i:4 * i + 4], ALU.add).then_inc(S["mod_ready"], 1)

        def add_update(U, gain, after=None):
            dve.wait_ge(S["half_used"], U)
            for q in range(4):
                if callable(gain):
                    for k in range(2):
                        last = stt(xT[:, 2 * q + k], P[q][:, k * T:k * T + T], gain(2 * q + k), xT[:, 2 * q + k], ALU.mult, ALU.add)
                else:
                    x = xT[:, 2 * q:2 * q + 2].rearrange("p a b -> p (a b)")
                    last = stt(x, P[q][:], gain, x, ALU.mult, ALU.add)
                last.then_inc(S["x_ready"], 1)
                if after and q:
                    late_lo(after, q - 1)
            if after:
                late_lo(after, 3)

        def ffn(i, f, after=None):
            p = phases[f"up{i}{f}"]
            U, E, s0 = p["U"], p["E"], FT * (2 * i + f)

            def normalised(u, e, s, j):
                dve.wait_ge(S["half_used"], u + 1)
                if j >= 2:
                    dve.wait_ge(S["sil_ready"], s - 1)
                    dve.wait_ge(S["prod_ready"], s - 1)
                tt(GUP[:, j % 2], P[4 + (E + j) % 2][:].rearrange("p (a b) -> p a b", a=2),
                   rstd[:].unsqueeze(1).broadcast_to([128, 2, T]), ALU.mult).then_inc(S["bank_free"], 1)

            def product(e, s, j):
                dve.wait_ge(S["bank_free"], e + 1)
                dve.wait_ge(S["sil_ready"], s + 1)
                if j:
                    dve.wait_ge(S["act_lo"], s)
                tt(PRD[:, j % 2], SIL[:, j % 2], GUP[:, j % 2, 1], ALU.mult).then_inc(S["prod_ready"], 1)

            def lo_act(s, j, lo, hitile):
                dve.wait_ge(S["act_hi"], s + 1)
                tt(lo, PRD[:, j % 2], hitile.bitcast(F32), ALU.subtract).then_inc(S["act_lo"], 1)

            def step(j):
                if j == 0:
                    split(U + 2)
                    late_rstd(f"up{i}{f}")
                normalised(U + j, E + j, s0 + j, j)
                if j >= 2:
                    lo_act(s0 + j - 2, j - 2, actL[:, j - 2], actH[:, j - 2])
                if j:
                    product(E + j - 1, s0 + j - 1, j - 1)
                    split(U + j + 2)
            step(0)
            step(1)
            with dve.Fori(0, 4) as r:
                for j in range(2, 6):
                    normalised(r * 4 + (U + j), r * 4 + (E + j), r * 4 + (s0 + j), j)
                    one = [b[:, bass.ds(r * 4 + (j - 2), 1), :].rearrange("p a t -> p (a t)") for b in (actL, actH)]
                    lo_act(r * 4 + (s0 + j - 2), j - 2, one[0], one[1])
                    product(r * 4 + (E + j - 1), r * 4 + (s0 + j - 1), j - 1)
                    split_loop(U + j + 2, r)
            for j in range(18, 22):
                step(j)
            lo_act(s0 + 20, 20, actL[:, 20], actH[:, 20])
            product(E + 21, s0 + 21, 21)
            lo_act(s0 + 21, 21, actL[:, 21], actH[:, 21])
            p = phases[f"down{i}{f}"]
            for v in range(p["n"]):
                split(p["U"] + v + 2)
                ada(f"down{i}{f}", v)
            add_update(p["U"] + p["n"], 0.5, after)

        def mix_lo(g):
            dve.wait_ge(S["mix_hi"], g + 1)
            tt(actL[:, 2 * g:2 * g + 2], ptmp[:, 2 * g:2 * g + 2], actH[:, 2 * g:2 * g + 2].bitcast(F32), ALU.subtract)\
                .then_inc(S["mix_lo"], 1)

        def subkeys(t, j):
            hs = range(2 * j[0], 2 * j[-1] + 2)
            sk = sks[t]
            dve.wait_ge(S["s_ready"], j[-1] + 1)
            for h in hs:
                last = nc.vector.max(v16[:, h, 0:8], sk[:, h])
            chain(last)
            for h in hs:
                nc.vector.max_index(i16[:, h, 0:8], v16[:, h, 0:8], sk[:, h])
            for h in hs:
                last = nc.vector.match_replace(skw[:, h], v16[:, h, 0:8], sk[:, h], TAKEN)
            chain(last)
            for h in hs:
                last = nc.vector.max(v16[:, h, 8:16], skw[:, h])
            chain(last)
            for h in hs:
                last = nc.vector.max_index(i16[:, h, 8:16], v16[:, h, 8:16], skw[:, h])
            chain(last)

        def choose(t):
            if t == 0:
                dve.wait_ge(S["iota_ready"], 1)
            nc.vector.tensor_copy(i16f, i16)
            v = v16.rearrange("p (h q) i -> p h q i", q=2)
            wide = [128, 8, 16, 16]
            chain(tt(cand, v[:, :, 0].unsqueeze(3).broadcast_to(wide), v[:, :, 1].unsqueeze(2).broadcast_to(wide), ALU.add))
            flat = cand.rearrange("p h i j -> p h (i j)")
            for h in range(8):
                last = nc.vector.max(gs[:, h, 0:8], flat[:, h])
            chain(last)
            for h in range(8):
                nc.vector.max_index(pos[:, h, 0:8], gs[:, h, 0:8], flat[:, h])
            for h in range(8):
                last = nc.vector.match_replace(candw[:, h], gs[:, h, 0:8], flat[:, h], TAKEN)
            chain(last)
            for h in range(8):
                last = nc.vector.max(gs[:, h, 8:16], candw[:, h])
            chain(last)
            tt(gate[:, t], gs, gs[:, :, 0:1].broadcast_to([128, 8, 16]), ALU.subtract).then_inc(S["gdiff_ready"], 1)
            for h in range(8):
                last = nc.vector.max_index(pos[:, h, 8:16], gs[:, h, 8:16], candw[:, h])
            chain(last)
            p = pos.rearrange("p h k -> p (h k)")
            pd = posd.bitcast(U32)
            ts(pd[:, 0], p, 4, None, ALU.logical_shift_right)
            chain(ts(pd[:, 1], p, 15, None, ALU.bitwise_and))
            chain(nc.vector.tensor_copy(posf, pd))
            ix = i16f.rearrange("p (h q) i -> p h q i", q=2)
            for q in range(2):
                pf = posf[:, q].rearrange("p (h k) -> p h k", h=8)
                chain(tt(hot, pf.unsqueeze(3).broadcast_to(wide), iota16.unsqueeze(1).unsqueeze(1).broadcast_to(wide), ALU.is_equal))
                chain(tt(hot, hot, ix[:, :, q].unsqueeze(2).broadcast_to(wide), ALU.mult))
                chain(nc.vector.tensor_reduce(psel[:, q].rearrange("p (h k) -> p h k", h=8), hot, AX.X, ALU.add))
            stt(eidx[:, t * 128:t * 128 + 128], psel[:, 0], float(128), psel[:, 1], ALU.mult, ALU.add).then_inc(S["index_ready"], 1)
            dve.wait_ge(S["gexp_ready"], t + 1)
            gsum = small[:, 8:16]
            chain(nc.vector.tensor_reduce(gsum, gate[:, t], AX.X, ALU.add))
            chain(nc.vector.reciprocal(gsum, gsum))
            chain(tt(gate[:, t], gate[:, t], gsum.unsqueeze(2).broadcast_to([128, 8, 16]), ALU.mult))

        def attention(units):
            def logits(x):
                a, b, n = x["a"], 4 * (x["a"] % 2), len(x["qk"])
                dve.wait_ge(S["score_done"], a + 1)
                if a >= 2:
                    dve.wait_ge(S["tr_done"], a - 1)
                if x["bias"] is not None:
                    dve.wait_ge(*x["bias_sem"])
                for c in range(n):
                    o = LB[:, a % 2, 2 * c:2 * c + 2]
                    i = P[b + c][:].rearrange("p (a b) -> p a b", a=2)
                    if x["bias"] is None:
                        last = ts(o, i, x["scale"], None, ALU.mult)
                    else:
                        last = stt(o, i, x["scale"], x["bias"], ALU.mult, ALU.add)
                last.then_inc(S["logits_ready"], 1)
                dve.wait_ge(S["logits_ready"], a + 1)
                nc.vector.tensor_reduce(st[:, rb(a):rb(a) + 2 * n], LB[:, a % 2, 0:2 * n], AX.X, ALU.max, negate=True)\
                    .then_inc(S["neg_max"], 1)

            def rsums(x):
                a, n = x["a"], 2 * len(x["qk"])
                dve.wait_ge(S["exp_done"], a + 1)
                if n == 4:
                    chain(nc.vector.reciprocal(st[:, rb(a) + 8:rb(a) + 8 + n], st[:, rb(a) + 4:rb(a) + 4 + n]))
                    ts(st[:, rb(a) + 10:rb(a) + 12], st[:, rb(a) + 10:rb(a) + 12], small[:, 5:6], None, ALU.mult)\
                        .then_inc(S["rsum_ready"], 1)
                else:
                    nc.vector.reciprocal(st[:, rb(a) + 8:rb(a) + 8 + n], st[:, rb(a) + 4:rb(a) + 4 + n]).then_inc(S["rsum_ready"], 1)

            def diffs(x):
                a = x["a"]
                dve.wait_ge(S["prob_ready"], a + 1)
                for t in range(2):
                    last = stt(LB[:, a % 2, t], LB[:, a % 2, 2 + t], rinv(a, 2 + t), LB[:, a % 2, t], ALU.mult, ALU.add)
                last.then_inc(S["diffp_ready"], 1)

            def result(x):
                a, (r0, r1) = x["a"], x["rows"]
                if not x["split"]:
                    dve.wait_ge(S["o_done"], a + 1)
                    nc.vector.tensor_copy(dQ[:, x["head"]], P[6 + a % 2][:, 0:T]).then_inc(S["o_ready"], 1)
                    return
                ohi = a + 1 - (8 if a >= ATT["mem1"] else 0)
                dve.wait_ge(S["o_hi"], ohi)
                tt(actL[r0:r1, x["tile"]], P[6 + a % 2][r0:r1, 0:T], actH[r0:r1, x["tile"]].bitcast(F32), ALU.subtract)\
                    .then_inc(S["o_ready"], 1)

            logits(units[0])
            for i in range(len(units) + 1):
                if i + 1 < len(units):
                    logits(units[i + 1])
                if i < len(units):
                    rsums(units[i])
                    if len(units[i]["qk"]) == 2:
                        diffs(units[i])
                if i >= 1:
                    result(units[i - 1])

        for q in range(4):
            dve.wait_ge(S["x_tr"], q + 1)
            nc.vector.tensor_copy(xT[:, 2 * q:2 * q + 2].rearrange("p a b -> p (a b)"), P[q][:]).then_inc(S["x_ready"], 1)
        dve.wait_ge(S["cols_tr"], 1)
        nc.vector.tensor_copy(badac[:], P[0][:, 128:176])
        nc.vector.tensor_copy(cols[:, 0:97], P[0][:, 0:97]).then_inc(S["cols_ready"], 1)
        dve.wait_ge(S["cols_ready"], 1)
        split(0)
        split(1)
        norm("mem", memT, col(G_MEM))
        for l in range(2):
            p = phases[f"kv{l}"]
            for j in range(4):
                split(p["U"] + j + 2)
                dst = memK[:, l, 2 * j:2 * j + 2] if j < 2 else memV[:, l, :, (j - 2) * 256:(j - 2) * 256 + 256]
                post_copy(p["U"] + j, p["E"] + j, dst)
        for q in range(4):
            late_lo("up00", q)
        ffn(0, 0, "pool_in")

        p = phases["pool_in"]
        dve.wait_ge(S["pad_ready"], 1)
        for j in range(6):
            split(p["U"] + j + 2)
            dst = uT[:, 2 * j:2 * j + 2, 16:] if j < 4 else xq0[:, 2 * (j - 4):2 * (j - 4) + 2]
            if j == 0:
                late_rstd("pool_in")
            post_scaled(p["U"] + j, p["E"] + j, dst)
        for g in range(4):
            last = nc.vector.tensor_scalar_min(inv[:, g], inv[:, g], float(2 << g))
        chain(last)
        dve.wait_ge(S["bank_free"], p["E"] + 6)
        chain(nc.vector.reciprocal(inv[:], inv[:]))
        for g in range(4):
            src, w = uT[:, 2 * g:2 * g + 2], 1
            for s in range(g + 1):
                dst = wa if s % 2 == 0 else wb
                chain(tt(dst[:, :, 16:], src[:, :, 16:], src[:, :, 16 - w:PADW - w], ALU.add))
                src, w = dst, 2 * w
            iv = inv[:, g].unsqueeze(1).broadcast_to([128, 2, T])
            pg = ptmp[:, 2 * g:2 * g + 2]
            chain(tt(pg, src[:, :, 16:], iv, ALU.mult))
            tt(pg, pg, uT[:, 2 * g:2 * g + 2, 16:], ALU.subtract).then_inc(S["pooled_ready"], 1)
        for g in range(4):
            dve.wait_ge(S["pool_hi"], g + 1)
            tt(hTl[:, 2 * g:2 * g + 2], ptmp[:, 2 * g:2 * g + 2], hTh[:, 2 * g:2 * g + 2].bitcast(F32), ALU.subtract)\
                .then_inc(S["pool_lo"], 1)
        attention(heads_of("mem0"))
        p = phases["group"]
        for g in range(4):
            if g % 2:
                split(p["U"] + g // 2 + 2)
                dve.wait_ge(S["half_used"], p["U"] + g // 2 + 1)
            else:
                dve.wait_ge(S["group_done"], g // 2 + 1)
            for b in range(2):
                k = 2 * g + b
                last = ts(ptmp[:, k], P[4 + (p["E"] + g) % 2][:, b * T:b * T + T], cols[:, G_POOL + k:G_POOL + k + 1], None, ALU.mult)
            last.then_inc(S["bank_free"], 1)
            if g:
                mix_lo(g - 1)
        mix_lo(3)
        p = phases["pool_out"]
        for v in range(p["n"]):
            split(p["U"] + v + 2)
        add_update(p["U"] + p["n"], 1.0, "up01")
        ffn(0, 1, "up10")
        dve.wait_ge(S["lam_landed"], 16)
        lw = lamw.rearrange("p (a b) n -> p a b n", a=2)
        chain(tt(lamp, lw[:, :, 0], lw[:, :, 1], ALU.mult))
        nc.vector.tensor_reduce(small[:, 0:2], lamp, AX.X, ALU.add).then_inc(S["lam_ready"], 1)
        ffn(1, 0, "diff_in")
        dve.wait_ge(S["lam_exp"], 1)
        chain(tt(small[:, 4:5], small[:, 3:4], small[:, 2:3], ALU.subtract))
        chain(ts(small[:, 5:6], small[:, 4:5], -LAM_INIT, None, ALU.add))
        chain(ts(cols[:, 97:98], cols[:, G_DIFF:G_DIFF + 1], 1.0 - LAM_INIT, None, ALU.mult))

        p = phases["diff_in"]
        for j in range(14):
            split(p["U"] + j + 2)
            if j < 8:
                dst = (dQ if j < 4 else dK)[:, 2 * (j % 4):2 * (j % 4) + 2]
            elif j < 12:
                dst = dV[:, :, (j - 8) * 256:(j - 8) * 256 + 256]
            else:
                dst = xq1[:, 2 * (j - 12):2 * (j - 12) + 2]
            if j == 0:
                late_rstd("diff_in")
            if j == 4:
                dve.wait_ge(S["rcol_tr"], 1)
                for t in range(2):
                    last = nc.vector.tensor_copy(rcol[:, t:t + 1], P[7][:, t * 128:t * 128 + 1])
                last.then_inc(S["rcol_ready"], 1)
                dve.wait_ge(S["rcol_ready"], 1)
            (post_values if 8 <= j < 12 else post_scaled)(p["U"] + j, p["E"] + j, dst)
            ada("diff_in", j)
        attention(heads_of("diff") + heads_of("mem1"))
        for q in range(4):
            r = M[:, MX + 2048 + 512 * q:MX + 2560 + 512 * q]
            dve.wait_ge(S["ostd_ready"], q + 1)
            chain(nc.vector.reciprocal(r, r))
            o = M[:, MX + 512 * q:MX + 512 * q + 512]
            stt(o, o, cols[:, 97:98], r, ALU.mult, ALU.mult).then_inc(S["on_ready"], 1)
        for q in range(4):
            dve.wait_ge(S["on_hi"], q + 1)
            tt(actL[:, 2 * q:2 * q + 2], dQ[:, 2 * q:2 * q + 2], actH[:, 2 * q:2 * q + 2].bitcast(F32), ALU.subtract)\
                .then_inc(S["on_lo"], 1)
        p = phases["diff_out"]
        for v in range(p["n"]):
            split(p["U"] + v + 2)
        add_update(p["U"] + p["n"], 1.0, "up11")
        ffn(1, 1)
        dve.wait_ge(S["std_ready"], NORMS["final"][0] + 1)
        chain(nc.vector.reciprocal(rstd[:], rstd[:]))
        dve.wait_ge(S["ss_ready"], NORMS["in2"][0] + 1)
        chain(tt(rstd2, P[7][:, 0:T], rstd[:], ALU.mult))
        tt(rstd2, rstd2, rstd[:], ALU.mult).then_inc(S["m2_ready"], 1)
        for k in range(KT):
            last = stt(xT[:, k], xT[:, k], cols[:, G_FIN + k:G_FIN + k + 1], rstd[:], ALU.mult, ALU.mult)
            if k % 2:
                last.then_inc(S["x_ready"], 1)

        dve.wait_ge(S["mod_ready"], 12)
        for j, (g, s) in enumerate(((G_ATT, 8), (G_FFN, 32))):
            last = stt(gmod[:, 8 * j:8 * j + 8], modc[:, s:s + 8], 1.0, cols[:, g:g + 8], ALU.add, ALU.mult)
        chain(last)
        norm("in2", xT, lambda k: gmod[:, k:k + 1], lambda k: modc[:, k:k + 1], rstd2)
        p = phases["in2"]
        for j in range(12):
            split(p["U"] + j + 2)
            jj, half = j % 6, j // 6
            if jj < 2:
                dst = hQ[:, 4 * half + 2 * jj:4 * half + 2 * jj + 2]
            elif jj < 4:
                dst = hK[:, 4 * half + 2 * (jj - 2):4 * half + 2 * (jj - 2) + 2]
            else:
                dst = hV[:, :, half * 512 + (jj - 4) * 256:half * 512 + (jj - 4) * 256 + 256]
            post_copy(p["U"] + j, p["E"] + j, dst)
        p = phases["in2x"]
        split(p["U"] + 2)
        post_copy(p["U"], p["E"], iQ)
        split(p["U"] + 3)
        dve.wait_ge(S["ik_std"], 1)
        b = P[4 + (p["E"] + 1) % 2]
        chain(ts(iw, b[:, T:T + 8].rearrange("p (a b) -> p a b", a=2), 0.5, None, ALU.mult))
        chain(nc.vector.reciprocal(rstd[:], rstd[:]))
        tt(iK, b[:, 0:T], rstd[:], ALU.mult).then_inc(S["bank_free"], 1)
        for t in range(2):
            for h in range(4):
                n = 4 * t + h
                dve.wait_ge(S["idx_relu"], n + 1)
                w, r = iw[:, t, h:h + 1], relu2[:, n % 2, 0]
                if h:
                    dve.wait_ge(S["idx_summed"], n)
                    last = stt(score[:, t], r, w, score[:, t], ALU.mult, ALU.add)
                else:
                    last = ts(score[:, t], r, w, None, ALU.mult)
                last.then_inc(S["idx_summed"], 1)
        dve.wait_ge(S["masked_ready"], 1)
        for i in range(TOPK // 8):
            for t in range(2):
                last = nc.vector.max(small[:, 16 + 8 * t:24 + 8 * t], score[:, t] if i == 0 else work[:, t])
            chain(last)
            for t in range(2):
                last = nc.vector.match_replace(work[:, t], small[:, 16 + 8 * t:24 + 8 * t], score[:, t] if i == 0 else work[:, t],
                                               TAKEN)
            chain(last)
        for t in range(2):
            ts(pen[:, t], work[:, t], TAKEN / 2, NEG, ALU.is_gt, ALU.mult).then_inc(S["pen_ready"], 1)
        dve.wait_ge(S["pen_ready"], 2)
        attention(heads_of("heads"))
        p = phases["out2"]
        for v in range(p["n"]):
            split(p["U"] + v + 2)
        add_update(p["U"] + p["n"], lambda k: modc[:, 16 + k:17 + k])

        norm("wq", xT, lambda k: gmod[:, 8 + k:9 + k], lambda k: modc[:, 24 + k:25 + k])
        p = phases["wq"]
        for j in range(p["n"]):
            split(p["U"] + j + 2)
            if j >= 4:
                dve.wait_ge(S["sk_scores"], j - 3)
            post_copy(p["U"] + j, p["E"] + j, pQ[:, j % 4])
            if j >= 3:
                subkeys(0, [j - 3])
        for j in (5, 6, 7):
            subkeys(0, [j])
        choose(0)
        subkeys(1, range(8))
        choose(1)

        def experts(t, r, g, first=False):
            n = t * GROUPS + g
            dve.wait_ge(u_landed[g], r * (16 * NG) + (t * GROUPS // 2 + 1) * 16 * NG)
            if not first:
                dve.wait_ge(S["gelu_ready"], r * 2 + (n - 1))
            for i in range(NG):
                last = nc.vector.tensor_tensor_reduce(out=GU[:, g, i], in0=GU[:, g, i], in1=htok[:, t], scale=1.0, scalar=0.0,
                                                      op0=ALU.mult, op1=ALU.add, accum_out=dots[:, g, i:i + 1])
            last.then_inc(S["dots_ready"], 1)
            dve.wait_ge(S["gelu_ready"], r * 2 + (n + 1))
            if not first:
                dve.wait_ge(S["diag_ready"], r * 2 + (n - 1))
            if isinstance(r, int):
                gt = gatec[:, (2 * r + n) * NG:(2 * r + n + 1) * NG]
            else:
                gt = gatec[:, bass.ds(r * (2 * NG) + n * NG, NG)]
            tt(coef8[:, g], gel8[:, g], gt, ALU.mult).then_inc(S["coef_ready"], 1)
        for g in range(2):
            experts(0, 0, g, True)
        with dve.Fori(1, GROUPS // 2) as r:
            for g in range(2):
                experts(0, r, g)
        with dve.Fori(0, GROUPS // 2) as r:
            for g in range(2):
                experts(1, r, g)
        dve.wait_ge(S["g2_ready"], 1)
        dve.wait_ge(S["gfin_landed"], 16)
        for t in range(2):
            dve.wait_ge(S["acc_done"], t + 1)
            if t:
                dve.wait_ge(S["fss_ready"], 1)
            for q in range(2):
                last = tt(tmpf[:, q * 512:q * 512 + 512], P[2 * t + q][:], g2bc[:, q * 512:q * 512 + 512], ALU.mult)
            chain(last)
            tt(xtok[:, t], xtok[:, t], tmpf, ALU.add).then_inc(S["xf_ready"], 1)
        for t in range(2):
            dve.wait_ge(S["fstd_ready"], t + 1)
            chain(nc.vector.reciprocal(small[:, 48 + t:49 + t], small[:, 46 + t:47 + t]))
            stt(xtok[:, t], xtok[:, t], small[:, 48 + t:49 + t], gfin, ALU.mult, ALU.mult).then_inc(S["y_ready"], 1)


INPUTS = ["x", "mem", "norm_g", "ffn_w_up", "ffn_w_down", "mem_norm_g", "mem_w_kv", "pool_w_in", "pool_w_group", "pool_scale",
          "pool_w_out", "diff_w_in", "diff_lambda", "diff_norm_g", "diff_w_out", "final_norm_g", "c_2", "w_ada_2", "b_ada_2",
          "norm_attn_2", "norm_ffn_2", "w_in_2", "w_out_2", "rel_bias_2", "peer_wq_2", "peer_subkeys_2", "peer_u_2",
          "peer_v_2", "norm_final_2"]


def kernel(**inputs):
    import numpy as np
    import concourse.bacc as bacc
    from concourse.bass_utils import run_bass_kernel_spmd as run

    nc = bacc.Bacc("TRN2", target_bir_lowering=False, num_devices=1)
    arrays, aps = {}, {}
    for name in INPUTS:
        v = np.ascontiguousarray(inputs[name])
        arrays["in_" + name] = v
        aps[name] = nc.dram_tensor("in_" + name, v.shape, mybir.dt.from_np(v.dtype), kind="ExternalInput").ap()
    out = nc.dram_tensor("out_0", (1, T, D), F32, kind="ExternalOutput").ap()
    program(nc, aps, out)
    r = run(nc, [arrays], core_ids=[0])
    return r.results[0]["out_0"]
```

```python
import math

import concourse.bass as bass
from concourse import mybir
from contextlib import ExitStack

F32 = mybir.dt.float32
F32R = mybir.dt.float32r
I32 = mybir.dt.int32
U32 = mybir.dt.uint32
ALU = mybir.AluOpType
ACT = mybir.ActivationFunctionType
AX = mybir.AxisListType

D = 1024
T = 256
KT = D // 128
FF = 2816
FT = FF // 128
NEG = -1.0e30
TAKEN = -3.0e38
BUCKET_START = [*range(16), 23, 32, 46, 64, 91, 128, 182]
TOPK = min(256, T // 4)
NG = 8
GROUPS = 128 // NG


def bucket_ranges():
    starts = [*range(16), 16, 23, 32, 46, 64, 91, 128, 182]
    return [(b, s, (starts[b + 1] if b + 1 < len(starts) else T)) for b, s in enumerate(starts)]


def program(nc, a, out):
    ctx = ExitStack()
    stage_a = ExitStack()

    def sb(name, shape, dt=F32, where=None):
        return (where or ctx).enter_context(nc.sbuf_tensor(name, shape, dt))

    def sem(name):
        return ctx.enter_context(nc.semaphore(name))

    xT = sb("xT", [128, KT, T])
    ident = sb("ident", [128, 128])
    ones = sb("ones", [128, 128])
    cols = sb("cols", [128, 104])
    modc = sb("modc", [128, 48])
    badac = sb("badac", [128, 48])
    silc = sb("silc", [128, KT])
    eps = sb("eps", [128, 4])
    gmod = sb("gmod", [128, 2 * KT])
    rstd = sb("rstd", [128, T])
    small = sb("small", [128, 64])
    lam = sb("lam", [128, 384])
    st = sb("st", [128, 32])
    M = sb("M", [128, 3072 + 8704])
    WR = sb("WR", [128, 2, 4096], F32, stage_a)
    WH = sb("WH", [128, 2, 2048], F32R, stage_a)
    WL = sb("WL", [128, 2, 2048], F32R, stage_a)
    hTh = sb("hTh", [128, KT, T], F32R, stage_a)
    hTl = sb("hTl", [128, KT, T], F32R, stage_a)
    actH = sb("actH", [128, FT, T], F32R, stage_a)
    actL = sb("actL", [128, FT, T], F32R, stage_a)
    adaW = sb("adaW", [128, KT, 128], F32, stage_a)
    adaS = sb("adaS", [128, 2, 512], F32, stage_a)
    memK = sb("memK", [128, 2, 4, T], F32, stage_a)
    memV = sb("memV", [128, 2, 2, 512], F32, stage_a)
    stage_a.close()
    GU = sb("GU", [128, 2, NG, D])
    GV = sb("GV", [128, 2, NG, D])
    xtok = sb("xtok", [128, 2, D])
    htok = sb("htok", [128, 2, D])
    P = [ctx.enter_context(nc.psum_tensor(f"P{i}", [128, 512], F32)) for i in range(8)]
    rel_rows = nc.dram_tensor("rel_rows", (16, 128 * 512), F32, kind="Internal").ap()

    def view(at, *shape):
        n = math.prod(shape)
        v = M[:, at:at + n]
        if len(shape) == 1:
            return v
        names = "abcd"[:len(shape)]
        return v.rearrange(f"p ({' '.join(names)}) -> p {' '.join(names)}",
                           **dict(zip(names[1:], shape[1:])))

    NT = view(0, KT, T)
    LB = view(0, 2, 4, T)
    GUP = view(0, 2, 2, T)
    SIL = view(2048, 2, T)
    PRD = view(2560, 2, T)
    PTS = view(2048, 2, 2, T)
    MX = 3072
    xin, memin, memT = view(MX, 2, D), view(MX + 2048, 2, D), view(MX + 4096, KT, T)
    rows1 = view(MX + 6144, 128)
    rows2 = view(MX + 6272, 128)
    relr = view(MX + 6400, 512)
    relz = view(MX + 6912, 512)
    reltab = view(MX + 7424, 32)
    PADW = T + 16
    uT = view(MX, KT, PADW)
    wa = view(MX + 2176, 2, PADW)
    wb = view(MX + 2720, 2, PADW)
    inv = view(MX + 3264, 4, T)
    xq0 = view(MX + 4288, 4, T)
    ptmp = view(MX + 5312, KT, T)
    dQ, dK, dV = view(MX, 8, T), view(MX + 2048, 8, T), view(MX + 4096, 2, D)
    xq1 = view(MX + 6144, 4, T)
    dist = view(MX + 7168, 2, T)
    bias1 = view(MX + 7680, 2, 2, T)
    lamw = lam[:, 0:256].rearrange("p (a b) -> p a b", a=4)
    lamp = lam[:, 256:384].rearrange("p (a b) -> p a b", a=2)
    hQ, hK, hV = view(MX, 8, T), view(MX + 2048, 8, T), view(MX + 4096, 2, 1024)
    iQ, iK = view(MX + 6144, 2, T), view(MX + 6656, T)
    pen = view(MX + 6912, 2, T)
    bias2 = view(MX + 7424, 2, 2, T)
    iw = small[:, 32:40].rearrange("p (a b) -> p a b", a=2)
    score, work, relu2 = memK[:, 0, 0:2], memK[:, 0, 2:4], memK[:, 1]
    NT2, rstd2 = view(MX, KT, T), view(MX + 2048, T)
    rcol = small[:, 40:42]
    ikraw = memV[:, 0, 0]
    sks = [view(0, 16, 128), view(MX + 2048, 16, 128)]
    v16, i16, i16f = (view(at, 16, 16) for at in (2048, 2304, 2560))
    i16 = i16.bitcast(U32)
    gs, pos = view(2816, 8, 16), view(2944, 8, 16).bitcast(U32)
    pQ = view(MX, 4, 2, T)
    cand = view(0, 8, 16, 16)
    diag = view(MX, 2, NG, 128)
    tmpf = view(MX + 2048, D)
    skT = view(MX + 4096, 16, 128)
    posd, posf, psel = (lam[:, at:at + 96].rearrange("p (a n) -> p a n", a=2) for at in (0, 96, 192))
    iota16 = lam[:, 288:304]
    zro = view(MX + 5120, 128)
    dots, gel8, coef8 = (view(MX + at, 2, NG) for at in (5248, 5264, 5280))
    idxu, idxv = (lam[:, at:at + 2 * NG].rearrange("p (a n) -> p a n", a=2).bitcast(I32) for at in (304, 304 + 2 * NG))
    g2d = view(0, KT, 128)
    CALLS = [[range(0, 1), range(1, 4), range(4, 7), range(7, 8)],
             [range(0, 2), range(2, 5), range(5, 8)]]
    ALL_CALLS = [(t, hs) for t in range(2) for hs in CALLS[t]]
    CALL_AFTER = {1: 2, 2: 3, 7: 4, 8: 5, 9: 6}
    PEELED = 12
    skin = view(MX + 6144, 16, 128)
    skw = view(MX + 6144, 16, 128)
    candw = view(MX + 6144, 8, 256)
    hot = view(MX + 6144, 8, 16, 16)
    gfin, g2bc = view(MX + 6144, D), view(MX + 7168, D)
    eidx = view(MX + 8192, 256).bitcast(I32)
    gate = view(MX + 8448, 2, 8, 16)
    gatec = view(MX + 8448, 256)

    G_NORM, G_MEM, G_POOL, G_ATT, G_FFN, G_C, G_FIN, G_DIFF = 0, 48, 56, 64, 72, 80, 88, 96

    names = """x_landed mem_landed rows_landed rel_landed rel_stored iden_ready const_ready x_tr mem_tr mem_in
        cols_tr cols_ready silc_ready hi_ready lo_ready half_used bank_free sq_ready ss_ready std_ready
        hn_ready hh_ready hl_ready sil_ready act_hi act_lo x_ready dve_chain pool_chain ada_landed ada_sum
        ada_done mod_ready lam_landed lam_ready lam_exp pad_ready pooled_ready pool_hi pool_lo group_done
        mix_hi mix_lo score_done logits_ready neg_max exp_done rsum_ready prob_ready diffp_ready tr_done
        pt_ready o_done o_hi o_ready bias_ready osq_ready oss_ready ostd_ready on_ready on_hi on_lo ik_sq
        ik_ss ik_std ik_ready idx_products idx_relu idx_summed masked_ready iota_ready pen_ready sk_landed
        sk_tr sk_ready htok_tr htok_ready xtok_tr xtok_ready sk_scores s_ready gdiff_ready gexp_ready
        index_ready dots_ready gelu_ready coef_ready diag_ready v_used iu_ready iv_ready g2_diag g2_tr
        g2_ready gfin_landed acc_done update_done sqs_ready rstd_made prod_ready rcol_tr rcol_ready m2_ready
        xf_ready fss_ready fstd_ready y_ready stored zero_ready""".split()
    S = {n: sem(n) for n in names}
    raw_landed = [sem("raw_landed0"), sem("raw_landed1")]
    u_landed = [sem("u_landed0"), sem("u_landed1")]
    v_landed = [sem("v_landed0"), sem("v_landed1")]
    b_landed = [sem("b_landed0"), sem("b_landed1")]

    def kview(w):
        return w.rearrange("(k p) n -> p k n", p=128)

    chunks = []

    def raw(slot, kind, h):
        r = WR[:, slot, :]
        if kind == "cols":
            return r.rearrange("p (k n) -> p k n", k=KT)[:, :, h * 256:h * 256 + 256]
        if kind == "pair":
            return r.rearrange("p (k g j n) -> p k g j n", k=KT, g=2, j=2)[:, :, :, h, :]
        return r[:, h * 2048:h * 2048 + 2048]

    def raw_dst(slot, kind, part):
        r = WR[:, slot, :]
        if kind in ("cols", "pair"):
            return r.rearrange("p (k n) -> p k n", k=KT)[:, :, part * 256:part * 256 + 256]
        return r[:, part * 2048:part * 2048 + 2048].rearrange("p (k n) -> p k n", k=2)

    def split_view(buf, u, kind):
        b = buf[:, u, :]
        if kind == "cols":
            return b.rearrange("p (k n) -> p k n", k=KT)
        if kind == "pair":
            return b.rearrange("p (k g n) -> p k g n", k=KT, g=2)
        return b

    def add_rows(w, kts):
        for i in range(0, len(kts), 2):
            parts = [kview(w)[:, k:k + 2, :] for k in kts[i:i + 2]]
            chunks.append(("rows", len(parts), parts, None))

    phases = {}
    state = dict(U=0, C=0, E=0)

    def phase(name, add):
        c0 = len(chunks)
        add()
        n = sum(c[1] for c in chunks[c0:])
        phases[name] = dict(U=state["U"], C=c0, n=n, nc=len(chunks) - c0)
        state["U"] += n

    def cols_phase(name, w, starts, index=False):
        def add():
            if index:
                chunks.append(("cols", 2, [kview(w)[:, :, 3072:3328]], "index"))
            for i in range(0, len(starts), 2):
                chunks.append(("cols", 2, [kview(w)[:, :, n0:n0 + 256] for n0 in starts[i:i + 2]], None))
        phase(name, add)
        phases[name]["E"] = state["E"]
        state["E"] += phases[name]["n"]

    def ffn(i, f):
        def up():
            w = kview(a["ffn_w_up"][i, f])
            for c in range(FF // 256):
                chunks.append(("pair", 2, [w[:, :, g * FF + c * 256:g * FF + c * 256 + 256] for g in range(2)], None))
        phase(f"up{i}{f}", up)
        phases[f"up{i}{f}"]["E"] = state["E"]
        state["E"] += phases[f"up{i}{f}"]["n"]
        phase(f"down{i}{f}", lambda: add_rows(a["ffn_w_down"][i, f], range(0, FT, 2)))

    cols_phase("kv0", a["mem_w_kv"][0], range(0, 1024, 256))
    cols_phase("kv1", a["mem_w_kv"][1], range(0, 1024, 256))
    ffn(0, 0)
    cols_phase("pool_in", a["pool_w_in"][0], [1024, 1280, 0, 256, 512, 768])
    phase("pool_outx", lambda: add_rows(a["pool_w_out"][0], [8, 10]))

    def pool_group():
        w = a["pool_w_group"][0].rearrange("g (c p) n -> p (g c) n", p=128)
        chunks.append(("group", 2, [w[:, 4 * q:4 * q + 4, :] for q in range(2)], None))
    phase("group", pool_group)
    phases["group"]["E"] = state["E"]
    state["E"] += 4
    phase("pool_out", lambda: add_rows(a["pool_w_out"][0], [0, 2, 4, 6]))
    ffn(0, 1)
    ffn(1, 0)
    cols_phase("diff_in", a["diff_w_in"][0], [3072, 3328] + [n0 for i in range(0, 1024, 256) for n0 in (i, 1024 + i, 2048 + i)])
    phase("diff_out", lambda: add_rows(a["diff_w_out"][0], [8, 10, 0, 2, 4, 6]))
    ffn(1, 1)
    w2 = a["w_in_2"][0]
    cols_phase("in2", w2, [side + i + part for side in (0, 1536) for i in (0, 256) for part in (0, 512, 1024)],
               index=True)
    phase("out2", lambda: add_rows(a["w_out_2"][0], [0, 2, 4, 6]))
    cols_phase("wq", a["peer_wq_2"][0], range(0, 2048, 256))

    half_of = []
    for c, ch in enumerate(chunks):
        half_of += [(c, h) for h in range(ch[1])]
    last_half = [max(u for u, (cc, _) in enumerate(half_of) if cc == c) for c in range(len(chunks))]
    slot_loads = []
    total = [0, 0]
    for c, ch in enumerate(chunks):
        total[c % 2] += 16 * (4 if ch[3] == "index" else len(ch[2]))
        slot_loads.append(total[c % 2])

    block = ctx.enter_context(nc.Block())

    X_AFTER = {n: 4 * (i + 1) for i, n in enumerate(
        ["input", "down00", "pool_out", "down01", "down10", "diff_out", "down11", "final", "out2"])}
    ATT = dict(mem0=0, mem1=4, diff=8, moba=16, dsa=24)
    NORMS = dict(mem=(0, G_MEM, 0), up00=(1, G_NORM, 1), pool_in=(2, G_NORM + 8, 2), up01=(3, G_NORM + 16, 3),
                 up10=(4, G_NORM + 24, 4), diff_in=(5, G_NORM + 32, 5), up11=(6, G_NORM + 40, 6), final=(7, G_FIN, None),
                 in2=(8, None, 7), wq=(9, None, 8))
    HN = dict(mem=0, in2=1, wq=2)
    LAM_INIT = 0.8 - 0.6 * math.exp(-0.3 * 1)

    IN2_LAST = 8

    def heads_of(kind):
        if kind in ("mem0", "mem1"):
            l = int(kind[3])
            xq = xq1 if l else xq0
            return [dict(a=ATT[kind] + h, qk=[(xq[:, h], memK[:, l, h])], v=lambda s, h=h: memV[:, l, s, h * 128:h * 128 + 128],
                         scale=128.0 ** -0.5, base=0, rows=(0, 128), tile=8 + h, bias=None, split=True) for h in range(4)]
        if kind == "diff":
            return [dict(a=ATT[kind] + h, qk=[(dQ[64 * c:64 * c + 64, h], dK[64 * c:64 * c + 64, h]) for c in range(2)],
                         v=lambda s, h=h: dV[:, s, h * 128:h * 128 + 128], scale=0.125, base=0, rows=(0, 128), tile=h,
                         bias=bias1[:, h % 2], bias_sem=(S["bias_ready"], h + 1), split=False, head=h) for h in range(8)]
        out = []
        for h in range(16):
            r = slice(64 * (h % 2), 64 * (h % 2) + 64)
            s = (S["bias_ready"], h + 1) if h >= 8 else (b_landed[h % 2], 32 * (h // 2 + 1))
            out.append(dict(a=ATT["moba"] + h, qk=[(hQ[r, h // 2], hK[r, h // 2])], v=lambda s, h=h: hV[:, s, h * 64:h * 64 + 64],
                            scale=0.125, base=0 if h < IN2_LAST + 2 else 4, rows=(r.start, r.stop), tile=h // 2, bias=bias2[:, h % 2], bias_sem=s,
                            split=True))
        return out

    ADA = {}
    for i, (name, h) in enumerate([("down00", 5), ("down00", 9), ("down01", 0), ("down01", 4), ("down01", 8), ("down10", 0),
                                   ("down10", 4), ("down10", 8), ("diff_in", 10), ("down11", 0), ("down11", 1), ("down11", 9)]):
        ADA[(name, h)] = i

    def dest_diff(j):
        if j < 2:
            return xq1[:, 2 * j:2 * j + 2]
        i, part = divmod(j - 2, 3)
        return dV[:, :, i * 256:i * 256 + 256] if part == 2 else (dQ, dK)[part][:, 2 * i:2 * i + 2]

    def dest_in2(j):
        i, part = divmod(j - 2, 3)
        if part == 2:
            return hV[:, :, i * 256:i * 256 + 256]
        return (hQ, hK)[part][:, 2 * i:2 * i + 2]

    def is_values(name, j):
        return name in ("diff_in", "in2") and j >= 2 and (j - 2) % 3 == 2

    POOL_SLOTS = {i: 2 + i for i in range(4)}
    DIFF_SLOTS = {i: 4 + i for i in range(10)}
    IN2_SLOTS = {i: 5 + i for i in range(IN2_LAST + 1)}
    OUT2_SLOTS = {11: 0, 12: 1, 15: 2}

    def rb(x):
        return 16 * (x % 2)

    def nmax(x, j):
        return st[:, rb(x) + j:rb(x) + j + 1]

    def rsum(x, j):
        return st[:, rb(x) + 4 + j:rb(x) + 5 + j]

    def rinv(x, j):
        return st[:, rb(x) + 8 + j:rb(x) + 9 + j]

    class Chain:
        def __init__(self, eng, s):
            self.eng, self.s, self.n = eng, s, 0

        def __call__(self, ins):
            self.n += 1
            ins.then_inc(self.s, 1)
            self.eng.wait_ge(self.s, self.n)

    @block.sync
    def _(sp):
        sp.dma_start(xin, a["x"][0].rearrange("(a p) n -> p a n", p=128)).then_inc(S["x_landed"], 16)
        sp.dma_start(memin, a["mem"][0].rearrange("(a p) n -> p a n", p=128)).then_inc(S["mem_landed"], 16)

        def vec(w):
            return w.rearrange("(a n) -> a n", n=128)
        loads = [(rows1, 0, a["norm_g"].rearrange("l s (a n) -> (l s a) n", n=128), 48), (rows1, G_MEM, vec(a["mem_norm_g"]), 8),
                 (rows1, G_POOL, vec(a["pool_scale"][0]), 8), (rows1, G_ATT, vec(a["norm_attn_2"][0]), 8),
                 (rows1, G_FFN, vec(a["norm_ffn_2"][0]), 8), (rows1, G_C, vec(a["c_2"][0]), 8),
                 (rows1, G_FIN, vec(a["final_norm_g"]), 8), (rows1, G_DIFF, a["diff_norm_g"], 1),
                 (rows2, 0, vec(a["b_ada_2"][0]), 48)]
        for r, at, src, n in loads:
            sp.dma_start(r[at:at + n, :], src).then_inc(S["rows_landed"], 16)

        def load(c):
            kind, n, parts, special = chunks[c]
            if c >= 2:
                sp.wait_ge(S["lo_ready"], last_half[c - 2] + 1)
            for q, src in enumerate(parts):
                sp.dma_start(raw_dst_of(c % 2, kind, q), src).then_inc(raw_landed[c % 2], 16)
            if special == "index":
                r = WR[:, c % 2, :].rearrange("p (k n) -> p k n", k=KT)
                for at, n0, n in ((256, 3328, 64), (320, 3328, 64), (384, 3392, 4)):
                    sp.dma_start(r[:, :, at:at + n], kview(w2)[:, :, n0:n0 + n]).then_inc(raw_landed[c % 2], 16)

        def raw_dst_of(slot, kind, part):
            if kind == "group":
                return WR[:, slot, part * 1024:part * 1024 + 1024].rearrange("p (k n) -> p k n", k=4)
            return raw_dst(slot, kind, part)

        def load_up(i, f):
            p = phases[f"up{i}{f}"]
            for c in range(3):
                load(p["C"] + c)
            w = kview(a["ffn_w_up"][i, f])
            with sp.Fori(0, 4) as r:
                for j in range(2):
                    c = 3 + j
                    sp.wait_ge(S["lo_ready"], r * 4 + last_half[p["C"] + c - 2] + 1)
                    for g in range(2):
                        sp.dma_start(raw_dst_of((p["C"] + c) % 2, "pair", g),
                                     w[:, :, bass.ds(r * 512 + (g * FF + c * 256), 256)]).then_inc(raw_landed[(p["C"] + c) % 2], 16)

        for name, p in phases.items():
            if name.startswith("up"):
                load_up(int(name[2]), int(name[3]))
            else:
                for c in range(p["C"], p["C"] + p["nc"]):
                    load(c)
        sp.wait_ge(S["index_ready"], len(CALLS[0]) + len(CALLS[1]))
        sp.dma_start(gfin, a["norm_final_2"].partition_broadcast(128)).then_inc(S["gfin_landed"], 16)
        for t in range(2):
            sp.wait_ge(S["y_ready"], t + 1)
            sp.dma_start(out[0, t * 128:t * 128 + 128, :], xtok[:, t, :]).then_inc(S["stored"], 16)
        sp.wait_ge(S["stored"], 32)

    @block.gpsimd
    def _(pool):
        chain = Chain(pool, S["pool_chain"])
        pool.dma_start(reltab[0:16, :], a["rel_bias_2"]).then_inc(S["rel_landed"], 16)
        chain(nc.gpsimd.memset(ident[:], 0.0))
        nc.gpsimd.affine_select(out=ident[:], in_=ident[:], compare_op=ALU.not_equal, fill=1.0, base=0,
                                pattern=[[-1, 128]], channel_multiplier=1).then_inc(S["iden_ready"], 1)
        nc.gpsimd.memset(small[:, :], 0.0)
        nc.gpsimd.memset(eps[:, 0:1], 1e-6)
        nc.gpsimd.memset(eps[:, 1:2], 1e-5)
        nc.gpsimd.memset(ones[:], 1.0).then_inc(S["const_ready"], 1)
        nc.gpsimd.memset(relz[0:16, :], 0.0)
        chain(nc.gpsimd.memset(relr[0:16, :], NEG))
        pool.wait_ge(S["rel_landed"], 16)
        for b, lo, hi in bucket_ranges():
            if hi > lo:
                last = nc.gpsimd.tensor_scalar(relr[0:16, T - hi:T - lo], relz[0:16, T - hi:T - lo], reltab[0:16, b:b + 1],
                                               None, ALU.add)
        chain(last)
        pool.dma_start(rel_rows.rearrange("h (r n) -> h r n", n=512), relr[0:16, :].unsqueeze(1).broadcast_to([16, 128, 512])).then_inc(S["rel_stored"], 16)

        pool.wait_ge(S["silc_ready"], 1)
        wada = kview(a["w_ada_2"][0])
        cb = silc[:, :].unsqueeze(2).broadcast_to([128, KT, 128])
        base = chain.n

        def ada_piece(dram, buf, steps, landed, sums):
            for q in range(4):
                pool.dma_start(adaW[:], dram(q)).then_inc(S["ada_landed"], 16)
                pool.wait_ge(S["ada_landed"], landed(q))
                nc.gpsimd.tensor_tensor(adaW[:], adaW[:], cb, ALU.mult).then_inc(S["pool_chain"], 1)
                pool.wait_ge(S["pool_chain"], steps(3 * q + 1))
                nc.gpsimd.tensor_tensor(adaW[:, 0:4], adaW[:, 0:4], adaW[:, 4:8], ALU.add).then_inc(S["pool_chain"], 1)
                pool.wait_ge(S["pool_chain"], steps(3 * q + 2))
                nc.gpsimd.tensor_tensor(adaW[:, 0:2], adaW[:, 0:2], adaW[:, 2:4], ALU.add).then_inc(S["pool_chain"], 1)
                pool.wait_ge(S["pool_chain"], steps(3 * q + 3))
                nc.gpsimd.tensor_tensor(adaS[:, buf, q * 128:q * 128 + 128], adaW[:, 0], adaW[:, 1], ALU.add)\
                    .then_inc(S["ada_sum"], 1)
                pool.wait_ge(S["ada_sum"], sums(q + 1))

        for n in range(2):
            if n == 1:
                pool.wait_ge(S["hl_ready"], 4)
                pool.wait_ge(S["cols_ready"], 1)
                nc.gpsimd.memset(uT[:, :, 0:16], 0.0)
                nc.gpsimd.memset(wa[:, :, 0:16], 0.0)
                nc.gpsimd.memset(wb[:, :, 0:16], 0.0)
                nc.gpsimd.iota(inv[:], pattern=[[0, 4], [1, T]], base=1, channel_multiplier=0,
                               allow_small_or_imprecise_dtypes=True).then_inc(S["pad_ready"], 1)
            ada_piece(lambda q: wada[:, :, n * 512 + q * 128:n * 512 + q * 128 + 128], n,
                      lambda k: base + n * 12 + k, lambda q: n * 64 + 16 * q + 16, lambda k: 4 * n + k)

        def ada_pairs(first, n):
            with pool.Fori(0, n) as r:
                for m in range(2):
                    i = 2 * first + m
                    pool.wait_ge(S["ada_done"], r * 2 + (i - 1))
                    nc.gpsimd.tensor_tensor(small[:, 61:62], ones[:, 0:1], ones[:, 0:1], ALU.add)
                    ada_piece(lambda q: wada[:, :, bass.ds(r * 1024 + (i * 512 + q * 128), 128)], m,
                              lambda k: r * 24 + (base + 12 * i + k), lambda q: r * 128 + (i * 64 + 16 * q + 16),
                              lambda k: r * 8 + (4 * i + k))

        ada_pairs(1, 1)

        pool.wait_ge(S["x_ready"], X_AFTER["pool_out"])
        chain.n = base + 12 * 4
        chain(nc.gpsimd.iota(dist[:], pattern=[[128, 2], [-1, T]], base=0, channel_multiplier=1,
                             allow_small_or_imprecise_dtypes=True))
        chain(nc.gpsimd.affine_select(out=dist[:], in_=dist[:], compare_op=ALU.is_ge, fill=-NEG, base=0,
                                      pattern=[[128, 2], [-1, T]], channel_multiplier=1))
        base += 2
        ada_pairs(2, 2)
        for h in range(2):
            nc.gpsimd.tensor_scalar(bias1[:, h % 2], dist[:], -(2.0 ** -(h + 1)), None, ALU.mult).then_inc(S["bias_ready"], 1)
        ada_pairs(4, 1)
        for h in range(2, 8):
            pool.wait_ge(S["logits_ready"], ATT["diff"] + h - 1)
            nc.gpsimd.tensor_scalar(bias1[:, h % 2], dist[:], -(2.0 ** -(h + 1)), None, ALU.mult).then_inc(S["bias_ready"], 1)

        ada_pairs(5, 1)

        def bias_rows(h):
            for t in range(2):
                pool.dma_start(bias2[:, h % 2, t], bass.AP(rel_rows.tensor, h * 65536 + 255 - 128 * t, [[511, 128], [1, T]]))\
                    .then_inc(b_landed[h % 2], 16)
        pool.wait_ge(S["rel_stored"], 16)
        pool.wait_ge(S["logits_ready"], ATT["moba"])
        for h in range(2):
            bias_rows(h)
        pool.wait_ge(S["idx_summed"], 8)
        nc.gpsimd.affine_select(out=score[:], in_=score[:], compare_op=ALU.is_ge, fill=NEG, base=0,
                                pattern=[[128, 2], [-1, T]], channel_multiplier=1).then_inc(S["masked_ready"], 1)
        for h in range(2, 16):
            pool.wait_ge(S["logits_ready"], ATT["moba"] + h - 1)
            bias_rows(h)
            if h >= 8:
                pool.wait_ge(b_landed[h % 2], 32 * (h // 2 + 1))
                pool.wait_ge(S["pen_ready"], 2)
                nc.gpsimd.tensor_tensor(bias2[:, h % 2], bias2[:, h % 2], pen[:], ALU.add).then_inc(S["bias_ready"], 1)

        ub, vb = a["peer_u_2"][0], a["peer_v_2"][0]

        def gathers(buf, idx, table, landed, par):
            for i in range(NG):
                pool.indirect_dma_start(buf[:, par, i, :], None, table,
                                        bass.IndirectOffsetOnAxis(ap=idx[:, par, i:i + 1], axis=0)).then_inc(landed[par], 16)
        nc.gpsimd.iota(iota16, pattern=[[1, 16]], base=0, channel_multiplier=0,
                       allow_small_or_imprecise_dtypes=True).then_inc(S["iota_ready"], 1)
        pool.wait_ge(S["index_ready"], 1)
        pool.wait_ge(S["half_used"], len(half_of))
        for g in range(2):
            nc.gpsimd.tensor_copy(idxu[:, g, :], eidx[:, g * NG:g * NG + NG]).then_inc(S["iu_ready"], 1)
            pool.wait_ge(S["iu_ready"], g + 1)
            gathers(GU, idxu, ub, u_landed, g)
        for g in range(2):
            nc.gpsimd.tensor_copy(idxv[:, g, :], eidx[:, g * NG:g * NG + NG]).then_inc(S["iv_ready"], 1)
            pool.wait_ge(S["iv_ready"], g + 1)
            gathers(GV, idxv, vb, v_landed, g)
        pool.wait_ge(S["s_ready"], 8)
        nc.gpsimd.memset(zro, 0.0).then_inc(S["zero_ready"], 1)
        with pool.Fori(0, GROUPS - 1) as r:
            for g in range(2):
                pool.wait_ge(S["dots_ready"], r * 2 + (g + 1))
                nc.gpsimd.tensor_tensor(small[:, 50 + g:51 + g], small[:, 58:59], small[:, 58:59], ALU.add)
                nc.gpsimd.tensor_copy(idxu[:, g, :], eidx[:, bass.ds(r * 2 * NG + ((2 + g) * NG), NG)]).then_inc(S["iu_ready"], 1)
                pool.wait_ge(S["iu_ready"], r * 2 + (g + 3))
                nc.gpsimd.tensor_tensor(small[:, 52 + g:53 + g], small[:, 58:59], small[:, 58:59], ALU.add)
                gathers(GU, idxu, ub, u_landed, g)
                pool.wait_ge(S["v_used"], r * 2 + (g + 1))
                nc.gpsimd.tensor_tensor(small[:, 54 + g:55 + g], small[:, 58:59], small[:, 58:59], ALU.add)
                nc.gpsimd.tensor_copy(idxv[:, g, :], eidx[:, bass.ds(r * 2 * NG + ((2 + g) * NG), NG)]).then_inc(S["iv_ready"], 1)
                pool.wait_ge(S["iv_ready"], r * 2 + (g + 3))
                nc.gpsimd.tensor_tensor(small[:, 56 + g:57 + g], small[:, 58:59], small[:, 58:59], ALU.add)
                gathers(GV, idxv, vb, v_landed, g)

    @block.tensor
    def _(pe):
        mm = nc.tensor.matmul

        def product(o, wh, wl, xh, xl, first, last, skip=False):
            mm(o, wh, xh, start=first, stop=False, skip_group_check=skip)
            mm(o, wh, xl, start=False, stop=False, skip_group_check=skip)
            return mm(o, wl, xh, start=False, stop=last, skip_group_check=skip)

        def cols_half(U, u, E, e, wait_bank=True, pieces=None, between=None):
            pe.wait_ge(S["lo_ready"], U + 1)
            if wait_bank:
                pe.wait_ge(S["bank_free"], E - 1)
            order = [(b, k) for b in range(2) for k in range(KT)]
            if pieces is not None:
                order = [(b, k) for k in range(KT) for b in range(2)]
            for i, (b, k) in enumerate(order):
                if i == KT and between:
                    between()
                if pieces is not None and i % 4 == 0:
                    pe.wait_ge(S["hl_ready"], 4 * pieces + k // 2 + 1)
                c = k * 256 + b * 128
                last = product(P[4 + e][:, b * 256:b * 256 + 256], WH[:, u, c:c + 128], WL[:, u, c:c + 128],
                               hTh[:, k], hTl[:, k], k == 0 and (b == 0 or pieces is None), k == KT - 1, pieces is not None)
            last.then_inc(S["half_used"], 1)

        def values_half(U, E):
            u, e = U % 2, E % 2
            pe.wait_ge(S["lo_ready"], U + 1)
            pe.wait_ge(S["bank_free"], E - 1)
            for t in range(2):
                o = P[4 + e][:, t * 256:t * 256 + 256]
                for k in range(KT):
                    w = slice(k * 256, k * 256 + 256)
                    xh, xl = hTh[:, k, t * 128:t * 128 + 128], hTl[:, k, t * 128:t * 128 + 128]
                    mm(o, xh, WH[:, u, w], start=(k == 0), stop=False)
                    mm(o, xh, WL[:, u, w], start=False, stop=False)
                    last = mm(o, xl, WH[:, u, w], start=False, stop=(k == KT - 1))
            last.then_inc(S["half_used"], 1)

        def rows_half(U, kt0, first, last_half):
            pe.wait_ge(S["lo_ready"], U + 1)

            def one(kk, d):
                k, c = kt0 + kk, kk * 1024 + d * 128
                return product(P[d // 2][:, (d % 2) * 256:(d % 2) * 256 + 256], WH[:, U % 2, c:c + 128],
                               WL[:, U % 2, c:c + 128], actH[:, k], actL[:, k], first and kk == 0 and d % 2 == 0,
                               last_half and kk == 1, True)
            if last_half:
                for d in range(KT):
                    for kk in range(2):
                        last = one(kk, d)
                    if d % 2 and d < KT - 1:
                        last.then_inc(S["update_done"], 1)
            else:
                for kk in range(2):
                    for d in range(KT):
                        last = one(kk, d)
            last.then_inc(S["half_used"], 1)

        def ada(name, h):
            i = ADA.get((name, h))
            if i is None:
                return
            pe.wait_ge(S["ada_sum"], 4 * i + 4)
            if i == 8:
                pe.wait_ge(S["rcol_ready"], 1)
            if i:
                pe.wait_ge(S["mod_ready"], i)
            for j in range(4):
                last = mm(P[7][:, j:j + 1], adaS[:, i % 2, j * 128:j * 128 + 128], ones[:, 0:1], start=True, stop=True)
            last.then_inc(S["ada_done"], 1)

        def norm(name):
            n = NORMS[name][0]
            if n:
                pe.wait_ge(S["std_ready"], n)
            for q in range(4):
                pe.wait_ge(S["sq_ready"], 4 * n + q + 1)
                for k in (2 * q, 2 * q + 1):
                    last = mm(P[6][:, 0:T], ones[:], NT[:, k], start=(k == 0), stop=(k == KT - 1))
            last.then_inc(S["ss_ready"], 1)

        def split_ready(name):
            pe.wait_ge(S["hl_ready"], 4 * (NORMS[name][2] + 1))

        def first_halves(name):
            n, _, m = NORMS[name]
            U, E = phases[name]["U"], phases[name]["E"]

            def statistics():
                pe.wait_ge(S["std_ready"], n)
                pe.wait_ge(S["sqs_ready"], m)
                mm(P[6][:, 0:T], ones[:], NT[:, 0], start=True, stop=True).then_inc(S["ss_ready"], 1)
            cols_half(U, U % 2, E, E % 2, pieces=m)
            cols_half(U + 1, (U + 1) % 2, E + 1, (E + 1) % 2, between=statistics)

        def ffn(i, f):
            first_halves(f"up{i}{f}")
            p = phases[f"up{i}{f}"]
            U, E = p["U"], p["E"]
            with pe.Fori(0, 5) as r:
                for j in range(2, 6):
                    cols_half(r * 4 + (U + j), (U + j) % 2, r * 4 + (E + j), (E + j) % 2)
            p = phases[f"down{i}{f}"]
            for v in range(p["n"]):
                pe.wait_ge(S["act_lo"], FT * (2 * i + f) + 2 * v + 2)
                rows_half(p["U"] + v, 2 * v, v == 0, v == FT // 2 - 1)
                ada(f"down{i}{f}", v)

        def attention(units, dense):
            def scores(x, before=None):
                a = x["a"]
                both_one = before is not None and len(x["qk"]) == len(before["qk"]) == 1
                seen = a - 1 if both_one else a
                if seen > 0:
                    pe.wait_ge(S["logits_ready"], seen)
                if "need" in x:
                    pe.wait_ge(S["bank_free"], x["need"])
                for c, (q, k) in enumerate(x["qk"]):
                    b = x["base"] + (c if len(x["qk"]) == 2 else a % 2)
                    for t in range(2):
                        last = mm(P[b][:, t * T:t * T + T], q[:, t * 128:t * 128 + 128], k, start=True, stop=True)
                last.then_inc(S["score_done"], 1)

            def transposes(x):
                a = x["a"]
                if len(x["qk"]) == 2:
                    pe.wait_ge(S["diffp_ready"], x["head"] + 1)
                pe.wait_ge(S["prob_ready"], a + 1)
                if a:
                    pe.wait_ge(S["pt_ready"], a)
                for s in range(2):
                    for t in range(2):
                        last = nc.tensor.transpose(P[x["base"] + 2][:, s * T + t * 128:s * T + t * 128 + 128],
                                                   LB[:, a % 2, t, s * 128:s * 128 + 128], ident[:])
                last.then_inc(S["tr_done"], 1)

            def weighted(x):
                a = x["a"]
                pe.wait_ge(S["pt_ready"], a + 1)
                if a:
                    pe.wait_ge(S["o_ready"], a)
                for s in range(2):
                    last = mm(P[x["base"] + 3][x["rows"][0]:x["rows"][1], 0:T], x["v"](s), PTS[:, a % 2, s],
                              start=(s == 0), stop=(s == 1))
                last.then_inc(S["o_done"], 1)

            scores(units[0])
            for i in range(len(units) + 1):
                if i + 1 < len(units):
                    scores(units[i + 1], units[i])
                dense(i)
                if i < len(units):
                    transposes(units[i])
                if i >= 1:
                    weighted(units[i - 1])

        def half(name, j):
            p = phases[name]
            if is_values(name, j):
                values_half(p["U"] + j, p["E"] + j)
            else:
                cols_half(p["U"] + j, (p["U"] + j) % 2, p["E"] + j, (p["E"] + j) % 2)
            ada(name, j)

        pe.wait_ge(S["iden_ready"], 1)
        pe.wait_ge(S["const_ready"], 1)
        for b0, src, landed, done in ((4, memin, "mem_landed", "mem_tr"), (0, xin, "x_landed", "x_tr")):
            pe.wait_ge(S[landed], 16)
            for q in range(4):
                for kk in range(2):
                    for t in range(2):
                        k = 2 * q + kk
                        last = nc.tensor.transpose(P[b0 + q][:, kk * T + t * 128:kk * T + t * 128 + 128],
                                                   src[:, t, k * 128:k * 128 + 128], ident[:])
                last.then_inc(S[done], 1)
        pe.wait_ge(S["rows_landed"], 9 * 16)
        pe.wait_ge(S["x_ready"], 1)
        nc.tensor.transpose(P[0][:, 0:97], rows1[0:97, :], ident[0:97, 0:97])
        nc.tensor.transpose(P[0][:, 128:176], rows2[0:48, :], ident[0:48, 0:48]).then_inc(S["cols_tr"], 1)

        norm("mem")
        split_ready("mem")
        for l in range(2):
            p = phases[f"kv{l}"]
            for j in range(2):
                U, E = p["U"] + j, p["E"] + j
                cols_half(U, U % 2, E, E % 2, wait_bank=E >= 2)
            for j in range(2, 4):
                values_half(p["U"] + j, p["E"] + j)
        ffn(0, 0)

        first_halves("pool_in")
        pe.wait_ge(S["bank_free"], phases["pool_in"]["E"] + 2)
        attention(heads_of("mem0"), lambda i: half("pool_in", POOL_SLOTS[i]) if i in POOL_SLOTS else None)
        p = phases["pool_outx"]
        pe.wait_ge(S["o_ready"], 4)
        for v in range(2):
            rows_half(p["U"] + v, 8 + 2 * v, v == 0, False)
        p = phases["group"]
        pe.wait_ge(S["pool_lo"], 4)
        for g in range(4):
            U, E = p["U"] + g // 2, p["E"] + g
            pe.wait_ge(S["lo_ready"], U + 1)
            pe.wait_ge(S["bank_free"], E - 1)
            for b in range(2):
                for c in range(2):
                    w = ((g % 2) * 2 + c) * 256 + b * 128
                    last = product(P[4 + E % 2][:, b * 256:b * 256 + 256], WH[:, U % 2, w:w + 128], WL[:, U % 2, w:w + 128],
                                   hTh[:, 2 * g + c], hTl[:, 2 * g + c], c == 0, c == 1)
            last.then_inc(S["group_done" if g % 2 == 0 else "half_used"], 1)
        p = phases["pool_out"]
        for v in range(4):
            pe.wait_ge(S["mix_lo"], v + 1)
            rows_half(p["U"] + v, 2 * v, False, v == 3)
        ffn(0, 1)
        ffn(1, 0)

        first_halves("diff_in")
        half("diff_in", 2)
        pe.wait_ge(S["rstd_made"], NORMS["diff_in"][2])
        pe.wait_ge(S["mod_ready"], 8)
        for t in range(2):
            last = nc.tensor.transpose(P[7][:, t * 128:t * 128 + 128], rstd[:, t * 128:t * 128 + 128], ident[:])
        last.then_inc(S["rcol_tr"], 1)
        half("diff_in", 3)
        pe.wait_ge(S["bank_free"], phases["diff_in"]["E"] + 4)

        def dense_diff(i):
            if i in DIFF_SLOTS:
                half("diff_in", DIFF_SLOTS[i])
        attention_units = heads_of("mem1") + heads_of("diff")
        for n in (6, 8, 10):
            attention_units[n]["need"] = phases["diff_in"]["E"] + 4 + 3 * (n // 2 - 2)
        attention(attention_units, dense_diff)
        p = phases["diff_out"]
        pe.wait_ge(S["o_ready"], ATT["moba"])
        rows_half(p["U"], 8, True, False)
        pe.wait_ge(S["osq_ready"], 1)
        pe.wait_ge(S["mod_ready"], 9)
        pe.wait_ge(S["bank_free"], phases["diff_in"]["E"] + 14)
        for q in range(4):
            mm(P[4 + q][:], ones[:], M[:, 512 * q:512 * q + 512], start=True, stop=True).then_inc(S["oss_ready"], 1)
        rows_half(p["U"] + 1, 10, False, False)
        for v in range(4):
            pe.wait_ge(S["on_lo"], v + 1)
            rows_half(p["U"] + 2 + v, 2 * v, False, v == 3)
        ffn(1, 1)
        pe.wait_ge(S["mod_ready"], 12)
        pe.wait_ge(S["std_ready"], NORMS["final"][0])
        for q in range(4):
            for i, (b, squares) in enumerate(((6, NT), (7, NT2))):
                pe.wait_ge(S["sq_ready"], 4 * NORMS["final"][0] + 2 * q + i + 1)
                for k in (2 * q, 2 * q + 1):
                    last = mm(P[b][:, 0:T], ones[:], squares[:, k], start=(k == 0), stop=(k == KT - 1))
                if q == 3:
                    last.then_inc(S["ss_ready"], 1)

        p = phases["in2"]
        cols_half(p["U"], p["U"] % 2, p["E"], p["E"] % 2, pieces=NORMS["in2"][2])
        U, E = p["U"] + 1, p["E"] + 1
        u, o = U % 2, P[4 + E % 2]
        pe.wait_ge(S["lo_ready"], U + 1)
        pe.wait_ge(S["bank_free"], E - 1)
        for k in range(KT):
            c = k * 256
            product(o[:, 0:T], WH[:, u, c:c + 128], WL[:, u, c:c + 128], hTh[:, k], hTl[:, k], k == 0, k == KT - 1)
        for t in range(2):
            for k in range(KT):
                w = slice(k * 256 + 128, k * 256 + 132)
                xh, xl = hTh[:, k, t * 128:t * 128 + 128], hTl[:, k, t * 128:t * 128 + 128]
                ot = o[:, T + 4 * t:T + 4 * t + 4]
                mm(ot, xh, WH[:, u, w], start=(k == 0), stop=False)
                mm(ot, xh, WL[:, u, w], start=False, stop=False)
                last = mm(ot, xl, WH[:, u, w], start=False, stop=(k == KT - 1))
        last.then_inc(S["half_used"], 1)
        half("in2", 2)
        pe.wait_ge(S["ik_sq"], 1)
        mm(P[6][:, 0:T], ones[:], relu2[:, 0], start=True, stop=True).then_inc(S["ik_ss"], 1)
        half("in2", 3)
        pe.wait_ge(S["ik_ready"], 1)
        for t in range(2):
            for h in (0, 2, 1, 3):
                r = slice(64 * (h % 2), 64 * (h % 2) + 64)
                last = mm(P[2 * t + h % 2][:, (h // 2) * T:(h // 2) * T + T], iQ[r, h // 2, t * 128:t * 128 + 128], iK[r, :],
                          start=True, stop=True)
                if h >= 2:
                    last.then_inc(S["idx_products"], 1)
        half("in2", 4)
        pe.wait_ge(S["idx_relu"], 4)
        pe.wait_ge(S["bank_free"], p["E"] + 5)

        def dense_in2(i):
            if i in IN2_SLOTS:
                half("in2", IN2_SLOTS[i])
            if i in OUT2_SLOTS:
                v = OUT2_SLOTS[i]
                pe.wait_ge(S["o_ready"], ATT["moba"] + (4 * v + 4 if v else IN2_LAST + 2))
                rows_half(phases["out2"]["U"] + v, 2 * v, v == 0, False)
        units = heads_of("heads")
        for h in (4, 8, 12):
            units[h]["need"] = p["E"] + 4 + 3 * (h // 4)
        units[IN2_LAST + 2]["need"] = p["E"] + 14
        attention(units, dense_in2)
        pe.wait_ge(S["o_ready"], ATT["moba"] + 16)
        rows_half(phases["out2"]["U"] + 3, 6, False, True)

        norm("wq")
        for t in range(2):
            for q in range(2):
                for k in range(4):
                    last = nc.tensor.transpose(P[2 * t + q][:, k * 128:k * 128 + 128],
                                               xT[:, 4 * q + k, t * 128:t * 128 + 128], ident[:])
                last.then_inc(S["xtok_tr"], 1)
        pe.wait_ge(S["sk_landed"], 16)
        for q, b in enumerate((4, 5, 7, 0)):
            if q == 3:
                pe.wait_ge(S["xtok_ready"], 1)
            for k in range(4):
                last = nc.tensor.transpose(P[b][:, k * 128:k * 128 + 128], skin[:, 4 * q + k], ident[:])
            last.then_inc(S["sk_tr"], 1)
        pe.wait_ge(S["hn_ready"], 4 * 3)
        pe.wait_ge(S["xtok_ready"], 4)
        pe.wait_ge(S["sk_ready"], 3)
        for n, b in enumerate((1, 2, 3, 7)):
            for k in range(4):
                last = nc.tensor.transpose(P[b][:, k * 128:k * 128 + 128],
                                           NT[:, 4 * (n % 2) + k, (n // 2) * 128:(n // 2) * 128 + 128], ident[:])
            last.then_inc(S["htok_tr"], 1)
        p = phases["wq"]

        def subkey_scores(j):
            if j == 0:
                pe.wait_ge(S["sk_ready"], 4)
            if j == 1:
                pe.wait_ge(S["htok_ready"], 1)
            pe.wait_ge(S["bank_free"], p["E"] + j + 1)
            if j >= 2:
                pe.wait_ge(S["s_ready"], j - 1)
            for t in range(2):
                for b in range(2):
                    last = mm(P[j % 2][:, t * 256 + b * 128:t * 256 + b * 128 + 128], pQ[:, j % 4, b, t * 128:t * 128 + 128],
                              skT[:, 2 * j + b], start=True, stop=True)
            last.then_inc(S["sk_scores"], 1)
        for j in range(8):
            cols_half(p["U"] + j, (p["U"] + j) % 2, p["E"] + j, (p["E"] + j) % 2, pieces=None if j else NORMS["wq"][2])
            if j:
                subkey_scores(j - 1)
        subkey_scores(7)
        pe.wait_ge(S["zero_ready"], 1)
        pe.wait_ge(S["htok_ready"], 4)
        for b in range(4):
            mm(P[b][:], zro, xtok[:, 0, 0:512], start=True, stop=False, skip_group_check=True)

        def experts(t, r, g):
            pe.wait_ge(S["diag_ready"], r * 2 + (t * GROUPS + g + 1))
            pe.wait_ge(v_landed[g], r * (16 * NG) + (t * GROUPS // 2 + 1) * 16 * NG)
            for i in range(NG):
                for q in range(2):
                    last = mm(P[2 * t + q][:], diag[:, g, i], GV[:, g, i, q * 512:q * 512 + 512], start=False, stop=False,
                              skip_group_check=True)
            last.then_inc(S["v_used"], 1)
        for t in range(2):
            with pe.Fori(0, GROUPS // 2) as r:
                for g in range(2):
                    experts(t, r, g)
            for q in range(2):
                last = mm(P[2 * t + q][:], zro, xtok[:, 1, 0:512], start=False, stop=True, skip_group_check=True)
            last.then_inc(S["acc_done"], 1)
            if t == 0:
                pe.wait_ge(S["g2_diag"], 1)
                for k in range(KT):
                    last = mm(P[4 + k // 4][:, (k % 4) * 128:(k % 4) * 128 + 128], ones[:], g2d[:, k], start=True, stop=True)
                last.then_inc(S["g2_tr"], 1)

    @block.scalar
    def _(act):
        copy = ACT.Copy

        def split(U):
            if U >= len(half_of):
                return
            c, h = half_of[U]
            kind = chunks[c][0]
            if U >= 2:
                act.wait_ge(S["half_used"], U - 1)
            act.wait_ge(raw_landed[c % 2], slot_loads[c])
            if kind == "group":
                nc.scalar.activation(WH[:, U % 2, 0:1024], WR[:, c % 2, h * 1024:h * 1024 + 1024], copy).then_inc(S["hi_ready"], 1)
            else:
                nc.scalar.activation(split_view(WH, U % 2, kind), raw(c % 2, kind, h), copy).then_inc(S["hi_ready"], 1)

        def split_loop(U, r):
            c, h = half_of[U]
            act.wait_ge(S["half_used"], r * 4 + (U - 1))
            act.wait_ge(raw_landed[c % 2], r * 32 + slot_loads[c])
            nc.scalar.activation(split_view(WH, U % 2, "pair"), raw(c % 2, "pair", h), copy).then_inc(S["hi_ready"], 1)

        def norm(name, src, ready, base, between=None):
            n, _, m = NORMS[name]
            if n == 1:
                act.wait_ge(S["hl_ready"], 4)
            for q in range(4):
                act.wait_ge(S[ready], base + q + 1)
                nc.scalar.activation(NT[:, 2 * q:2 * q + 2], src[:, 2 * q:2 * q + 2], ACT.Square).then_inc(S["sq_ready"], 1)
            act.wait_ge(S["ss_ready"], n + 1)
            nc.scalar.activation(rstd[:], P[6][:, 0:T], ACT.Sqrt, bias=eps[:, 0:1], scale=1.0 / D).then_inc(S["std_ready"], 1)
            if m is None:
                return
            if between:
                between()
            nxt = {"mem": "kv0"}.get(name, name)
            if phases[nxt]["U"]:
                act.wait_ge(S["half_used"], phases[nxt]["U"])
            for q in range(4):
                act.wait_ge(S["hn_ready"], 4 * HN[name] + q + 1)
                nc.scalar.activation(hTh[:, 2 * q:2 * q + 2], NT[:, 2 * q:2 * q + 2], copy).then_inc(S["hh_ready"], 1)

        def late_norm(name, base):
            n, gain, m = NORMS[name]

            if n == 1:
                act.wait_ge(S["hl_ready"], 4)
                for q in range(4):
                    act.wait_ge(S["x_ready"], base + q + 1)
                    nc.scalar.activation(NT[:, 2 * q:2 * q + 2], xT[:, 2 * q:2 * q + 2], ACT.Square).then_inc(S["sq_ready"], 1)
                act.wait_ge(S["half_used"], phases[name]["U"])
            for q in range(4):
                act.wait_ge(S["x_ready"], base + q + 1)
                for k in (2 * q, 2 * q + 1):
                    last = nc.scalar.activation(hTh[:, k], xT[:, k], copy, scale=cols[:, gain + k:gain + k + 1])
                last.then_inc(S["hh_ready"], 1)
            if n > 1:
                split(phases[name]["U"] + 1)
                for q in range(4):
                    nc.scalar.activation(NT[:, 2 * q:2 * q + 2], xT[:, 2 * q:2 * q + 2], ACT.Square).then_inc(S["sq_ready"], 1)

        def late_std(name):
            n = NORMS[name][0]
            act.wait_ge(S["ss_ready"], n + 1)
            nc.scalar.activation(rstd[:], P[6][:, 0:T], ACT.Sqrt, bias=eps[:, 0:1], scale=1.0 / D).then_inc(S["std_ready"], 1)

        def gate_silu(E, s, j):
            act.wait_ge(S["bank_free"], E + 1)
            if j >= 2:
                act.wait_ge(S["prod_ready"], s - 1)
            nc.scalar.activation(SIL[:, j % 2], GUP[:, j % 2, 0], ACT.Silu).then_inc(S["sil_ready"], 1)

        def hi_act(s, j, tile):
            act.wait_ge(S["prod_ready"], s)
            nc.scalar.activation(tile, PRD[:, j % 2], copy).then_inc(S["act_hi"], 1)

        def ffn(i, f, base):
            late_norm(f"up{i}{f}", base)
            p = phases[f"up{i}{f}"]
            U, E, s0 = p["U"], p["E"], FT * (2 * i + f)

            def step(j):
                split(U + j + 2)
                if j == 0:
                    late_std(f"up{i}{f}")
                gate_silu(E + j, s0 + j, j)
                if j:
                    hi_act(s0 + j, j - 1, actH[:, j - 1])
            step(0)
            step(1)
            with act.Fori(0, 4) as r:
                for j in range(2, 6):
                    split_loop(U + j + 2, r)
                    gate_silu(r * 4 + (E + j), r * 4 + (s0 + j), j)
                    hi_act(r * 4 + (s0 + j), j - 1, actH[:, bass.ds(r * 4 + (j - 1), 1), :].rearrange("p a t -> p (a t)"))
            for j in range(18, 22):
                step(j)
            hi_act(s0 + 22, 21, actH[:, 21])
            p = phases[f"down{i}{f}"]
            for v in range(p["n"] - (f"down{i}{f}" != "down11")):
                split(p["U"] + v + 2)

        def attention(units, dense):
            def exps(x):
                a, n = x["a"], 2 * len(x["qk"])
                act.wait_ge(S["neg_max"], a + 1)
                for j in range(n):
                    last = nc.scalar.activation(LB[:, a % 2, j], LB[:, a % 2, j], ACT.Exp, bias=nmax(a, j), scale=1.0,
                                                accum_out=rsum(a, j))
                last.then_inc(S["exp_done"], 1)

            def normalise(x):
                a = x["a"]
                act.wait_ge(S["rsum_ready"], a + 1)
                for t in range(2):
                    last = nc.scalar.activation(LB[:, a % 2, t], LB[:, a % 2, t], copy, scale=rinv(a, t))
                last.then_inc(S["prob_ready"], 1)

            def pt(x):
                a = x["a"]
                act.wait_ge(S["tr_done"], a + 1)
                if a >= 2:
                    act.wait_ge(S["o_done"], a - 1)
                nc.scalar.activation(PTS[:, a % 2].rearrange("p a b -> p (a b)"), P[x["base"] + 2][:], copy).then_inc(S["pt_ready"], 1)

            def result(x):
                if not x["split"]:
                    return
                a, (r0, r1) = x["a"], x["rows"]
                act.wait_ge(S["o_done"], a + 1)
                nc.scalar.activation(actH[r0:r1, x["tile"]], P[x["base"] + 3][r0:r1, 0:T], copy).then_inc(S["o_hi"], 1)

            exps(units[0])
            for i in range(len(units) + 2):
                if i < len(units):
                    normalise(units[i])
                if i + 1 < len(units):
                    exps(units[i + 1])
                if i >= 2:
                    result(units[i - 2])
                dense(i)
                if i < len(units):
                    pt(units[i])

        act.dma_start(lamw, a["diff_lambda"][0].partition_broadcast(128)).then_inc(S["lam_landed"], 16)
        for q in range(4):
            act.wait_ge(S["mem_tr"], q + 1)
            nc.scalar.activation(memT[:, 2 * q:2 * q + 2].rearrange("p a b -> p (a b)"), P[4 + q][:], copy).then_inc(S["mem_in"], 1)
        split(0)
        split(1)
        act.wait_ge(S["const_ready"], 1)
        act.wait_ge(S["cols_ready"], 1)
        nc.scalar.activation(silc[:], cols[:, G_C:G_C + KT], ACT.Silu).then_inc(S["silc_ready"], 1)
        norm("mem", memT, "mem_in", 0)
        for U in range(8):
            split(U + 2)
        ffn(0, 0, 0)
        late_norm("pool_in", X_AFTER["down00"] - 4)
        p = phases["pool_in"]
        split(p["U"] + 2)
        late_std("pool_in")
        split(p["U"] + 3)

        def dense_pool(i):
            if i in POOL_SLOTS:
                split(phases["pool_in"]["U"] + POOL_SLOTS[i] + 2)
        attention(heads_of("mem0"), dense_pool)
        act.wait_ge(S["half_used"], p["U"] + 6)
        for g in range(4):
            act.wait_ge(S["pooled_ready"], g + 1)
            nc.scalar.activation(hTh[:, 2 * g:2 * g + 2], ptmp[:, 2 * g:2 * g + 2], copy).then_inc(S["pool_hi"], 1)
        p = phases["pool_outx"]
        for v in range(p["n"]):
            split(p["U"] + v + 2)
        p = phases["group"]
        for j in range(2):
            for g in (2 * j, 2 * j + 1):
                if g % 2:
                    split(p["U"] + j + 2)
                act.wait_ge(S["bank_free"], p["E"] + g + 1)
                nc.scalar.activation(actH[:, 2 * g:2 * g + 2], ptmp[:, 2 * g:2 * g + 2], copy).then_inc(S["mix_hi"], 1)
        p = phases["pool_out"]
        for v in range(p["n"] - 1):
            split(p["U"] + v + 2)
        ffn(0, 1, X_AFTER["pool_out"] - 4)
        ffn(1, 0, X_AFTER["down01"] - 4)

        act.wait_ge(S["lam_ready"], 1)
        nc.scalar.activation(small[:, 2:4], small[:, 0:2], ACT.Exp).then_inc(S["lam_exp"], 1)
        late_norm("diff_in", X_AFTER["down10"] - 4)
        p = phases["diff_in"]
        for j in range(4):
            split(p["U"] + j + 2)
            if j == 0:
                late_std("diff_in")

        def dense_diff(i):
            if i in DIFF_SLOTS:
                split(phases["diff_in"]["U"] + DIFF_SLOTS[i] + 2)
        attention(heads_of("mem1") + heads_of("diff"), dense_diff)
        act.wait_ge(S["o_ready"], ATT["moba"])
        nc.scalar.activation(M[:, 0:2048], M[:, MX:MX + 2048], ACT.Square).then_inc(S["osq_ready"], 1)
        p = phases["diff_out"]
        split(p["U"] + 2)
        for q in range(4):
            act.wait_ge(S["oss_ready"], q + 1)
            nc.scalar.activation(M[:, MX + 2048 + 512 * q:MX + 2560 + 512 * q], P[4 + q][:], ACT.Sqrt, bias=eps[:, 1:2],
                                 scale=1.0 / 128).then_inc(S["ostd_ready"], 1)
        for q in range(4):
            act.wait_ge(S["on_ready"], q + 1)
            nc.scalar.activation(actH[:, 2 * q:2 * q + 2], dQ[:, 2 * q:2 * q + 2], copy).then_inc(S["on_hi"], 1)
            if q < 2:
                split(p["U"] + q + 3)
        split(p["U"] + 5)
        split(p["U"] + 6)
        ffn(1, 1, X_AFTER["diff_out"] - 4)

        for q in range(4):
            act.wait_ge(S["x_ready"], X_AFTER["down11"] - 4 + q + 1)
            nc.scalar.activation(NT[:, 2 * q:2 * q + 2], xT[:, 2 * q:2 * q + 2], ACT.Square).then_inc(S["sq_ready"], 1)
            for k in (2 * q, 2 * q + 1):
                last = nc.scalar.activation(NT2[:, k], xT[:, k], ACT.Square, scale=cols[:, G_FIN + k:G_FIN + k + 1])
            last.then_inc(S["sq_ready"], 1)
        late_std("final")
        act.wait_ge(S["m2_ready"], 1)
        nc.scalar.activation(rstd2, rstd2, ACT.Sqrt, bias=eps[:, 0:1], scale=1.0 / D).then_inc(S["std_ready"], 1)
        for q in range(4):
            act.wait_ge(S["hn_ready"], 4 * HN["in2"] + q + 1)
            for k in (2 * q, 2 * q + 1):
                last = nc.scalar.activation(hTh[:, k], NT[:, k], ACT.Identity, bias=modc[:, k:k + 1], scale=1.0)
            last.then_inc(S["hh_ready"], 1)
        p = phases["in2"]
        split(p["U"] + 2)
        split(p["U"] + 3)
        act.wait_ge(S["bank_free"], p["E"] + 2)
        nc.scalar.activation(relu2[:, 0], ikraw[:, 0:T], ACT.Square).then_inc(S["ik_sq"], 1)
        split(p["U"] + 4)
        act.wait_ge(S["ik_ss"], 1)
        nc.scalar.activation(rstd[:], P[6][:, 0:T], ACT.Sqrt, bias=eps[:, 0:1], scale=1.0 / 128).then_inc(S["ik_std"], 1)
        split(p["U"] + 5)
        for n in range(4):
            act.wait_ge(S["idx_products"], n + 1)
            if n >= 2:
                act.wait_ge(S["idx_summed"], 2 * (n - 1))
            nc.scalar.activation(relu2[:, 2 * (n % 2):2 * (n % 2) + 2], P[n][:].rearrange("p (a b) -> p a b", a=2), ACT.Relu)\
                .then_inc(S["idx_relu"], 1)
        split(p["U"] + 6)

        def dense_in2(i):
            if i in IN2_SLOTS:
                split(phases["in2"]["U"] + IN2_SLOTS[i] + 2)
            if i in OUT2_SLOTS:
                split(phases["out2"]["U"] + OUT2_SLOTS[i] + 2)
        attention(heads_of("heads"), dense_in2)
        split(phases["out2"]["U"] + 5)

        act.wait_ge(S["x_ready"], X_AFTER["out2"])
        act.dma_start(skin, a["peer_subkeys_2"][0].rearrange("h q n d -> n (h q) d")).then_inc(S["sk_landed"], 16)

        def peer_tiles():
            for n in range(4):
                act.wait_ge(S["xtok_tr"], n + 1)
                nc.scalar.activation(xtok[:, n // 2, (n % 2) * 512:(n % 2) * 512 + 512], P[n][:], copy).then_inc(S["xtok_ready"], 1)
            for q, b in enumerate((4, 5, 7, 0)):
                act.wait_ge(S["sk_tr"], q + 1)
                nc.scalar.activation(skT[:, 4 * q:4 * q + 4].rearrange("p a b -> p (a b)"), P[b][:], copy).then_inc(S["sk_ready"], 1)
        norm("wq", xT, "x_ready", X_AFTER["out2"] - 4, peer_tiles)
        for n, b in enumerate((1, 2, 3, 7)):
            act.wait_ge(S["htok_tr"], n + 1)
            nc.scalar.activation(htok[:, n // 2, (n % 2) * 512:(n % 2) * 512 + 512], P[b][:], copy).then_inc(S["htok_ready"], 1)
        p = phases["wq"]

        def scores_out(j):
            act.wait_ge(S["sk_scores"], j + 1)
            for t in range(2):
                last = nc.scalar.activation(sks[t][:, 2 * j:2 * j + 2].rearrange("p a b -> p (a b)"),
                                            P[j % 2][:, t * 256:t * 256 + 256], copy)
            last.then_inc(S["s_ready"], 1)
        for j in range(p["n"]):
            split(p["U"] + j + 2)
            if j >= 2:
                scores_out(j - 2)
        scores_out(6)
        scores_out(7)

        def gate_exps(n, t, hs):
            act.wait_ge(S["gdiff_ready"], n + 1)
            x = gate[:, t, hs[0]:hs[-1] + 1]
            nc.scalar.activation(x, x, ACT.Exp).then_inc(S["gexp_ready"], 1)
        for n in range(2):
            gate_exps(n, *ALL_CALLS[n])

        def experts(t, r, g, first=False):
            n = t * GROUPS + g
            act.wait_ge(S["dots_ready"], r * 2 + (n + 1))
            if not first:
                act.wait_ge(S["coef_ready"], r * 2 + (n - 1))
            nc.scalar.activation(gel8[:, g], dots[:, g], ACT.Gelu).then_inc(S["gelu_ready"], 1)
            act.wait_ge(S["coef_ready"], r * 2 + (n + 1))
            if not first:
                act.wait_ge(S["v_used"], r * 2 + (n - 1))
            for i in range(NG):
                last = nc.scalar.activation(diag[:, g, i], ident[:], copy, scale=coef8[:, g, i:i + 1])
            last.then_inc(S["diag_ready"], 1)
        for n in range(PEELED):
            experts(0, n // 2, n % 2, n < 2)
            if n in CALL_AFTER:
                gate_exps(CALL_AFTER[n], *ALL_CALLS[CALL_AFTER[n]])
        with act.Fori(PEELED // 2, GROUPS // 2) as r:
            for g in range(2):
                experts(0, r, g)
        act.wait_ge(S["index_ready"], len(CALLS[0]) + len(CALLS[1]))
        for k in range(KT):
            last = nc.scalar.activation(g2d[:, k], ident[:], copy, scale=modc[:, 40 + k:41 + k])
        last.then_inc(S["g2_diag"], 1)
        act.wait_ge(S["g2_tr"], 1)
        for q in range(2):
            last = nc.scalar.activation(g2bc[:, q * 512:q * 512 + 512], P[4 + q][:], copy)
        last.then_inc(S["g2_ready"], 1)
        with act.Fori(0, GROUPS // 2) as r:
            for g in range(2):
                experts(1, r, g)
        for t in range(2):
            act.wait_ge(S["xf_ready"], t + 1)
            nc.scalar.activation(tmpf, xtok[:, t], ACT.Square, accum_out=small[:, 44 + t:45 + t]).then_inc(S["fss_ready"], 1)
            act.wait_ge(S["fss_ready"], t + 1)
            nc.scalar.activation(small[:, 46 + t:47 + t], small[:, 44 + t:45 + t], ACT.Sqrt, bias=eps[:, 0:1], scale=1.0 / D)\
                .then_inc(S["fstd_ready"], 1)

    @block.vector
    def _(dve):
        chain = Chain(dve, S["dve_chain"])
        tt, ts, stt = nc.vector.tensor_tensor, nc.vector.tensor_scalar, nc.vector.scalar_tensor_tensor

        def split(U):
            if U >= len(half_of):
                return
            c, h = half_of[U]
            kind = chunks[c][0]
            dve.wait_ge(S["hi_ready"], U + 1)
            if kind == "group":
                tt(WL[:, U % 2, 0:1024], WR[:, c % 2, h * 1024:h * 1024 + 1024], WH[:, U % 2, 0:1024].bitcast(F32), ALU.subtract)\
                    .then_inc(S["lo_ready"], 1)
            else:
                tt(split_view(WL, U % 2, kind), raw(c % 2, kind, h), split_view(WH, U % 2, kind).bitcast(F32), ALU.subtract)\
                    .then_inc(S["lo_ready"], 1)

        def split_loop(U, r):
            c, h = half_of[U]
            dve.wait_ge(S["hi_ready"], r * 4 + (U + 1))
            tt(split_view(WL, U % 2, "pair"), raw(c % 2, "pair", h), split_view(WH, U % 2, "pair").bitcast(F32), ALU.subtract)\
                .then_inc(S["lo_ready"], 1)

        def norm(name, src, gain, shift=None):
            n, _, m = NORMS[name]
            dve.wait_ge(S["std_ready"], n + 1)
            chain(nc.vector.reciprocal(rstd[:], rstd[:]))
            step = []
            for q in range(5):
                for k in (2 * q, 2 * q + 1):
                    if q < 4:
                        last = stt(NT[:, k], src[:, k], gain(k), rstd[:], ALU.mult, ALU.mult)
                if q < 4:
                    if shift is None:
                        last.then_inc(S["hn_ready"], 1)
                    else:
                        last.then_inc(S["dve_chain"], 1)
                        chain.n += 1
                        step.append(chain.n)
                if shift is not None and q:
                    dve.wait_ge(S["dve_chain"], step[q - 1])
                    for k in (2 * q - 2, 2 * q - 1):
                        last = ts(NT[:, k], NT[:, k], shift(k), None, ALU.add)
                    last.then_inc(S["hn_ready"], 1)
            for q in range(4):
                dve.wait_ge(S["hh_ready"], 4 * m + q + 1)
                tt(hTl[:, 2 * q:2 * q + 2], NT[:, 2 * q:2 * q + 2], hTh[:, 2 * q:2 * q + 2].bitcast(F32), ALU.subtract)\
                    .then_inc(S["hl_ready"], 1)

        def col(at):
            return lambda k: cols[:, at + k:at + k + 1]

        def late_lo(name, q):
            _, gain, m = NORMS[name]
            dve.wait_ge(S["hh_ready"], 4 * m + q + 1)
            for k in (2 * q, 2 * q + 1):
                last = stt(hTl[:, k], xT[:, k], cols[:, gain + k:gain + k + 1], hTh[:, k].bitcast(F32), ALU.mult, ALU.subtract)
            last.then_inc(S["hl_ready"], 1)

        def late_rstd(name):
            dve.wait_ge(S["std_ready"], NORMS[name][0] + 1)
            nc.vector.reciprocal(rstd[:], rstd[:]).then_inc(S["rstd_made"], 1)
            dve.wait_ge(S["rstd_made"], NORMS[name][2])

        def post_scaled(U, E, dst):
            dve.wait_ge(S["half_used"], U + 1)
            tt(dst, P[4 + E % 2][:].rearrange("p (a b) -> p a b", a=2), rstd[:].unsqueeze(1).broadcast_to([128, 2, T]), ALU.mult)\
                .then_inc(S["bank_free"], 1)

        def post_values(U, E, dst):
            dve.wait_ge(S["half_used"], U + 1)
            for t in range(2):
                last = ts(dst[:, t], P[4 + E % 2][:, t * 256:t * 256 + 256], rcol[:, t:t + 1], None, ALU.mult)
            last.then_inc(S["bank_free"], 1)

        def post_copy(U, E, dst):
            dve.wait_ge(S["half_used"], U + 1)
            nc.vector.tensor_copy(dst, P[4 + E % 2][:].rearrange("p (a b) -> p a b", a=2)).then_inc(S["bank_free"], 1)

        def ada(name, h):
            i = ADA.get((name, h))
            if i is not None:
                dve.wait_ge(S["ada_done"], i + 1)
                tt(modc[:, 4 * i:4 * i + 4], P[7][:, 0:4], badac[:, 4 * i:4 * i + 4], ALU.add).then_inc(S["mod_ready"], 1)

        def sum_squares(name):
            dve.wait_ge(S["sq_ready"], 4 * NORMS[name][0] + 4)
            chain(tt(NT[:, 0:4], NT[:, 0:4], NT[:, 4:8], ALU.add))
            chain(tt(NT[:, 0:2], NT[:, 0:2], NT[:, 2:4], ALU.add))
            tt(NT[:, 0], NT[:, 0], NT[:, 1], ALU.add).then_inc(S["sqs_ready"], 1)

        updates = []

        def add_update(U, gain, after=None):
            n = 3 * len(updates)
            updates.append(U)
            for q in range(4):
                if q < 3:
                    dve.wait_ge(S["update_done"], n + q + 1)
                else:
                    dve.wait_ge(S["half_used"], U)
                if callable(gain):
                    for k in range(2):
                        last = stt(xT[:, 2 * q + k], P[q][:, k * T:k * T + T], gain(2 * q + k), xT[:, 2 * q + k], ALU.mult, ALU.add)
                else:
                    x = xT[:, 2 * q:2 * q + 2].rearrange("p a b -> p (a b)")
                    last = stt(x, P[q][:], gain, x, ALU.mult, ALU.add)
                last.then_inc(S["x_ready"], 1)
                if q == 0:
                    split(U)
                if after and q:
                    late_lo(after, q - 1)
            if after:
                late_lo(after, 3)
            split(U + 1)
            if after:
                sum_squares(after)

        def ffn(i, f, after=None, between=None):
            p = phases[f"up{i}{f}"]
            U, E, s0 = p["U"], p["E"], FT * (2 * i + f)

            def normalised(u, e, s, j):
                dve.wait_ge(S["half_used"], u + 1)
                if j >= 2:
                    dve.wait_ge(S["sil_ready"], s - 1)
                    dve.wait_ge(S["prod_ready"], s - 1)
                tt(GUP[:, j % 2], P[4 + (E + j) % 2][:].rearrange("p (a b) -> p a b", a=2),
                   rstd[:].unsqueeze(1).broadcast_to([128, 2, T]), ALU.mult).then_inc(S["bank_free"], 1)

            def product(e, s, j):
                dve.wait_ge(S["bank_free"], e + 1)
                dve.wait_ge(S["sil_ready"], s + 1)
                if j:
                    dve.wait_ge(S["act_lo"], s)
                tt(PRD[:, j % 2], SIL[:, j % 2], GUP[:, j % 2, 1], ALU.mult).then_inc(S["prod_ready"], 1)

            def lo_act(s, j, lo, hitile):
                dve.wait_ge(S["act_hi"], s + 1)
                tt(lo, PRD[:, j % 2], hitile.bitcast(F32), ALU.subtract).then_inc(S["act_lo"], 1)

            def step(j):
                if j == 0:
                    split(U + 2)
                    late_rstd(f"up{i}{f}")
                normalised(U + j, E + j, s0 + j, j)
                if j >= 2:
                    lo_act(s0 + j - 2, j - 2, actL[:, j - 2], actH[:, j - 2])
                if j:
                    product(E + j - 1, s0 + j - 1, j - 1)
                    split(U + j + 2)
            step(0)
            step(1)
            with dve.Fori(0, 4) as r:
                for j in range(2, 6):
                    normalised(r * 4 + (U + j), r * 4 + (E + j), r * 4 + (s0 + j), j)
                    one = [b[:, bass.ds(r * 4 + (j - 2), 1), :].rearrange("p a t -> p (a t)") for b in (actL, actH)]
                    lo_act(r * 4 + (s0 + j - 2), j - 2, one[0], one[1])
                    product(r * 4 + (E + j - 1), r * 4 + (s0 + j - 1), j - 1)
                    split_loop(U + j + 2, r)
            for j in range(18, 22):
                step(j)
            lo_act(s0 + 20, 20, actL[:, 20], actH[:, 20])
            product(E + 21, s0 + 21, 21)
            lo_act(s0 + 21, 21, actL[:, 21], actH[:, 21])
            p = phases[f"down{i}{f}"]
            for v in range(p["n"]):
                if v < p["n"] - 2:
                    split(p["U"] + v + 2)
                ada(f"down{i}{f}", v)
                if between:
                    between(v)
            add_update(p["U"] + p["n"], 0.5, after)

        def mix_lo(g):
            dve.wait_ge(S["mix_hi"], g + 1)
            tt(actL[:, 2 * g:2 * g + 2], ptmp[:, 2 * g:2 * g + 2], actH[:, 2 * g:2 * g + 2].bitcast(F32), ALU.subtract)\
                .then_inc(S["mix_lo"], 1)

        def subkeys(t, j):
            hs = range(2 * j[0], 2 * j[-1] + 2)
            sk = sks[t]
            dve.wait_ge(S["s_ready"], j[-1] + 1)
            for h in hs:
                last = nc.vector.max(v16[:, h, 0:8], sk[:, h])
            chain(last)
            for h in hs:
                nc.vector.max_index(i16[:, h, 0:8], v16[:, h, 0:8], sk[:, h])
            for h in hs:
                last = nc.vector.match_replace(skw[:, h], v16[:, h, 0:8], sk[:, h], TAKEN)
            chain(last)
            for h in hs:
                last = nc.vector.max(v16[:, h, 8:16], skw[:, h])
            chain(last)
            for h in hs:
                last = nc.vector.max_index(i16[:, h, 8:16], v16[:, h, 8:16], skw[:, h])
            chain(last)

        def choose(t, hs):
            h0, h1, nh = hs[0], hs[-1] + 1, len(hs)
            wide = [128, nh, 16, 16]
            nc.vector.tensor_copy(i16f[:, 2 * h0:2 * h1], i16[:, 2 * h0:2 * h1])
            v = v16[:, 2 * h0:2 * h1].rearrange("p (h q) i -> p h q i", q=2)
            chain(tt(cand[:, h0:h1], v[:, :, 0].unsqueeze(3).broadcast_to(wide), v[:, :, 1].unsqueeze(2).broadcast_to(wide), ALU.add))
            flat = cand.rearrange("p h i j -> p h (i j)")
            for h in hs:
                last = nc.vector.max(gs[:, h, 0:8], flat[:, h])
            chain(last)
            for h in hs:
                nc.vector.max_index(pos[:, h, 0:8], gs[:, h, 0:8], flat[:, h])
            for h in hs:
                last = nc.vector.match_replace(candw[:, h], gs[:, h, 0:8], flat[:, h], TAKEN)
            chain(last)
            for h in hs:
                last = nc.vector.max(gs[:, h, 8:16], candw[:, h])
            chain(last)
            tt(gate[:, t, h0:h1], gs[:, h0:h1], gs[:, h0:h1, 0:1].broadcast_to([128, nh, 16]), ALU.subtract)\
                .then_inc(S["gdiff_ready"], 1)
            for h in hs:
                last = nc.vector.max_index(pos[:, h, 8:16], gs[:, h, 8:16], candw[:, h])
            chain(last)
            n = 16 * nh
            p = pos[:, h0:h1].rearrange("p h k -> p (h k)")
            pd, pf, ps = posd[:, :, 0:n].bitcast(U32), posf[:, :, 0:n], psel[:, :, 0:n]
            ts(pd[:, 0], p, 4, None, ALU.logical_shift_right)
            chain(ts(pd[:, 1], p, 15, None, ALU.bitwise_and))
            chain(nc.vector.tensor_copy(pf, pd))
            ix = i16f[:, 2 * h0:2 * h1].rearrange("p (h q) i -> p h q i", q=2)
            hot_h = hot[:, h0:h1]
            for q in range(2):
                f = pf[:, q].rearrange("p (h k) -> p h k", h=nh)
                chain(tt(hot_h, f.unsqueeze(3).broadcast_to(wide), iota16.unsqueeze(1).unsqueeze(1).broadcast_to(wide), ALU.is_equal))
                chain(tt(hot_h, hot_h, ix[:, :, q].unsqueeze(2).broadcast_to(wide), ALU.mult))
                chain(nc.vector.tensor_reduce(ps[:, q].rearrange("p (h k) -> p h k", h=nh), hot_h, AX.X, ALU.add))
            at = t * 128 + 16 * h0
            stt(eidx[:, at:at + n], ps[:, 0], float(128), ps[:, 1], ALU.mult, ALU.add).then_inc(S["index_ready"], 1)

        def gates(n):
            dve.wait_ge(S["gexp_ready"], n + 1)
            t, hs = ALL_CALLS[n]
            x, gsum = gate[:, t, hs[0]:hs[-1] + 1], small[:, 8:8 + len(hs)]
            chain(nc.vector.tensor_reduce(gsum, x, AX.X, ALU.add))
            chain(nc.vector.reciprocal(gsum, gsum))
            chain(tt(x, x, gsum.unsqueeze(2).broadcast_to([128, len(hs), 16]), ALU.mult))

        def attention(units, dense):
            def logits(x):
                a, n = x["a"], len(x["qk"])
                dve.wait_ge(S["score_done"], a + 1)
                if a >= 2:
                    dve.wait_ge(S["tr_done"], a - 1)
                if x["bias"] is not None:
                    dve.wait_ge(*x["bias_sem"])
                for c in range(n):
                    o = LB[:, a % 2, 2 * c:2 * c + 2]
                    i = P[x["base"] + (c if n == 2 else a % 2)][:].rearrange("p (a b) -> p a b", a=2)
                    if x["bias"] is None:
                        last = ts(o, i, x["scale"], None, ALU.mult)
                    else:
                        last = stt(o, i, x["scale"], x["bias"], ALU.mult, ALU.add)
                last.then_inc(S["logits_ready"], 1)
                dve.wait_ge(S["logits_ready"], a + 1)
                nc.vector.tensor_reduce(st[:, rb(a):rb(a) + 2 * n], LB[:, a % 2, 0:2 * n], AX.X, ALU.max, negate=True)\
                    .then_inc(S["neg_max"], 1)

            def rsums(x):
                a, n = x["a"], 2 * len(x["qk"])
                dve.wait_ge(S["exp_done"], a + 1)
                if n == 4:
                    chain(nc.vector.reciprocal(st[:, rb(a) + 8:rb(a) + 8 + n], st[:, rb(a) + 4:rb(a) + 4 + n]))
                    ts(st[:, rb(a) + 10:rb(a) + 12], st[:, rb(a) + 10:rb(a) + 12], small[:, 5:6], None, ALU.mult)\
                        .then_inc(S["rsum_ready"], 1)
                else:
                    nc.vector.reciprocal(st[:, rb(a) + 8:rb(a) + 8 + n], st[:, rb(a) + 4:rb(a) + 4 + n]).then_inc(S["rsum_ready"], 1)

            def diffs(x):
                a = x["a"]
                dve.wait_ge(S["prob_ready"], a + 1)
                for t in range(2):
                    last = stt(LB[:, a % 2, t], LB[:, a % 2, 2 + t], rinv(a, 2 + t), LB[:, a % 2, t], ALU.mult, ALU.add)
                last.then_inc(S["diffp_ready"], 1)

            def result(x):
                a, (r0, r1) = x["a"], x["rows"]
                if not x["split"]:
                    dve.wait_ge(S["o_done"], a + 1)
                    nc.vector.tensor_copy(dQ[:, x["head"]], P[x["base"] + 3][:, 0:T]).then_inc(S["o_ready"], 1)
                    return
                ohi = a + 1 - (8 if a >= ATT["moba"] else 0)
                dve.wait_ge(S["o_hi"], ohi)
                tt(actL[r0:r1, x["tile"]], P[x["base"] + 3][r0:r1, 0:T], actH[r0:r1, x["tile"]].bitcast(F32), ALU.subtract)\
                    .then_inc(S["o_ready"], 1)

            logits(units[0])
            for i in range(len(units) + 2):
                if i < len(units):
                    rsums(units[i])
                if i + 1 < len(units):
                    logits(units[i + 1])
                if i < len(units) and len(units[i]["qk"]) == 2:
                    diffs(units[i])
                if i >= 2:
                    result(units[i - 2])
                dense(i)

        for q in range(4):
            dve.wait_ge(S["x_tr"], q + 1)
            nc.vector.tensor_copy(xT[:, 2 * q:2 * q + 2].rearrange("p a b -> p (a b)"), P[q][:]).then_inc(S["x_ready"], 1)
        dve.wait_ge(S["cols_tr"], 1)
        nc.vector.tensor_copy(badac[:], P[0][:, 128:176])
        nc.vector.tensor_copy(cols[:, 0:97], P[0][:, 0:97]).then_inc(S["cols_ready"], 1)
        dve.wait_ge(S["cols_ready"], 1)
        split(0)
        split(1)
        norm("mem", memT, col(G_MEM))
        for l in range(2):
            p = phases[f"kv{l}"]
            for j in range(4):
                split(p["U"] + j + 2)
                dst = memK[:, l, 2 * j:2 * j + 2] if j < 2 else memV[:, l, :, (j - 2) * 256:(j - 2) * 256 + 256]
                post_copy(p["U"] + j, p["E"] + j, dst)
        for q in range(4):
            late_lo("up00", q)
        sum_squares("up00")

        def window_counts(v):
            if v == 0:
                dve.wait_ge(S["pad_ready"], 1)
            if v < 4:
                chain(nc.vector.tensor_scalar_min(inv[:, v], inv[:, v], float(2 << v)))
                chain(nc.vector.reciprocal(inv[:, v], inv[:, v]))
        ffn(0, 0, "pool_in", window_counts)

        p = phases["pool_in"]
        for j in range(2):
            split(p["U"] + j + 2)
            if j == 0:
                late_rstd("pool_in")
            post_scaled(p["U"] + j, p["E"] + j, xq0[:, 2 * j:2 * j + 2])

        def dense_pool(i):
            if i not in POOL_SLOTS:
                return
            p, j, g = phases["pool_in"], POOL_SLOTS[i], i
            split(p["U"] + j + 2)
            post_scaled(p["U"] + j, p["E"] + j, uT[:, 2 * g:2 * g + 2, 16:])
            dve.wait_ge(S["bank_free"], p["E"] + j + 1)
            src, w = uT[:, 2 * g:2 * g + 2], 1
            for s in range(g + 1):
                dst = wa if s % 2 == 0 else wb
                chain(tt(dst[:, :, 16:], src[:, :, 16:], src[:, :, 16 - w:PADW - w], ALU.add))
                src, w = dst, 2 * w
            iv = inv[:, g].unsqueeze(1).broadcast_to([128, 2, T])
            pg = ptmp[:, 2 * g:2 * g + 2]
            chain(tt(pg, src[:, :, 16:], iv, ALU.mult))
            tt(pg, pg, uT[:, 2 * g:2 * g + 2, 16:], ALU.subtract).then_inc(S["pooled_ready"], 1)
        attention(heads_of("mem0"), dense_pool)
        for g in range(4):
            dve.wait_ge(S["pool_hi"], g + 1)
            tt(hTl[:, 2 * g:2 * g + 2], ptmp[:, 2 * g:2 * g + 2], hTh[:, 2 * g:2 * g + 2].bitcast(F32), ALU.subtract)\
                .then_inc(S["pool_lo"], 1)
        p = phases["pool_outx"]
        for v in range(p["n"]):
            split(p["U"] + v + 2)
        p = phases["group"]
        for g in range(4):
            if g % 2:
                split(p["U"] + g // 2 + 2)
                dve.wait_ge(S["half_used"], p["U"] + g // 2 + 1)
            else:
                dve.wait_ge(S["group_done"], g // 2 + 1)
            for b in range(2):
                k = 2 * g + b
                last = ts(ptmp[:, k], P[4 + (p["E"] + g) % 2][:, b * T:b * T + T], cols[:, G_POOL + k:G_POOL + k + 1], None, ALU.mult)
            last.then_inc(S["bank_free"], 1)
            if g:
                mix_lo(g - 1)
        mix_lo(3)
        p = phases["pool_out"]
        for v in range(p["n"] - 2):
            split(p["U"] + v + 2)
        add_update(p["U"] + p["n"], 1.0, "up01")
        ffn(0, 1, "up10")
        dve.wait_ge(S["lam_landed"], 16)
        lw = lamw.rearrange("p (a b) n -> p a b n", a=2)
        chain(tt(lamp, lw[:, :, 0], lw[:, :, 1], ALU.mult))
        nc.vector.tensor_reduce(small[:, 0:2], lamp, AX.X, ALU.add).then_inc(S["lam_ready"], 1)
        ffn(1, 0, "diff_in")
        dve.wait_ge(S["lam_exp"], 1)
        chain(tt(small[:, 4:5], small[:, 3:4], small[:, 2:3], ALU.subtract))
        chain(ts(small[:, 5:6], small[:, 4:5], -LAM_INIT, None, ALU.add))
        chain(ts(cols[:, 97:98], cols[:, G_DIFF:G_DIFF + 1], 1.0 - LAM_INIT, None, ALU.mult))

        p = phases["diff_in"]

        def half_diff(j):
            p = phases["diff_in"]
            split(p["U"] + j + 2)
            if j == 0:
                late_rstd("diff_in")
            if j == 4:
                dve.wait_ge(S["rcol_tr"], 1)
                for t in range(2):
                    last = nc.vector.tensor_copy(rcol[:, t:t + 1], P[7][:, t * 128:t * 128 + 1])
                last.then_inc(S["rcol_ready"], 1)
                dve.wait_ge(S["rcol_ready"], 1)
            (post_values if is_values("diff_in", j) else post_scaled)(p["U"] + j, p["E"] + j, dest_diff(j))
            ada("diff_in", j)
        for j in range(4):
            half_diff(j)
        attention(heads_of("mem1") + heads_of("diff"), lambda i: half_diff(DIFF_SLOTS[i]) if i in DIFF_SLOTS else None)
        p = phases["diff_out"]
        split(p["U"] + 2)
        for q in range(4):
            r = M[:, MX + 2048 + 512 * q:MX + 2560 + 512 * q]
            dve.wait_ge(S["ostd_ready"], q + 1)
            chain(nc.vector.reciprocal(r, r))
            o = M[:, MX + 512 * q:MX + 512 * q + 512]
            stt(o, o, cols[:, 97:98], r, ALU.mult, ALU.mult).then_inc(S["on_ready"], 1)
            dve.wait_ge(S["on_hi"], q + 1)
            tt(actL[:, 2 * q:2 * q + 2], dQ[:, 2 * q:2 * q + 2], actH[:, 2 * q:2 * q + 2].bitcast(F32), ALU.subtract)\
                .then_inc(S["on_lo"], 1)
            if q < 2:
                split(p["U"] + q + 3)
        split(p["U"] + 5)
        add_update(p["U"] + p["n"], 1.0, "up11")
        ffn(1, 1)
        dve.wait_ge(S["std_ready"], NORMS["final"][0] + 1)
        chain(nc.vector.reciprocal(rstd[:], rstd[:]))
        dve.wait_ge(S["ss_ready"], NORMS["in2"][0] + 1)
        chain(tt(rstd2, P[7][:, 0:T], rstd[:], ALU.mult))
        tt(rstd2, rstd2, rstd[:], ALU.mult).then_inc(S["m2_ready"], 1)
        dve.wait_ge(S["mod_ready"], 12)
        for j, (g, sc) in enumerate(((G_ATT, 8), (G_FFN, 32))):
            last = stt(gmod[:, 8 * j:8 * j + 8], modc[:, sc:sc + 8], 1.0, cols[:, g:g + 8], ALU.add, ALU.mult)
        chain(last)
        chain(tt(gmod[:, 0:KT], gmod[:, 0:KT], cols[:, G_FIN:G_FIN + KT], ALU.mult))
        dve.wait_ge(S["std_ready"], NORMS["in2"][0] + 1)
        chain(nc.vector.reciprocal(rstd2, rstd2))
        chain(tt(rstd2, rstd2, rstd[:], ALU.mult))
        for k in range(KT):
            last = stt(NT[:, k], xT[:, k], gmod[:, k:k + 1], rstd2, ALU.mult, ALU.mult)
            if k % 2:
                last.then_inc(S["hn_ready"], 1)
        for q in range(4):
            dve.wait_ge(S["hh_ready"], 4 * NORMS["in2"][2] + q + 1)
            for k in (2 * q, 2 * q + 1):
                last = stt(hTl[:, k], NT[:, k], modc[:, k:k + 1], hTh[:, k].bitcast(F32), ALU.add, ALU.subtract)
            last.then_inc(S["hl_ready"], 1)
        for k in range(KT):
            last = stt(xT[:, k], xT[:, k], cols[:, G_FIN + k:G_FIN + k + 1], rstd[:], ALU.mult, ALU.mult)
            if k % 2:
                last.then_inc(S["x_ready"], 1)
        p = phases["in2"]

        def half_in2(j):
            p = phases["in2"]
            split(p["U"] + j + 2)
            post_copy(p["U"] + j, p["E"] + j, dest_in2(j))
        split(p["U"] + 2)
        post_copy(p["U"], p["E"], iQ)
        split(p["U"] + 3)
        dve.wait_ge(S["half_used"], p["U"] + 2)
        nc.vector.tensor_copy(ikraw[:, 0:T + 8], P[4 + (p["E"] + 1) % 2][:, 0:T + 8]).then_inc(S["bank_free"], 1)
        half_in2(2)
        ts(iw, ikraw[:, T:T + 8].rearrange("p (a b) -> p a b", a=2), 0.5, None, ALU.mult)
        dve.wait_ge(S["ik_std"], 1)
        chain(nc.vector.reciprocal(rstd[:], rstd[:]))
        tt(iK, ikraw[:, 0:T], rstd[:], ALU.mult).then_inc(S["ik_ready"], 1)
        half_in2(3)
        for t in range(2):
            for i, h in enumerate((0, 2, 1, 3)):
                n = 4 * t + i
                dve.wait_ge(S["idx_relu"], n // 2 + 1)
                w, r = iw[:, t, h:h + 1], relu2[:, n % 4]
                if h:
                    dve.wait_ge(S["idx_summed"], n)
                    last = stt(score[:, t], r, w, score[:, t], ALU.mult, ALU.add)
                else:
                    last = ts(score[:, t], r, w, None, ALU.mult)
                last.then_inc(S["idx_summed"], 1)
        half_in2(4)

        def topk(i):
            if i == 0:
                dve.wait_ge(S["masked_ready"], 1)
            for t in range(2):
                last = nc.vector.max(small[:, 16 + 8 * t:24 + 8 * t], score[:, t] if i == 0 else work[:, t])
            chain(last)
            for t in range(2):
                last = nc.vector.match_replace(work[:, t], small[:, 16 + 8 * t:24 + 8 * t], score[:, t] if i == 0 else work[:, t],
                                               TAKEN)
            chain(last)
            if i == TOPK // 8 - 1:
                for t in range(2):
                    ts(pen[:, t], work[:, t], TAKEN / 2, NEG, ALU.is_gt, ALU.mult).then_inc(S["pen_ready"], 1)

        def dense_in2(i):
            for n in range(2 * i, 2 * i + 2):
                if n < TOPK // 8:
                    topk(n)
            if i in IN2_SLOTS:
                half_in2(IN2_SLOTS[i])
            if i in OUT2_SLOTS and OUT2_SLOTS[i] < 2:
                split(phases["out2"]["U"] + OUT2_SLOTS[i] + 2)
        attention(heads_of("heads"), dense_in2)
        p = phases["out2"]
        add_update(p["U"] + p["n"], lambda k: modc[:, 16 + k:17 + k])

        norm("wq", xT, lambda k: gmod[:, 8 + k:9 + k], lambda k: modc[:, 24 + k:25 + k])
        p = phases["wq"]
        for j in range(p["n"]):
            split(p["U"] + j + 2)
            if j >= 4:
                dve.wait_ge(S["sk_scores"], j - 3)
            post_copy(p["U"] + j, p["E"] + j, pQ[:, j % 4])
            if j >= 3:
                subkeys(0, [j - 3])
            if j == 5:
                dve.wait_ge(S["iota_ready"], 1)
                choose(0, CALLS[0][0])
        for j in (5, 6, 7):
            subkeys(0, [j])
        choose(0, CALLS[0][1])
        gates(0)
        gates(1)

        def experts(t, r, g, first=False):
            n = t * GROUPS + g
            dve.wait_ge(u_landed[g], r * (16 * NG) + (t * GROUPS // 2 + 1) * 16 * NG)
            if not first:
                dve.wait_ge(S["gelu_ready"], r * 2 + (n - 1))
            for i in range(NG):
                last = nc.vector.tensor_tensor_reduce(out=GU[:, g, i], in0=GU[:, g, i], in1=htok[:, t], scale=1.0, scalar=0.0,
                                                      op0=ALU.mult, op1=ALU.add, accum_out=dots[:, g, i:i + 1])
            last.then_inc(S["dots_ready"], 1)
            dve.wait_ge(S["gelu_ready"], r * 2 + (n + 1))
            if not first:
                dve.wait_ge(S["diag_ready"], r * 2 + (n - 1))
            if isinstance(r, int):
                gt = gatec[:, (2 * r + n) * NG:(2 * r + n + 1) * NG]
            else:
                gt = gatec[:, bass.ds(r * (2 * NG) + n * NG, NG)]
            tt(coef8[:, g], gel8[:, g], gt, ALU.mult).then_inc(S["coef_ready"], 1)
        for n in range(PEELED):
            experts(0, n // 2, n % 2, n < 2)
            if n - 1 in CALL_AFTER:
                gates(CALL_AFTER[n - 1])
            if 3 <= n < 7:
                subkeys(1, [2 * n - 6, 2 * n - 5])
            if n in CALL_AFTER:
                choose(*ALL_CALLS[CALL_AFTER[n]])
        with dve.Fori(PEELED // 2, GROUPS // 2) as r:
            for g in range(2):
                experts(0, r, g)
        with dve.Fori(0, GROUPS // 2) as r:
            for g in range(2):
                experts(1, r, g)
        dve.wait_ge(S["g2_ready"], 1)
        dve.wait_ge(S["gfin_landed"], 16)
        for t in range(2):
            dve.wait_ge(S["acc_done"], t + 1)
            if t:
                dve.wait_ge(S["fss_ready"], 1)
            for q in range(2):
                last = tt(tmpf[:, q * 512:q * 512 + 512], P[2 * t + q][:], g2bc[:, q * 512:q * 512 + 512], ALU.mult)
            chain(last)
            tt(xtok[:, t], xtok[:, t], tmpf, ALU.add).then_inc(S["xf_ready"], 1)
        for t in range(2):
            dve.wait_ge(S["fstd_ready"], t + 1)
            chain(nc.vector.reciprocal(small[:, 48 + t:49 + t], small[:, 46 + t:47 + t]))
            stt(xtok[:, t], xtok[:, t], small[:, 48 + t:49 + t], gfin, ALU.mult, ALU.mult).then_inc(S["y_ready"], 1)


INPUTS = ["x", "mem", "norm_g", "ffn_w_up", "ffn_w_down", "mem_norm_g", "mem_w_kv", "pool_w_in", "pool_w_group", "pool_scale",
          "pool_w_out", "diff_w_in", "diff_lambda", "diff_norm_g", "diff_w_out", "final_norm_g", "c_2", "w_ada_2", "b_ada_2",
          "norm_attn_2", "norm_ffn_2", "w_in_2", "w_out_2", "rel_bias_2", "peer_wq_2", "peer_subkeys_2", "peer_u_2",
          "peer_v_2", "norm_final_2"]


def kernel(**inputs):
    import numpy as np
    import concourse.bacc as bacc
    from concourse.bass_utils import run_bass_kernel_spmd as run

    nc = bacc.Bacc("TRN2", target_bir_lowering=False, num_devices=1)
    arrays, aps = {}, {}
    for name in INPUTS:
        v = np.ascontiguousarray(inputs[name])
        arrays["in_" + name] = v
        aps[name] = nc.dram_tensor("in_" + name, v.shape, mybir.dt.from_np(v.dtype), kind="ExternalInput").ap()
    out = nc.dram_tensor("out_0", (1, T, D), F32, kind="ExternalOutput").ap()
    program(nc, aps, out)
    r = run(nc, [arrays], core_ids=[0])
    return r.results[0]["out_0"]
```
